# Optimizing a Trainium2 kernel written in Bass

```python
import jax, jax.numpy as jnp
from jax import lax
import numpy as np

D_MODEL = 1024
BATCH = 1
SEQ = 128
DEPTH = 1
DEC_BATCH = 1
DEC_SEQ = 256
PAST_LEN = 128

GRID_W = 64
D_MIX = D_MODEL
D_RNN = D_MIX // 2
D_FOURIER = D_MIX - D_RNN
RNN_HEADS = 8
RNN_HEAD_DIM = D_RNN // RNN_HEADS
CONV_W = 4
CONV_LEFT = 2
RG_C = 8.0
FOURIER_GROUPS = 4
FOURIER_GROUP_DIM = D_FOURIER // FOURIER_GROUPS
D_IN = 2 * D_RNN + D_FOURIER
N_GROUPS = 4
EXPERTS_PER_GROUP = 4
N_EXPERTS = N_GROUPS * EXPERTS_PER_GROUP
TOP_K = 2
D_EXPERT = D_MODEL // 2
ALPHA = (2.0 * DEPTH) ** 0.25
BETA = (8.0 * DEPTH) ** -0.25
LN_EPS = 1e-5
N_MOD = 6

kernel_name = "hybrid_rglru_fnet_hmoe_flow_step"

def layer_norm(x, g, b):
    xf = x.astype(jnp.float32)
    mu = jnp.mean(xf, axis=-1, keepdims=True)
    var = jnp.mean(jnp.square(xf - mu), axis=-1, keepdims=True)
    y = (xf - mu) * lax.rsqrt(var + LN_EPS)
    return (y * g.astype(jnp.float32) + b.astype(jnp.float32)).astype(x.dtype)

def pos_embed_2d(n, d, dtype):
    rows = n // GRID_W
    r = jnp.repeat(jnp.arange(rows, dtype=jnp.float32), GRID_W)
    col = jnp.tile(jnp.arange(GRID_W, dtype=jnp.float32), rows)
    q = d // 4
    freqs = 1.0 / (10000.0 ** (jnp.arange(q, dtype=jnp.float32) / q))
    ar = r[:, None] * freqs[None]
    ac = col[:, None] * freqs[None]
    emb = jnp.concatenate([jnp.sin(ar), jnp.cos(ar), jnp.sin(ac), jnp.cos(ac)], axis=-1)
    return emb.astype(dtype)

def centred_conv(x, w, b):
    n = x.shape[1]
    xp = jnp.pad(x, ((0, 0), (CONV_LEFT, CONV_W - 1 - CONV_LEFT), (0, 0)))
    out = xp[:, 0:n] * w[0]
    for k in range(1, CONV_W):
        out = out + xp[:, k:k + n] * w[k]
    return out + b

def block_diag(x, w, b):
    bsz, n, _ = x.shape
    xh = x.reshape(bsz, n, RNN_HEADS, RNN_HEAD_DIM)
    y = jnp.einsum('bnhi,hij->bnhj', xh, w).reshape(bsz, n, D_RNN)
    return y + b

def _lin_combine(left, right):
    a1, b1 = left
    a2, b2 = right
    return a1 * a2, a2 * b1 + b2

def rglru_scan(x, wa, ba, wi, bi, lam, h0, reverse):
    xf = x.astype(jnp.float32)
    r = jax.nn.sigmoid(block_diag(x, wa, ba).astype(jnp.float32))
    i = jax.nn.sigmoid(block_diag(x, wi, bi).astype(jnp.float32))
    log_a = -RG_C * r * jax.nn.softplus(-lam.astype(jnp.float32))
    a = jnp.exp(log_a)
    mult = jnp.sqrt(-jnp.expm1(2.0 * log_a))
    bt = mult * i * xf
    h0f = h0.astype(jnp.float32)
    if reverse:
        bt = bt.at[:, -1].add(a[:, -1] * h0f)
    else:
        bt = bt.at[:, 0].add(a[:, 0] * h0f)
    _, h = lax.associative_scan(_lin_combine, (a, bt), axis=1, reverse=reverse)
    final = h[:, 0] if reverse else h[:, -1]
    return h.astype(x.dtype), final.astype(x.dtype)

def rglru_bidir(x, wa, ba, wi, bi, lam, h0):
    hf, sf = rglru_scan(x, wa[0], ba[0], wi[0], bi[0], lam[0], h0[:, 0], False)
    hb, sb = rglru_scan(x, wa[1], ba[1], wi[1], bi[1], lam[1], h0[:, 1], True)
    return hf + hb, jnp.stack([sf, sb], axis=1)

def fourier_mix(x, w, b):
    bsz, n, _ = x.shape
    xg = x.reshape(bsz, n, FOURIER_GROUPS, FOURIER_GROUP_DIM).astype(jnp.float32)
    f = jnp.fft.fft2(xg, axes=(1, 3), norm='ortho').real.astype(x.dtype)
    y = jnp.einsum('bngi,gij->bngj', f, w).reshape(bsz, n, D_FOURIER)
    return y + b

def hier_moe(h, wg, bg, we, be, w_gate, w_up, w_down):
    bsz, n, d = h.shape
    t = h.reshape(bsz * n, d)
    ntok = t.shape[0]
    pg = jax.nn.softmax((t @ wg + bg).astype(jnp.float32), axis=-1)
    g = jnp.argmax(pg, axis=-1)
    p_top = jnp.take_along_axis(pg, g[:, None], axis=-1)
    le = (t @ we + be).astype(jnp.float32).reshape(ntok, N_GROUPS, EXPERTS_PER_GROUP)
    le_g = jnp.take_along_axis(le, g[:, None, None], axis=1)[:, 0]
    pe = jax.nn.softmax(le_g, axis=-1)
    v, idx = lax.top_k(pe, TOP_K)
    v = v / jnp.sum(v, axis=-1, keepdims=True)
    w_k = p_top * v
    eidx = g[:, None] * EXPERTS_PER_GROUP + idx
    comb = jnp.sum(jax.nn.one_hot(eidx, N_EXPERTS, dtype=jnp.float32) * w_k[..., None], axis=1)
    hg = jnp.einsum('td,edf->tef', t, w_gate)
    hu = jnp.einsum('td,edf->tef', t, w_up)
    hid = jax.nn.silu(hg) * hu * comb[..., None].astype(t.dtype)
    out = jnp.einsum('tef,efd->td', hid, w_down)
    return out.reshape(bsz, n, d)

def trunk_layer(x, mod, h0, p):
    sh1, sc1, g1, sh2, sc2, g2 = [mod[:, k, None, :] for k in range(N_MOD)]
    h = x * (1.0 + sc1) + sh1
    u = h @ p['w_in']
    xr = u[..., :D_RNN]
    gr = u[..., D_RNN:2 * D_RNN]
    xf = u[..., 2 * D_RNN:]
    xr = centred_conv(xr, p['conv_w'], p['conv_b'])
    yr, states = rglru_bidir(xr, p['rg_wa'], p['rg_ba'], p['rg_wi'], p['rg_bi'], p['rg_lam'], h0)
    yr = yr * jax.nn.gelu(gr)
    yf = fourier_mix(xf, p['fn_w'], p['fn_b'])
    mix = jnp.concatenate([yr, yf], axis=-1) @ p['w_out']
    x = layer_norm(ALPHA * x + g1 * mix, p['ln1_g'], p['ln1_b'])
    h2 = x * (1.0 + sc2) + sh2
    y2 = hier_moe(h2, p['router_g_w'], p['router_g_b'], p['router_e_w'], p['router_e_b'],
                  p['ex_w_gate'], p['ex_w_up'], p['ex_w_down'])
    x = layer_norm(ALPHA * x + g2 * y2, p['ln2_g'], p['ln2_b'])
    return x, states

def setup_inputs(seed: int = 0) -> dict:
    key = jax.random.key(seed)
    ks = jax.random.split(key, 40)
    f32 = jnp.float32

    def nrm(k, shape, s):
        return jax.random.normal(k, shape, f32) * s

    lam_u = jax.random.uniform(ks[13], (DEPTH, 2, D_RNN), f32, 0.9, 0.999)
    return {
        'x_prompt': nrm(ks[0], (BATCH, SEQ, D_MODEL), 1.0),
        'x_sample': nrm(ks[1], (DEC_BATCH, DEC_SEQ, D_MODEL), 1.0),
        'state_rglru': nrm(ks[2], (DEC_BATCH, DEPTH, 2, D_RNN), 0.5),
        'c': nrm(ks[3], (DEC_BATCH, D_MODEL), 1.0),
        'c_ctx': nrm(ks[4], (D_MODEL,), 1.0),
        'ln_in_g': 1.0 + nrm(ks[5], (D_MODEL,), 0.02),
        'ln_in_b': nrm(ks[6], (D_MODEL,), 0.02),
        'w_ada': nrm(ks[7], (DEPTH, D_MODEL, N_MOD * D_MODEL), 0.5 * D_MODEL ** -0.5),
        'b_ada': nrm(ks[8], (DEPTH, N_MOD * D_MODEL), 0.02),
        'w_in': nrm(ks[9], (DEPTH, D_MODEL, D_IN), D_MODEL ** -0.5),
        'conv_w': nrm(ks[10], (DEPTH, CONV_W, D_RNN), CONV_W ** -0.5),
        'conv_b': nrm(ks[11], (DEPTH, D_RNN), 0.02),
        'rg_wa': nrm(ks[12], (DEPTH, 2, RNN_HEADS, RNN_HEAD_DIM, RNN_HEAD_DIM), RNN_HEAD_DIM ** -0.5),
        'rg_ba': nrm(ks[14], (DEPTH, 2, D_RNN), 0.02),
        'rg_wi': nrm(ks[15], (DEPTH, 2, RNN_HEADS, RNN_HEAD_DIM, RNN_HEAD_DIM), RNN_HEAD_DIM ** -0.5),
        'rg_bi': nrm(ks[16], (DEPTH, 2, D_RNN), 0.02),
        'rg_lam': jnp.log(lam_u) - jnp.log1p(-lam_u),
        'fn_w': nrm(ks[17], (DEPTH, FOURIER_GROUPS, FOURIER_GROUP_DIM, FOURIER_GROUP_DIM), FOURIER_GROUP_DIM ** -0.5),
        'fn_b': nrm(ks[18], (DEPTH, D_FOURIER), 0.02),
        'w_out': nrm(ks[19], (DEPTH, D_MIX, D_MODEL), BETA * D_MIX ** -0.5),
        'ln1_g': 1.0 + nrm(ks[20], (DEPTH, D_MODEL), 0.02),
        'ln1_b': nrm(ks[21], (DEPTH, D_MODEL), 0.02),
        'router_g_w': nrm(ks[22], (DEPTH, D_MODEL, N_GROUPS), D_MODEL ** -0.5),
        'router_g_b': nrm(ks[23], (DEPTH, N_GROUPS), 0.01),
        'router_e_w': nrm(ks[24], (DEPTH, D_MODEL, N_EXPERTS), D_MODEL ** -0.5),
        'router_e_b': nrm(ks[25], (DEPTH, N_EXPERTS), 0.01),
        'ex_w_gate': nrm(ks[26], (DEPTH, N_EXPERTS, D_MODEL, D_EXPERT), D_MODEL ** -0.5),
        'ex_w_up': nrm(ks[27], (DEPTH, N_EXPERTS, D_MODEL, D_EXPERT), D_MODEL ** -0.5),
        'ex_w_down': nrm(ks[28], (DEPTH, N_EXPERTS, D_EXPERT, D_MODEL), BETA * D_EXPERT ** -0.5),
        'ln2_g': 1.0 + nrm(ks[29], (DEPTH, D_MODEL), 0.02),
        'ln2_b': nrm(ks[30], (DEPTH, D_MODEL), 0.02),
    }

def reference(x_prompt, x_sample, state_rglru, c, c_ctx, ln_in_g, ln_in_b, w_ada, b_ada, w_in,
              conv_w, conv_b, rg_wa, rg_ba, rg_wi, rg_bi, rg_lam, fn_w, fn_b, w_out, ln1_g, ln1_b,
              router_g_w, router_g_b, router_e_w, router_e_b, ex_w_gate, ex_w_up, ex_w_down,
              ln2_g, ln2_b):
    n_lat = x_sample.shape[1]
    xp = layer_norm(x_prompt, ln_in_g, ln_in_b)
    xs = layer_norm(x_sample + pos_embed_2d(n_lat, D_MODEL, x_sample.dtype)[None], ln_in_g, ln_in_b)
    silu_c = jax.nn.silu(c)
    silu_ctx = jax.nn.silu(c_ctx)[None]
    new_states = []
    for l in range(DEPTH):
        p = {
            'w_in': w_in[l], 'conv_w': conv_w[l], 'conv_b': conv_b[l],
            'rg_wa': rg_wa[l], 'rg_ba': rg_ba[l], 'rg_wi': rg_wi[l], 'rg_bi': rg_bi[l], 'rg_lam': rg_lam[l],
            'fn_w': fn_w[l], 'fn_b': fn_b[l], 'w_out': w_out[l], 'ln1_g': ln1_g[l], 'ln1_b': ln1_b[l],
            'router_g_w': router_g_w[l], 'router_g_b': router_g_b[l],
            'router_e_w': router_e_w[l], 'router_e_b': router_e_b[l],
            'ex_w_gate': ex_w_gate[l], 'ex_w_up': ex_w_up[l], 'ex_w_down': ex_w_down[l],
            'ln2_g': ln2_g[l], 'ln2_b': ln2_b[l],
        }
        mod_ctx = (silu_ctx @ w_ada[l] + b_ada[l]).reshape(1, N_MOD, D_MODEL)
        mod_lat = (silu_c @ w_ada[l] + b_ada[l]).reshape(-1, N_MOD, D_MODEL)
        h0_ctx = jnp.zeros((xp.shape[0], 2, D_RNN), xp.dtype)
        xp, st_ctx = trunk_layer(xp, mod_ctx, h0_ctx, p)
        new_states.append(st_ctx)
        xs, _ = trunk_layer(xs, mod_lat, state_rglru[:, l], p)
    new_state_rglru = jnp.stack(new_states, axis=1)
    return (xp, xs, new_state_rglru)


_drawn_inputs = setup_inputs


def setup_inputs(seed=0):
    import zlib

    import numpy as np

    out = dict(_drawn_inputs(seed))
    spreads = {}
    factors = {'state_rglru': 6.233,
     'rg_ba': 8.0,
     'rg_bi': 6.576,
     'fn_b': 25.2,
     'ln1_g': 2.905,
     'ln1_b': 2.694,
     'router_g_b': 21.77,
     'router_e_b': 41.8,
     'ln2_g': 8.628,
     'ln2_b': 8.138}
    for name, (base, spread) in spreads.items():
        noise = np.random.default_rng([zlib.crc32(name.encode()), seed]).standard_normal(out[name].shape)
        drawn = base * np.exp(spread * noise) if base else spread * noise
        out[name] = __import__('jax').numpy.asarray(drawn.astype(out[name].dtype))
    for name, factor in factors.items():
        out[name] = (out[name] * factor).astype(out[name].dtype)
    return out
```

```python
from contextlib import ExitStack

import numpy as np

import concourse.bass as bass
from concourse import mybir

F32 = mybir.dt.float32
F32R = mybir.dt.float32r
BF16 = mybir.dt.bfloat16
U32 = mybir.dt.uint32
I32 = mybir.dt.int32
ALU = mybir.AluOpType
ACT = mybir.ActivationFunctionType
AX = mybir.AxisListType

P = 128
D = 1024
KD = D // P
SEQ = 128
LAT = 256
TOK = SEQ + LAT
NT = TOK // P
DR = D // 2
CR = DR // P
FG = 4
NE = 16
NG = 4
EPG = NE // NG
FE = D // 2
KF = FE // P
GRID_W = 64
ALPHA = 2.0 ** 0.25
LN_EPS = 1e-5
W = SEQ + 3 + LAT + 1
TC = [0, SEQ + 3, SEQ + 3 + P]
SEG = [(0, SEQ), (SEQ + 3, LAT)]
SEGC = [(0, SEQ), (SEQ, LAT)]
XW = W + 3
UNIT = 4096
RING = 6
NP1 = 17
CAP = P
PASSES = TOK // CAP
YROWS = NE * CAP
FAR = 1e5

C_ID, C_TRI, C_ONE, C_IOTA = 0, 128, 256, 384
C_EROW, C_COD16, C_COD4 = C_IOTA + TOK, C_IOTA + TOK + 16, C_IOTA + TOK + 32
NCONST = C_COD4 + 4 + 2
C_SUM = C_COD4 + 4
F_CH, F_CTX, F_LAT = 0, 256, 512
NDFT = 512 + 2 * 512

A_C, A_CTX, A_BADA, A_LNG, A_LNB, A_CW, A_CB, NA = 0, 8, 16, 64, 72, 80, 96, 100
B_BA, B_BI, B_LAM, B_ST, B_FB, NB = 0, 8, 16, 24, 32, 36

SH1, SC1, G1, SH2, SC2, G2 = range(6)


def constants():
    c = np.zeros((P, NCONST), np.float32)
    c[:, C_ID:C_ID + P] = np.eye(P)
    c[:, C_TRI:C_TRI + P] = np.triu(np.ones((P, P)), 1)
    c[:, C_ONE:C_ONE + P] = 1
    c[:, C_IOTA:C_IOTA + TOK] = np.arange(TOK)
    c[:, C_EROW:C_EROW + NE] = np.arange(NE) * CAP
    c[:, C_COD16:C_COD16 + NE] = NE - np.arange(NE)
    c[:, C_COD4:C_COD4 + NG] = NG - np.arange(NG)
    for q in range(2):
        c[q::32, C_SUM + q] = 1

    def dft(n):
        a = 2 * np.pi * (np.outer(np.arange(n), np.arange(n)) % n) / n
        return np.cos(a) / np.sqrt(n), np.sin(a) / np.sqrt(n)

    f = np.zeros((P, NDFT), np.float32)
    co, si = dft(P)
    f[:, 0:P], f[:, P:2 * P] = co, si
    f[:, F_CTX:F_CTX + P], f[:, F_CTX + P:F_CTX + 2 * P] = co, -si
    co, si = dft(LAT)
    for m in range(2):
        f[:, F_LAT + 512 * m:F_LAT + 512 * m + LAT] = co[m * P:(m + 1) * P]
        f[:, F_LAT + 512 * m + LAT:F_LAT + 512 * (m + 1)] = -si[m * P:(m + 1) * P]

    q = D // 4
    freqs = (1.0 / (10000.0 ** (np.arange(q, dtype=np.float32) / q))).astype(np.float32)
    r = np.repeat(np.arange(LAT // GRID_W, dtype=np.float32), GRID_W)[:, None] * freqs[None]
    k = np.tile(np.arange(GRID_W, dtype=np.float32), LAT // GRID_W)[:, None] * freqs[None]
    pos = np.concatenate([np.sin(r), np.cos(r), np.sin(k), np.cos(k)], axis=-1).astype(np.float32)
    return c, f, pos


def build(nc, t):
    ctx = ExitStack()
    with ctx:
        def sem(name):
            return ctx.enter_context(nc.semaphore(name))

        def at(name, off, shape, dt=F32):
            return nc.alloc_sbuf_tensor_at(name, shape, dt, offset=off)

        base = (nc._sbuf_addr_for_side("left") + 31) // 32 * 32
        RB = UNIT * 4
        ring = [at(f"ring{s}", base + s * RB, [P, UNIT]) for s in range(RING)]
        wlo = [at(f"wlo{s}", base + s * RB, [P, UNIT], F32R) for s in range(RING)]
        o = base + RING * RB
        xn = at("xn", o, [P, NT, D])
        o += NT * D * 4
        place = [o]

        def keep(name, shape, dt=F32):
            n = int(np.prod(shape[1:])) * (2 if dt == BF16 else 4)
            n = (n + 31) // 32 * 32
            place[0] += n
            return at(name, place[0] - n, shape, dt)

        cst = keep("cst", [P, NCONST])
        modT = keep("modT", [P, 6 * KD, 2])
        mrow = keep("mrow", [P, 512])
        cols = keep("cols", [P, NA + NB])
        cond = keep("cond", [P, KD, 2])
        cond32 = keep("cond32", [P, KD, 32])
        cmod = keep("cmod", [P, 2, KD, 2])
        bga = keep("bga", [P, 16])
        spl = keep("spl", [P, 6, 8])
        stat = keep("stat", [P, NT, 16])
        stin = keep("stin", [P, 16])
        small = keep("small", [P, 8])
        strow = keep("strow", [P, P])
        rankA = keep("rankA", [P, NE + 1, NT])
        posn = keep("posn", [P, PASSES, 2, NT], U32)
        posf = keep("posf", [P, 3, 2, NT])
        wk = keep("wk", [P, 2, NT])
        cnt = keep("cnt", [P, 2], I32)
        wr = keep("wr", [P, KD, NG + NE])
        rb = keep("rb", [P, NG + NE])
        lg = keep("lg", [P, NT, NG + NE])
        rt = keep("rt", [P, 8, NT, NE])
        rs = keep("rs", [P, 12, NT])
        A0 = place[0]
        AREA = A0
        h2b = at("h2b", A0, [P, 3, NT, D], BF16)
        o = A0 + 3 * NT * D * 2
        M0 = o
        xsH = at("xsH", o, [P, KD, CAP], F32R); o += KD * CAP * 4
        xsL = at("xsL", o, [P, KD, CAP], F32R); o += KD * CAP * 4
        hTH = at("hTH", o, [P, KF, CAP], F32R); o += KF * CAP * 4
        hTL = at("hTL", o, [P, KF, CAP], F32R); o += KF * CAP * 4
        sel = at("sel", o, [P, NT, CAP], BF16); o += NT * CAP * 2
        sg = at("sg", o, [P, FE]); o += FE * 4
        hid = at("hid", o, [P, FE]); o += FE * 4
        ysb = at("ysb", o, [P, D]); o += D * 4
        tt = at("tt", M0, [P, 2, D])
        h2T = at("h2T", M0 + 2 * D * 4, [P, KD, TOK])
        B0 = max(o, M0 + 2 * D * 4 + KD * TOK * 4)
        whi = [at(f"whi{j}", B0 + j * RB, [P, UNIT], F32R) for j in range(3)]
        end = B0 + 3 * RB
        assert end <= base + nc.sbuf_bytes_remaining, (end, nc.sbuf_bytes_remaining)
        hT = at("hT", B0, [P, KD, W])
        mixT = at("mixT", B0, [P, KD, TOK])
        FTs = at("FTs", B0 + KD * W * 4, [P, 2, TOK])
        rtmp = at("rtmp", B0 + KD * W * 4, [P, 2, W])
        assert KD * W * 4 + 2 * W * 4 <= RB
        o = B0 + RB
        gr = at("gr", o, [P, CR, W]); o += CR * W * 4
        xf = at("xf", o, [P, FG, W]); o += FG * W * 4
        Z = at("Z", o, [P, 2, NT, 2 * P]); o += 2 * NT * 2 * P * 4
        dft = at("dft", o, [P, NDFT]); o += NDFT * 4
        fnw = at("fnw", o, [P, FG, P]); o += FG * P * 4
        hfb = at("hfb", o, [P, 2, W]); o += 2 * W * 4
        vtmp = at("vtmp", o, [P, W]); o += W * 4
        assert o <= end
        rows = at("rows", B0 + RB, [P, 8, D])
        o = A0
        gtmp = at("gtmp", o, [P, 3, 4, W])
        pos = at("pos", o, [P, 2, D])
        lnin = at("lnin", o + 2 * D * 4, [P, 2, D])
        o += max(3 * 4 * W * 4, 4 * D * 4)
        xc = at("xc", o, [P, CR, W]); o += CR * W * 4
        xpad = at("xpad", o, [P, CR, XW + 1]); o += CR * (XW + 1) * 4
        wbd = at("wbd", o, [P, 16, P]); o += 16 * P * 4
        assert o <= B0, (o, B0)
        rowA = at("rowA", B0 + 2 * RB, [P, P])
        rowB = at("rowB", B0 + 2 * RB + P * 4, [P, P])
        y12 = at("y12", base, [P, 2, NT, D])
        fin = at("fin", base + 2 * NT * D * 4, [P, NT, D])
        ln2 = at("ln2", base + 3 * NT * D * 4, [P, 2, D])

        PS = ctx.enter_context(nc.psum_tensor("PS", [P, 8, 512], F32))
        Y_dram = [nc.dram_tensor(f"y_rows{pb}", (YROWS, D), F32, kind="Internal").ap() for pb in range(PASSES)]

        s = {n: sem(n) for n in (
            "const_in rowA_in rowB_in x_in pos_in lnin_in wbd_in smallw_in ln1_in ln2_in rtr_in "
            "cols_ps cols_sb cond_done zeroed ln_xhat xT_ps xT_sb mrow_sb modT_ps mod_sb cm_done h_done "
            "win_ps win_sb conv_done gate_ps gate_act rec_v mult_done q_done tanh_done scan_done gelu_t gelu_th gelu_done yr_done "
            "z_ps z_sb f_ps f_sb yf_ps yf_sb row_ps row_sb mix_ps xn_done xn_pool mixsum x1n x1_done h2_done "
            "h2b1 h2r h2b2 h2b3 h2T_ps h2T_sb lg_ps assign_done rank_ps route_done pos_pool "
            "p1_used unit_used hi_done lo_done sel_ready x_disp xs_hi xs_ready silu_done up_ps hid_ready "
            "ht_ps ht_hi hts_ready y_sb y_stored passes_done gathered gathered0 gathered1 gathered2 g2_ps fin_act fin_done out_done var_done root_done state_done st_ps st_row st_out "
            "dve_step act_step pool_step").split()}
        ring_in = [sem(f"ring_in{k}") for k in range(RING)]

        def unit3(buf, n=512):
            return buf[:, :].rearrange("p (k n) -> p k n", n=n)

        def need(eng, name, value):
            if isinstance(value, int) and value <= 0:
                return
            eng.wait_ge(s[name], value)

        def p1_loaded(eng, u):
            slot = (u + 1) % RING
            eng.wait_ge(ring_in[slot], 16 * ((u + 1) // RING + (slot > 0)))

        block = ctx.enter_context(nc.Block())

        ada = t["w_ada"][0].rearrange("(k p) n -> p k n", p=P)
        win = t["w_in"][0].rearrange("(k p) n -> p k n", p=P)
        wout = t["w_out"][0].rearrange("(k p) n -> p k n", p=P)
        ADA = {SH1: 0, SC1: 2, G1: 7, SH2: 9, SC2: 11, G2: 15}
        p1_units = ([(ada, SH1 * D), (ada, SH1 * D + 512), (ada, SC1 * D), (ada, SC1 * D + 512)]
                    + [(win, 0), (win, 1024), (win, 512)]
                    + [(ada, G1 * D), (ada, G1 * D + 512), (ada, SH2 * D), (ada, SH2 * D + 512),
                       (ada, SC2 * D), (ada, SC2 * D + 512)]
                    + [(wout, 0), (wout, 512)] + [(ada, G2 * D), (ada, G2 * D + 512)])
        ADA_GROUPS = [4, 6, 10, 12]
        ADA_UNIT = [0, 1, 2, 3, 7, 8, 9, 10, 11, 12, 15, 16]
        ABANK = [6, 4] * 5 + [6, 6]
        ada_order = [SH1, SC1, G1, SH2, SC2, G2]
        experts = [
            t["ex_w_gate"][0].rearrange("e (k p) n -> p e k n", p=P),
            t["ex_w_up"][0].rearrange("e (k p) n -> p e k n", p=P),
            t["ex_w_down"][0].rearrange("e (k p) n -> p e k n", p=P),
        ]

        def passes(eng, body, after_counts):
            body(0)
            after_counts()
            most = eng.value_load(cnt[0:1, 0:1], min_val=0, max_val=TOK)
            with eng.Fori(1, PASSES) as pb:
                with eng.If(most > pb * CAP):
                    body(pb)

        def pairs(eng, prologue, body, pb):
            ge0 = pb * NE
            prologue(ge0)
            for p in range(2):
                body(ge0 + p, p, pb * (NE // 2), p, False)
            with eng.Fori(1, NE // 2 - 1) as it:
                for p in range(2):
                    body(ge0 + it * 2 + p, it * 2 + p, pb * (NE // 2) + it, p, False)
            for p in range(2):
                body(ge0 + NE - 2 + p, NE - 2 + p, pb * (NE // 2) + NE // 2 - 1, p, p == 1)

        @block.sync
        def _(sp):
            for i in range(NT):
                src = t["x_prompt"][0] if i == 0 else t["x_sample"][0, (i - 1) * P:i * P]
                sp.dma_start(xn[:, i, :], src).then_inc(s["x_in"], 16)
            sp.dma_start(pos[:, :, :], t["pos"].rearrange("(i p) d -> p i d", p=P)).then_inc(s["pos_in"], 16)
            sp.wait_ge(s["const_in"], 16)
            sp.wait_ge(s["rowA_in"], 16 * 7)
            sp.wait_ge(s["rowB_in"], 16 * 5)
            for u, (src, c0) in enumerate(p1_units):
                if u + 1 >= RING + 1:
                    sp.wait_ge(s["p1_used"], u + 1 - RING)
                sp.dma_start(unit3(ring[(u + 1) % RING]), src[:, :, c0:c0 + 512]).then_inc(ring_in[(u + 1) % RING], 16)

            def load(ge, e, p, first):
                for j in range(3):
                    if first:
                        sp.wait_ge(s["p1_used"], NP1 + 1 - RING + 3 * p + j)
                    else:
                        sp.wait_ge(s["unit_used"], ge * 3 + (j - 5))
                    slot = 3 * p + j
                    sp.dma_start(unit3(ring[slot], D if j == 2 else 512),
                                 experts[j][:, e]).then_inc(ring_in[slot], 16)

            for p in range(2):
                load(p, p, p, True)
            with sp.Fori(1, NE // 2) as it:
                for p in range(2):
                    load(it * 2 + p, it * 2 + p, p, False)
            sp.wait_ge(s["route_done"], 1)
            most = sp.value_load(cnt[0:1, 0:1], min_val=0, max_val=TOK)
            with sp.Fori(1, PASSES) as pb:
                with sp.If(most > pb * CAP):
                    with sp.Fori(0, NE // 2) as it:
                        for p in range(2):
                            load(pb * NE + it * 2 + p, it * 2 + p, p, False)
            sp.wait_ge(s["passes_done"], 1)
            for r, n in enumerate(("ln2_g", "ln2_b")):
                sp.dma_start(ln2[:, r, :], t[n].partition_broadcast(P)).then_inc(s["ln2_in"], 16)
            for i in range(NT):
                sp.wait_ge(s["fin_done"], i + 1)
                dst = t["y_prompt"][0] if i == 0 else t["y_sample"][0, (i - 1) * P:i * P]
                sp.dma_start(dst, fin[:, i, :]).then_inc(s["out_done"], 16)
            sp.wait_ge(s["out_done"], 16 * NT)

        @block.scalar
        def _(act):
            n_step = [0]

            def root(n):
                i = n % NT
                act.wait_ge(s["var_done"], n + 1)
                act.activation(stat[:, i, 13:14], stat[:, i, 13:14], ACT.Sqrt).then_inc(s["root_done"], 1)

            def link(ins):
                n_step[0] += 1
                ins.then_inc(s["act_step"], 1)
                act.wait_ge(s["act_step"], n_step[0])

            act.dma_start(cst[:, :], t["const"]).then_inc(s["const_in"], 16)
            for n, r0, k in (("c", A_C, 8), ("c_ctx", A_CTX, 8), ("b_ada", A_BADA, 48), ("ln_in_g", A_LNG, 8),
                             ("ln_in_b", A_LNB, 8), ("conv_w", A_CW, 16), ("conv_b", A_CB, 4)):
                act.dma_start(rowA[r0:r0 + k, :], t[n]).then_inc(s["rowA_in"], 16)
            for n, r0, k in (("rg_ba", B_BA, 8), ("rg_bi", B_BI, 8), ("rg_lam", B_LAM, 8), ("state", B_ST, 8),
                             ("fn_b", B_FB, 4)):
                act.dma_start(rowB[r0:r0 + k, :], t[n]).then_inc(s["rowB_in"], 16)
            for r, n in enumerate(("ln_in_g", "ln_in_b")):
                act.dma_start(lnin[:, r, :], t[n + "_row"].partition_broadcast(P)).then_inc(s["lnin_in"], 16)
            act.wait_ge(s["zeroed"], 1)
            for gi, n in enumerate(("rg_wa", "rg_wi")):
                for h in range(2):
                    act.dma_start(wbd[64 * h:64 * h + 64, 8 * gi:8 * gi + 8, 64 * h:64 * h + 64],
                                  t[n][0].rearrange("d (c q) i j -> q i (d c) j", q=2)[h]).then_inc(s["wbd_in"], 16)
            act.dma_start(fnw[:, :, :], t["fn_w"][0].rearrange("g i j -> i g j")).then_inc(s["smallw_in"], 16)
            act.dma_start(dft[:, :], t["dft"]).then_inc(s["smallw_in"], 16)
            act.dma_start(wr[:, :, 0:NG], t["router_g_w"][0].rearrange("(k p) n -> p k n", p=P)).then_inc(s["rtr_in"], 16)
            act.dma_start(wr[:, :, NG:], t["router_e_w"][0].rearrange("(k p) n -> p k n", p=P)).then_inc(s["rtr_in"], 16)
            act.dma_start(rb[:, 0:NG], t["router_g_b"].partition_broadcast(P)).then_inc(s["rtr_in"], 16)
            act.dma_start(rb[:, NG:], t["router_e_b"].partition_broadcast(P)).then_inc(s["rtr_in"], 16)

            for i in range(NT):
                root(i)
            act.wait_ge(s["cols_sb"], 1)
            for q, c0 in enumerate((A_CTX, A_C)):
                act.activation(cond[:, :, q], cols[:, c0:c0 + KD], ACT.Exp, scale=-1.0).then_inc(s["cond_done"], 1)
            act.activation(spl[:, 0, :], cols[:, NA + B_LAM:NA + B_LAM + 8], ACT.Abs).then_inc(s["act_step"], 1)
            n_step[0] += 1
            act.wait_ge(s["act_step"], n_step[0])
            act.activation(spl[:, 1, :], spl[:, 0, :], ACT.Exp, scale=-1.0).then_inc(s["cond_done"], 1)

            act.wait_ge(s["zeroed"], 3)
            for i in range(NT):
                for hf in range(2):
                    act.wait_ge(s["xT_ps"], 2 * i + hf + 1)
                    act.copy(hT[:, 4 * hf:4 * hf + 4, TC[i]:TC[i] + P],
                             PS[:, 2 * i + hf, :].rearrange("p (k n) -> p k n", n=P)).then_inc(s["xT_sb"], 1)

            def ada_rows(n):
                act.wait_ge(s["p1_used"], ADA_UNIT[n] + 1)
                need(act, "modT_ps", n)
                act.copy(mrow[:, :], PS[:, ABANK[n], :]).then_inc(s["mrow_sb"], 1)

            for n in range(4):
                ada_rows(n)

            for w in range(12):
                if w % 4 == 3:
                    act.wait_ge(s["p1_used"], 5 + w // 4)
                else:
                    act.wait_ge(s["win_ps"], w + 1 - w // 4)
                c = w % 4
                src = PS[:, w % 4, 0:W]
                if w < 4:
                    act.copy(xpad[:, c, 2:2 + W], src).then_inc(s["win_sb"], 1)
                elif w < 8:
                    act.copy(xf[:, c, :], src).then_inc(s["win_sb"], 1)
                else:
                    act.copy(gr[:, c, :], src).then_inc(s["win_sb"], 1)
            for n in range(4, 6):
                ada_rows(n)
            for g in range(FG):
                act.wait_ge(s["z_ps"], g + 1)
                if g >= 2:
                    act.wait_ge(s["f_ps"], g - 1)
                act.copy(Z[:, g % 2, 0:2, :], PS[:, 6, :].rearrange("p (i n) -> p i n", n=256))
                act.copy(Z[:, g % 2, 2, :], PS[:, 5, 0:256]).then_inc(s["z_sb"], 1)

            act.wait_ge(s["gelu_t"], 3)
            act.activation(xpad[:, :, 0:W], xpad[:, :, 0:W], ACT.Tanh, scale=float(np.sqrt(2 / np.pi))).then_inc(s["gelu_th"], 1)

            for it in range(8):
                c, d = it // 2, it % 2
                q = it % 4
                act.wait_ge(s["gate_ps"], it + 1)
                if it == 0:
                    act.wait_ge(s["yf_ps"], FG)
                if it >= 4:
                    act.wait_ge(s["scan_done"], it - 3)
                bk = 2 * (it % 2)
                tr, a_, q_, v_ = rtmp[:, it % 2], gtmp[:, 0, q], gtmp[:, 1, q], gtmp[:, 2, q]
                link(act.activation(tr, PS[:, bk, 0:W], ACT.Tanh, bias=bga[:, 4 * d + c:4 * d + c + 1], scale=0.5))
                act.activation(q_, PS[:, bk + 1, 0:W], ACT.Tanh, bias=bga[:, 8 + 4 * d + c:9 + 4 * d + c], scale=0.5)\
                    .then_inc(s["gate_act"], 1)
                sc = spl[:, 5, 4 * d + c:4 * d + c + 1]
                act.activation(v_, tr, ACT.Tanh, bias=sc, scale=sc).then_inc(s["tanh_done"], 1)
                act.activation(a_, tr, ACT.Exp, bias=sc, scale=sc).then_inc(s["tanh_done"], 1)
                act.wait_ge(s["tanh_done"], 2 * it + 2)
                if 2 <= it < 6:
                    ada_rows(it + 4)
                if q == 3:
                    act.wait_ge(s["rec_v"], it + 1)
                    act.activation(gtmp[:, 2], gtmp[:, 2], ACT.Sqrt).then_inc(s["mult_done"], 1)

            act.wait_ge(s["yr_done"], CR)
            for r in range(6):
                act.wait_ge(s["row_ps"], r + 1)
                act.activation(rows[:, r, :], PS[:, 6:8, :].rearrange("p a n -> p (a n)"), ACT.Identity,
                               bias=1.0 if r in (2, 3) else 0.0).then_inc(s["row_sb"], 1)
                if r == 0:
                    for k, n in enumerate(("ln1_g", "ln1_b")):
                        act.dma_start(rows[:, 6 + k, :], t[n].partition_broadcast(P)).then_inc(s["ln1_in"], 16)

            for n in range(10, 12):
                ada_rows(n)
            root(NT)
            root(NT + 1)
            for i in range(NT):
                if i == 1:
                    root(NT + 2)
                act.wait_ge(s["h2_done"], i + 1)
                act.copy(h2b[:, 0, i, :], tt[:, i % 2, :]).then_inc(s["h2b1"], 1)
                act.wait_ge(s["h2T_ps"], i + 1)
                act.copy(h2T[:, :, i * P:(i + 1) * P], PS[:, 2 * i:2 * i + 2, :].rearrange("p a (k n) -> p (a k) n", n=P))\
                    .then_inc(s["h2T_sb"], 1)
                act.wait_ge(s["h2r"], i + 1)
                act.copy(h2b[:, 1, i, :], tt[:, i % 2, :]).then_inc(s["h2b2"], 1)
            act.wait_ge(s["assign_done"], 1)
            act.activation(rt[:, 6, :, 0:NG], rt[:, 5, :, 0:NG], ACT.Exp).then_inc(s["pos_pool"], 1)
            act.activation(rs[:, 5, :], rs[:, 4, :], ACT.Exp).then_inc(s["pos_pool"], 1)

            halves = [(0, UNIT // 2), (UNIT // 2, UNIT)]

            def split_hi(ge, q, p, j):
                act.wait_ge(ring_in[3 * p + j], q * 16 + 16 * ((NP1 + 1) // RING + (3 * p + j > 0)))
                need(act, "unit_used", ge * 3 + (j - 2))
                for a, b in halves:
                    act.copy(whi[j][:, a:b], ring[3 * p + j][:, a:b]).then_inc(s["hi_done"], 1)

            def x_hi(ge):
                act.wait_ge(s["x_disp"], ge + 1)
                need(act, "unit_used", ge * 3 - 1)
                act.copy(xsH[:, :, :], PS[:, 0:2, :].rearrange("p a (k n) -> p (a k) n", n=CAP)).then_inc(s["xs_hi"], 1)

            def prologue(ge):
                q = ge // 2 if isinstance(ge, int) else ge // 2
                if isinstance(ge, int):
                    act.wait_ge(s["h2_done"], NT)
                    act.wait_ge(s["route_done"], 1)
                split_hi(ge, q, 0, 0)
                x_hi(ge)
                split_hi(ge, q, 0, 1)
                split_hi(ge, q, 0, 2)

            def body(ge, e, q, p, last):
                q1 = q + p
                if not last:
                    split_hi(ge + 1, q1, 1 - p, 0)
                act.wait_ge(s["unit_used"], ge * 3 + 1)
                need(act, "hid_ready", ge)
                act.activation(sg[:, :], PS[:, 2, :], ACT.Silu).then_inc(s["silu_done"], 1)
                if not last:
                    x_hi(ge + 1)
                act.wait_ge(s["ht_ps"], ge + 1)
                need(act, "unit_used", ge * 3)
                act.copy(hTH[:, :, :], PS[:, 4, :].rearrange("p (k n) -> p k n", n=CAP)).then_inc(s["ht_hi"], 1)
                if not last:
                    split_hi(ge + 1, q1, 1 - p, 1)
                act.wait_ge(s["unit_used"], ge * 3 + 3)
                need(act, "y_stored", ge * 16)
                act.copy(ysb[:, :], PS[:, 5:7, :].rearrange("p a n -> p (a n)")).then_inc(s["y_sb"], 1)
                if not last:
                    split_hi(ge + 1, q1, 1 - p, 2)

            passes(act, lambda pb: pairs(act, prologue, body, pb), lambda: None)
            for i in range(NT):
                root(2 * NT + i)

        @block.vector
        def _(dve):
            n_step = [0]
            n_norm = [0]

            def step(ins):
                n_step[0] += 1
                ins.then_inc(s["dve_step"], 1)

            def link(ins):
                step(ins)
                dve.wait_ge(s["dve_step"], n_step[0])

            def norm_stats(x, i, st):
                step(dve.bn_stats(st[:, 0:6], x[:, 0:512]))
                link(dve.bn_stats(st[:, 6:12], x[:, 512:1024]))
                link(dve.bn_aggr(st[:, 12:14], st[:, 0:12].rearrange("p (a b) -> p a b", b=6)))
                dve.tensor_scalar(st[:, 13:14], st[:, 13:14], LN_EPS, None, ALU.add).then_inc(s["var_done"], 1)
                n_norm[0] += 1
                dve.wait_ge(s["root_done"], n_norm[0])
                link(dve.reciprocal(st[:, 13:14], st[:, 13:14]))

            for i in range(NT):
                dve.wait_ge(s["x_in"], 16 * NT)
                if i > 0:
                    dve.wait_ge(s["xn_pool"], i)
                norm_stats(xn[:, i, :], i, stat[:, i, :])
                dve.tensor_scalar(xn[:, i, :], xn[:, i, :], stat[:, i, 12:13], stat[:, i, 13:14],
                                  ALU.subtract, ALU.mult).then_inc(s["ln_xhat"], 1)

            dve.wait_ge(s["cols_ps"], 1)
            dve.tensor_copy(cols[:, :], PS[:, 0, 0:NA + NB]).then_inc(s["cols_sb"], 1)
            dve.wait_ge(s["cols_sb"], 1)
            dve.wait_ge(s["cond_done"], 3)
            link(dve.tensor_scalar(cond[:, :, :], cond[:, :, :], 1.0, None, ALU.add))
            link(dve.reciprocal(cond[:, :, :], cond[:, :, :]))
            for q, c0 in enumerate((A_CTX, A_C)):
                dve.tensor_tensor(cond[:, :, q], cond[:, :, q], cols[:, c0:c0 + KD], ALU.mult).then_inc(s["cond_done"], 1)
            dve.wait_ge(s["zeroed"], 3)
            dve.wait_ge(s["cond_done"], 5)
            dve.tensor_copy(cond32[:, :, 0:2], cond[:, :, :]).then_inc(s["cond_done"], 1)
            dve.tensor_scalar(bga[:, :], cols[:, NA + B_BA:NA + B_BA + 16], 0.5, None, ALU.mult).then_inc(s["cond_done"], 1)
            z, w, w2, acc = spl[:, 1, :], spl[:, 2, :], spl[:, 3, :], spl[:, 4, :]
            link(dve.tensor_scalar(w, z, 2.0, None, ALU.add))
            link(dve.reciprocal(w, w))
            link(dve.tensor_tensor(w, w, z, ALU.mult))
            link(dve.tensor_tensor(w2, w, w, ALU.mult))
            link(dve.tensor_scalar(acc, w2, 1.0 / 17, 1.0 / 15, ALU.mult, ALU.add))
            for n in (13, 11, 9, 7, 5, 3, 1):
                link(dve.tensor_tensor(acc, acc, w2, ALU.mult))
                link(dve.tensor_scalar(acc, acc, 1.0 / n, None, ALU.add))
            link(dve.tensor_tensor(acc, acc, w, ALU.mult))
            link(dve.tensor_scalar(w, cols[:, NA + B_LAM:NA + B_LAM + 8], -1.0, 0.0, ALU.mult, ALU.max))
            link(dve.scalar_tensor_tensor(out=acc, in0=acc, scalar=2.0, in1=w, op0=ALU.mult, op1=ALU.add))
            dve.tensor_scalar(spl[:, 5, :], acc, -4.0, None, ALU.mult).then_inc(s["cond_done"], 1)

            def mod_out(n):
                c0 = ada_order[n // 2] * KD + 4 * (n % 2)
                dve.wait_ge(s["modT_ps"], next(g for g in ADA_GROUPS if g > n))
                dve.tensor_tensor(modT[:, c0:c0 + 4, :], PS[:, 7, 2 * c0:2 * c0 + 8].rearrange("p (n s) -> p n s", s=2),
                                  cols[:, A_BADA + c0:A_BADA + c0 + 4].unsqueeze(2).broadcast_to([P, 4, 2]),
                                  ALU.add).then_inc(s["mod_sb"], 1)

            for n in range(4):
                mod_out(n)
            dve.wait_ge(s["mod_sb"], 4)
            sc1 = cmod[:, 0]
            sh1 = cmod[:, 1]
            gcol = cols[:, A_LNG:A_LNG + KD].unsqueeze(2).broadcast_to([P, KD, 2])
            bcol = cols[:, A_LNB:A_LNB + KD].unsqueeze(2).broadcast_to([P, KD, 2])
            link(dve.tensor_scalar(sc1, modT[:, SC1 * KD:SC1 * KD + KD, :], 1.0, None, ALU.add))
            link(dve.tensor_tensor(sh1, sc1, bcol, ALU.mult))
            link(dve.tensor_tensor(sh1, sh1, modT[:, SH1 * KD:SH1 * KD + KD, :], ALU.add))
            link(dve.tensor_tensor(sc1, sc1, gcol, ALU.mult))
            dve.wait_ge(s["xT_sb"], 6)
            for k in range(KD):
                for q, (c0, n) in enumerate(SEG):
                    last = dve.tensor_scalar(hT[:, k, c0:c0 + n], hT[:, k, c0:c0 + n], cmod[:, 0, k, q:q + 1],
                                             cmod[:, 1, k, q:q + 1], ALU.mult, ALU.add)
                last.then_inc(s["h_done"], 1)

            dve.wait_ge(s["zeroed"], 3)
            for c in range(CR):
                dve.wait_ge(s["win_sb"], c + 1)
                for k in range(4):
                    cw = cols[:, A_CW + 4 * k + c:A_CW + 4 * k + c + 1]
                    if k == 0:
                        link(dve.tensor_scalar(xc[:, c, :], xpad[:, c, 0:W], cw, cols[:, A_CB + c:A_CB + c + 1],
                                               ALU.mult, ALU.add))
                    elif k < 3:
                        link(dve.scalar_tensor_tensor(out=xc[:, c, :], in0=xpad[:, c, k:k + W], scalar=cw,
                                                      in1=xc[:, c, :], op0=ALU.mult, op1=ALU.add))
                    else:
                        dve.scalar_tensor_tensor(out=xc[:, c, :], in0=xpad[:, c, k:k + W], scalar=cw,
                                                 in1=xc[:, c, :], op0=ALU.mult, op1=ALU.add).then_inc(s["conv_done"], 1)
            for g in range(FG):
                dve.wait_ge(s["f_ps"], g + 1)
                if g >= 2:
                    dve.wait_ge(s["yf_ps"], g - 1)
                dve.tensor_copy(FTs[:, g % 2, :], PS[:, 4, 0:TOK]).then_inc(s["f_sb"], 1)
                dve.wait_ge(s["yf_ps"], g + 1)
                dve.wait_ge(s["p1_used"], 7)
                dve.tensor_scalar(mixT[:, CR + g, :], PS[:, 5, 0:TOK], cols[:, NA + B_FB + g:NA + B_FB + g + 1], None,
                                  ALU.add).then_inc(s["yf_sb"], 1)
            for n in range(4, 6):
                mod_out(n)

            for b in range(2):
                for it in range(4 * b, 4 * b + 4):
                    v_, t_ = gtmp[:, 2, it % 4], vtmp[:, :]
                    dve.wait_ge(s["tanh_done"], 2 * it + 1)
                    link(dve.tensor_scalar(t_, v_, -1.0, 1.0, ALU.mult, ALU.add))
                    link(dve.reciprocal(t_, t_))
                    link(dve.scalar_tensor_tensor(out=v_, in0=v_, scalar=-2.0, in1=t_, op0=ALU.mult, op1=ALU.mult))
                    dve.tensor_scalar(v_, v_, 0.0, None, ALU.max).then_inc(s["rec_v"], 1)
                if b == 1:
                    for n in range(6, 10):
                        mod_out(n)
                dve.wait_ge(s["mult_done"], b + 1)
                dve.wait_ge(s["q_done"], 4 * b + 4)
                dve.wait_ge(s["tanh_done"], 8 * b + 8)
                link(dve.scalar_tensor_tensor(out=gtmp[:, 1], in0=gtmp[:, 2], scalar=0.5, in1=gtmp[:, 1],
                                              op0=ALU.mult, op1=ALU.mult))
                for it in range(4 * b, 4 * b + 4):
                    c, d = it // 2, it % 2
                    for n, (c0, m) in enumerate(SEG):
                        st = cols[:, NA + B_ST + 4 * d + c:NA + B_ST + 4 * d + c + 1] if n else 0.0
                        a_, b_, h_ = (v[:, c0:c0 + m] for v in (gtmp[:, 0, it % 4], gtmp[:, 1, it % 4], hfb[:, d]))
                        if d:
                            a_, b_, h_ = a_[:, ::-1], b_[:, ::-1], h_[:, ::-1]
                        sc_ = dve.tensor_tensor_scan(h_, a_, b_, st, ALU.mult, ALU.add)
                        if n == 0:
                            step(sc_)
                    sc_.then_inc(s["scan_done"], 1)
                    dve.wait_ge(s["scan_done"], it + 1)
                    dve.wait_ge(s["dve_step"], n_step[0])
                    edge = 0 if d else SEQ - 1
                    dve.tensor_copy(stin[:, 4 * d + c:4 * d + c + 1], hfb[:, d, edge:edge + 1]).then_inc(s["state_done"], 1)
                    dve.wait_ge(s["state_done"], it + 1)
                    if d:
                        dve.wait_ge(s["gelu_done"], 1)
                        for c0, m in SEG:
                            link(dve.tensor_tensor(hfb[:, 1, c0:c0 + m], hfb[:, 0, c0:c0 + m], hfb[:, 1, c0:c0 + m],
                                                   ALU.add))
                        for (c0, m), (k0, _) in zip(SEG, SEGC):
                            step(dve.scalar_tensor_tensor(out=mixT[:, c, k0:k0 + m], in0=hfb[:, 1, c0:c0 + m],
                                                          scalar=0.5, in1=gr[:, c, c0:c0 + m], op0=ALU.mult, op1=ALU.mult))
                        dve.wait_ge(s["dve_step"], n_step[0])
                        dve.nop().then_inc(s["yr_done"], 1)

            dve.wait_ge(s["row_sb"], 6)
            dve.wait_ge(s["xn_done"], NT)
            dve.wait_ge(s["ln1_in"], 32)

            def low_parts(i):
                dve.wait_ge(s["h2b1"], i + 1)
                dve.wait_ge(s["h2T_ps"], i + 1)
                dve.tensor_tensor(tt[:, i % 2, :], tt[:, i % 2, :], h2b[:, 0, i, :], ALU.subtract).then_inc(s["h2r"], 1)
                dve.wait_ge(s["h2b2"], i + 1)
                dve.wait_ge(s["h2r"], i + 1)
                dve.tensor_tensor(h2b[:, 2, i, :], tt[:, i % 2, :], h2b[:, 1, i, :], ALU.subtract).then_inc(s["h2b3"], 1)

            for i in range(NT):
                if i < NT - 1:
                    dve.wait_ge(s["mix_ps"], i + 1)
                else:
                    dve.wait_ge(s["p1_used"], 15)
                if i >= 2:
                    low_parts(i - 2)
                    dve.wait_ge(s["h2b3"], i - 1)
                m = tt[:, i % 2, :]
                link(dve.tensor_tensor(m, PS[:, 2 * i:2 * i + 2, :].rearrange("p a n -> p (a n)"),
                                       rows[:, 1 if i else 0, :], ALU.mult))
                link(dve.scalar_tensor_tensor(out=m, in0=xn[:, i, :], scalar=ALPHA, in1=m, op0=ALU.mult, op1=ALU.add))
                norm_stats(m, i, stat[:, i, :])
                dve.tensor_scalar(m, m, stat[:, i, 12:13], stat[:, i, 13:14], ALU.subtract, ALU.mult)\
                    .then_inc(s["x1n"], 1)
            low_parts(1)
            low_parts(2)
            for n in range(10, 12):
                mod_out(n)

            dve.wait_ge(s["lg_ps"], 1)
            dve.wait_ge(s["rtr_in"], 64)
            link(dve.tensor_tensor(lg[:, :, :], PS[:, 0, 0:NT * 20].rearrange("p (i n) -> p i n", n=20),
                                   rb[:, :].unsqueeze(1).broadcast_to([P, NT, 20]), ALU.add))
            gl, el = lg[:, :, 0:NG], lg[:, :, NG:]

            def wide(v, n):
                return v.unsqueeze(2).broadcast_to([P, NT, n])

            def first_max(x, n, code, oh, mx, tmp):
                link(dve.tensor_reduce(mx, x, AX.X, ALU.max))
                link(dve.tensor_tensor(tmp, x, wide(mx, n), ALU.is_equal))
                cd = cst[:, code:code + n].unsqueeze(1).broadcast_to([P, NT, n])
                link(dve.tensor_tensor(tmp, tmp, cd, ALU.mult))
                link(dve.tensor_reduce(rs[:, 11, :], tmp, AX.X, ALU.max))
                link(dve.tensor_tensor(oh, cd, wide(rs[:, 11, :], n), ALU.is_equal))

            dve.wait_ge(s["st_ps"], 1)
            dve.tensor_copy(strow[0:8, :], PS[0:8, 2, 128:256]).then_inc(s["st_row"], 1)

            og, oh1, oh2, asg = rt[:, 0, :, 0:NG], rt[:, 1], rt[:, 2], rt[:, 3]
            first_max(gl, NG, C_COD4, og, rs[:, 0, :], rt[:, 4, :, 0:NG])
            link(dve.tensor_tensor(rt[:, 5, :, 0:NG], gl, wide(rs[:, 0, :], NG), ALU.subtract))
            marks = og.unsqueeze(3).broadcast_to([P, NT, NG, EPG])
            m4 = rt[:, 4].rearrange("p i (g e) -> p i g e", e=EPG)
            link(dve.tensor_copy(m4, marks))
            link(dve.tensor_tensor(rt[:, 7], el, rt[:, 4], ALU.mult))
            link(dve.tensor_scalar(rt[:, 4], rt[:, 4], -1.0, 1e30, ALU.add, ALU.mult))
            link(dve.tensor_tensor(rt[:, 7], rt[:, 7], rt[:, 4], ALU.add))
            first_max(rt[:, 7], NE, C_COD16, oh1, rs[:, 1, :], rt[:, 4])
            link(dve.scalar_tensor_tensor(out=rt[:, 7], in0=oh1, scalar=-2e30, in1=rt[:, 7], op0=ALU.mult, op1=ALU.add))
            first_max(rt[:, 7], NE, C_COD16, oh2, rs[:, 2, :], rt[:, 4])
            link(dve.tensor_tensor(asg, oh1, oh2, ALU.add))
            dve.tensor_tensor(rs[:, 4, :], rs[:, 2, :], rs[:, 1, :], ALU.subtract).then_inc(s["assign_done"], 1)
            dve.wait_ge(s["pos_pool"], 2)
            link(dve.tensor_reduce(rs[:, 6, :], rt[:, 6, :, 0:NG], AX.X, ALU.add))
            link(dve.tensor_scalar(rs[:, 7, :], rs[:, 5, :], 1.0, None, ALU.add))
            link(dve.tensor_tensor(rs[:, 6, :], rs[:, 6, :], rs[:, 7, :], ALU.mult))
            link(dve.reciprocal(wk[:, 0, :], rs[:, 6, :]))
            link(dve.tensor_tensor(wk[:, 1, :], wk[:, 0, :], rs[:, 5, :], ALU.mult))
            dve.wait_ge(s["rank_ps"], 1)
            rank = PS[:, 1, 0:NT * NE].rearrange("p (i e) -> p i e", e=NE)
            link(dve.scalar_tensor_tensor(out=rt[:, 4], in0=rank, scalar=1.0, in1=asg, op0=ALU.add, op1=ALU.mult))
            link(dve.tensor_scalar(rankA[:, 0:NE, :].rearrange("p e i -> p i e"), rt[:, 4], -1.0, None, ALU.add))
            link(dve.tensor_reduce(small[:, 0:1], PS[:, 1, NT * NE:(NT + 1) * NE], AX.X, ALU.max))
            dve.tensor_copy(cnt[:, 0:1], small[:, 0:1]).then_inc(s["route_done"], 1)
            erow = cst[:, C_EROW:C_EROW + NE].unsqueeze(1).broadcast_to([P, NT, NE])
            for q, oh in enumerate((oh1, oh2)):
                for k, v in enumerate((rank, erow)):
                    link(dve.tensor_tensor(rt[:, 4], v, oh, ALU.mult))
                    link(dve.tensor_reduce(posf[:, k, q, :], rt[:, 4], AX.X, ALU.add))
            for pb in range(PASSES):
                r, b = posf[:, 0], posf[:, 2]
                if pb:
                    link(dve.tensor_scalar(r, r, float(-CAP), None, ALU.add))
                link(dve.tensor_scalar(b, r, 0.0, FAR, ALU.is_lt, ALU.mult))
                link(dve.tensor_tensor(b, b, r, ALU.add))
                link(dve.tensor_tensor(b, b, posf[:, 1], ALU.add))
                link(dve.tensor_copy(posn[:, pb], b))
                link(dve.tensor_scalar(b, r, CAP - 0.5, FAR, ALU.is_gt, ALU.mult))
                link(dve.tensor_tensor(b, b, posn[:, pb], ALU.add))
                link(dve.tensor_copy(posn[:, pb], b))
            dve.nop().then_inc(s["route_done"], 1)

            def split_lo(ge, p, j):
                for h, (a, b) in enumerate([(0, UNIT // 2), (UNIT // 2, UNIT)]):
                    dve.wait_ge(s["hi_done"], ge * 6 + (2 * j + h + 1))
                    dve.tensor_tensor(wlo[3 * p + j][:, a:b], ring[3 * p + j][:, a:b], whi[j][:, a:b].bitcast(F32),
                                      ALU.subtract).then_inc(s["lo_done"], 1)

            def x_lo(ge):
                dve.wait_ge(s["xs_hi"], ge + 1)
                need(dve, "unit_used", ge * 3 - 1)
                dve.tensor_tensor(xsL[:, :, :], PS[:, 0:2, :].rearrange("p a (k n) -> p (a k) n", n=CAP),
                                  xsH[:, :, :].bitcast(F32), ALU.subtract).then_inc(s["xs_ready"], 1)

            def choose(ge, e, pb):
                need(dve, "x_disp", ge)
                i0 = cst[:, bass.ds(pb * CAP + C_IOTA, CAP)] if not isinstance(pb, int) else \
                    cst[:, C_IOTA + pb * CAP:C_IOTA + (pb + 1) * CAP]
                ra = rankA[:, bass.ds(e, 1), :].rearrange("p a i -> p (a i)") if not isinstance(e, int) else rankA[:, e, :]
                dve.tensor_tensor(sel[:, :, :], i0.unsqueeze(1).broadcast_to([P, NT, CAP]),
                                   ra.unsqueeze(2).broadcast_to([P, NT, CAP]), ALU.is_equal).then_inc(s["sel_ready"], 1)

            def prologue(ge, pb):
                if isinstance(ge, int):
                    dve.wait_ge(s["route_done"], 2)
                choose(ge, 0, pb)
                split_lo(ge, 0, 0)
                x_lo(ge)
                split_lo(ge, 0, 1)
                split_lo(ge, 0, 2)

            def body(ge, e, q, p, last, pb):
                if not last:
                    choose(ge + 1, e + 1, pb)
                    split_lo(ge + 1, 1 - p, 0)
                dve.wait_ge(s["unit_used"], ge * 3 + 2)
                dve.wait_ge(s["silu_done"], ge + 1)
                dve.tensor_tensor(hid[:, :], sg[:, :], PS[:, 3, :], ALU.mult).then_inc(s["hid_ready"], 1)
                if not last:
                    x_lo(ge + 1)
                dve.wait_ge(s["ht_hi"], ge + 1)
                dve.tensor_tensor(hTL[:, :, :], PS[:, 4, :].rearrange("p (k n) -> p k n", n=CAP),
                                  hTH[:, :, :].bitcast(F32), ALU.subtract).then_inc(s["hts_ready"], 1)
                if not last:
                    split_lo(ge + 1, 1 - p, 1)
                    split_lo(ge + 1, 1 - p, 2)

            passes(dve, lambda pb: pairs(dve, lambda ge: prologue(ge, pb), lambda *a: body(*a, pb), pb), lambda: None)

            dve.wait_ge(s["g2_ps"], 1)
            dve.wait_ge(s["ln2_in"], 32)
            for i in range(NT):
                dve.wait_ge(s["gathered"], 1)
                m = fin[:, i, :]
                link(dve.tensor_scalar(m, y12[:, 0, i, :], wk[:, 0, i:i + 1], None, ALU.mult))
                link(dve.scalar_tensor_tensor(out=m, in0=y12[:, 1, i, :], scalar=wk[:, 1, i:i + 1], in1=m,
                                              op0=ALU.mult, op1=ALU.add))
                b = 2 if i else 0
                link(dve.tensor_tensor(m, m, PS[:, b:b + 2, :].rearrange("p a n -> p (a n)"), ALU.mult))
                link(dve.scalar_tensor_tensor(out=m, in0=xn[:, i, :], scalar=ALPHA, in1=m, op0=ALU.mult, op1=ALU.add))
                norm_stats(m, i, stat[:, i, :])
                link(dve.tensor_scalar(m, m, stat[:, i, 12:13], stat[:, i, 13:14], ALU.subtract, ALU.mult))
                link(dve.tensor_tensor(m, m, ln2[:, 0, :], ALU.mult))
                dve.tensor_tensor(m, m, ln2[:, 1, :], ALU.add).then_inc(s["fin_done"], 1)

        @block.gpsimd
        def _(pool):
            n_step = [0]

            def link(ins):
                n_step[0] += 1
                ins.then_inc(s["pool_step"], 1)
                pool.wait_ge(s["pool_step"], n_step[0])

            pool.memset(wbd[:, :, :], 0.0).then_inc(s["zeroed"], 1)
            pool.memset(cond32[:, :, :], 0.0).then_inc(s["zeroed"], 1)
            pool.memset(rankA[:, NE:NE + 1, :], -1.0)
            pool.memset(xpad[:, :, 0:2], 0.0)
            pool.memset(xpad[:, :, 2 + W:XW], 0.0)
            pool.memset(hT[:, :, SEQ:SEQ + 3], 0.0)
            pool.memset(hT[:, :, W - 1:W], 0.0).then_inc(s["zeroed"], 1)
            pool.wait_ge(s["x_in"], 16 * NT)
            pool.wait_ge(s["pos_in"], 16)
            for i in range(1, NT):
                pool.tensor_tensor(xn[:, i, :], xn[:, i, :], pos[:, i - 1, :], ALU.add).then_inc(s["xn_pool"], 1)
            pool.wait_ge(s["lnin_in"], 32)
            pool.wait_ge(s["xT_ps"], 6)
            for i in range(NT):
                link(pool.tensor_tensor(xn[:, i, :], xn[:, i, :], lnin[:, 0, :], ALU.mult))
                pool.tensor_tensor(xn[:, i, :], xn[:, i, :], lnin[:, 1, :], ALU.add).then_inc(s["xn_done"], 1)

            def q_item(it):
                pool.wait_ge(s["gate_act"], it + 1)
                g = gtmp[:, 1, it % 4]
                link(pool.tensor_scalar(g, g, 1.0, None, ALU.add))
                pool.tensor_tensor(g, g, xc[:, it // 2, :], ALU.mult).then_inc(s["q_done"], 1)

            pool.wait_ge(s["win_sb"], 12)
            pool.wait_ge(s["conv_done"], CR)
            tg = xpad[:, :, 0:W]
            pool.tensor_tensor(tg, gr[:, :, :], gr[:, :, :], ALU.mult).then_inc(s["gelu_t"], 1)
            pool.wait_ge(s["gelu_t"], 1)
            pool.tensor_scalar(tg, tg, 0.044715, 1.0, ALU.mult, ALU.add).then_inc(s["gelu_t"], 1)
            pool.wait_ge(s["gelu_t"], 2)
            pool.tensor_tensor(tg, tg, gr[:, :, :], ALU.mult).then_inc(s["gelu_t"], 1)
            pool.wait_ge(s["gelu_th"], 1)
            link(pool.tensor_scalar(tg, tg, 1.0, None, ALU.add))
            pool.tensor_tensor(gr[:, :, :], gr[:, :, :], tg, ALU.mult).then_inc(s["gelu_done"], 1)
            for it in range(8):
                q_item(it)

            for i in range(NT):
                q = 1 if i else 0
                m = tt[:, i % 2, :]
                pool.wait_ge(s["x1n"], i + 1)
                link(pool.tensor_tensor(m, m, rows[:, 6, :], ALU.mult))
                link(pool.tensor_tensor(xn[:, i, :], m, rows[:, 7, :], ALU.add))
                link(pool.tensor_tensor(m, xn[:, i, :], rows[:, 2 + q, :], ALU.mult))
                pool.tensor_tensor(m, m, rows[:, 4 + q, :], ALU.add).then_inc(s["h2_done"], 1)

            pool.wait_ge(s["st_row"], 1)
            pool.dma_start(t["new_state"], strow[0:2 * CR, :]).then_inc(s["st_out"], 16)
            pool.wait_ge(s["st_out"], 16)

            pool.wait_ge(s["route_done"], 2)

            def run(pb):
                def body(ge, e, q, p, last):
                    pool.wait_ge(s["y_sb"], ge + 1)
                    dst = Y_dram[pb][bass.ds(e * CAP, CAP)]
                    pool.dma_start(dst, ysb[:, :]).then_inc(s["y_stored"], 16)

                pairs(pool, lambda ge: None, body, pb)
                pool.wait_ge(s["y_stored"], pb * (16 * NE) + 16 * NE)

            run(0)
            most = pool.value_load(cnt[0:1, 0:1], min_val=0, max_val=TOK)
            for pb in range(1, PASSES):
                with pool.If(most > pb * CAP):
                    run(pb)
            pool.nop().then_inc(s["passes_done"], 1)

            def gather(pb, name):
                for i in range(NT):
                    for q in range(2):
                        pool.indirect_dma_start(
                            out=y12[:, q, i, :], out_offset=None, in_=Y_dram[pb],
                            in_offset=bass.IndirectOffsetOnAxis(ap=posn[:, pb, q, i:i + 1], axis=0),
                            bounds_check=YROWS - 1, oob_is_err=False,
                        ).then_inc(s[name], 16)
                pool.wait_ge(s[name], 16 * 2 * NT)

            gather(0, "gathered0")
            for pb in range(1, PASSES):
                with pool.If(most > pb * CAP):
                    gather(pb, f"gathered{pb}")
            pool.nop().then_inc(s["gathered"], 1)

        @block.tensor
        def _(pe):
            ident = cst[:, C_ID:C_ID + P]
            ones = cst[:, C_ONE:C_ONE + P]

            pe.wait_ge(s["const_in"], 16)
            pe.wait_ge(s["rowA_in"], 16 * 7)
            pe.transpose(PS[:, 0, 0:NA], rowA[0:NA, :], cst[0:NA, C_ID:C_ID + NA])
            pe.wait_ge(s["rowB_in"], 16 * 5)
            pe.transpose(PS[:, 0, NA:NA + NB], rowB[0:NB, :], cst[0:NB, C_ID:C_ID + NB]).then_inc(s["cols_ps"], 1)

            def ada_sums(n, u):
                p1_loaded(pe, u)
                w = unit3(ring[(u + 1) % RING])
                if n == 1:
                    pe.wait_ge(s["xT_sb"], 6)
                elif n >= 2:
                    pe.wait_ge(s["mrow_sb"], n - 1 if n < 10 else n)
                for k in range(KD):
                    j = k % 4
                    mm = pe.matmul(PS[32 * j:32 * j + 32, ABANK[n], :], cond32[:, k, :], w[:, k, :],
                                   start=(k < 4), stop=(k >= 4))
                mm.then_inc(s["p1_used"], 1)

            def ada_cols(n):
                c0 = ada_order[n // 2] * KD + 4 * (n % 2)
                if n in ADA_GROUPS:
                    pe.wait_ge(s["mod_sb"], n)
                pe.wait_ge(s["mrow_sb"], n + 1)
                for q in range(4):
                    mm = pe.matmul(PS[:, 7, 2 * (c0 + q):2 * (c0 + q) + 2], mrow[:, q * P:(q + 1) * P],
                                   cst[:, C_SUM:C_SUM + 2], start=True, stop=True)
                mm.then_inc(s["modT_ps"], 1)

            for i in range(NT):
                pe.wait_ge(s["ln_xhat"], i + 1)
                if i == 0:
                    pe.wait_ge(s["cols_sb"], 1)
                for k in range(KD):
                    mm = pe.transpose(PS[:, 2 * i + k // 4, (k % 4) * P:(k % 4 + 1) * P], xn[:, i, k * P:(k + 1) * P], ident)
                    if k % 4 == 3:
                        mm.then_inc(s["xT_ps"], 1)
            pe.wait_ge(s["cond_done"], 6)
            ada_sums(0, 0)
            for n in range(4):
                if n < 3:
                    ada_sums(n + 1, n + 1)
                ada_cols(n)

            def project(w):
                if w % 4 == 0:
                    p1_loaded(pe, 4 + w // 4)
                if w < 4:
                    pe.wait_ge(s["xT_sb"], 6)
                else:
                    pe.wait_ge(s["win_sb"], w - 3)
                wt = unit3(ring[(5 + w // 4) % RING])
                for k in range(KD):
                    if w == 0:
                        pe.wait_ge(s["h_done"], k + 1)
                    mm = pe.matmul(PS[:, w % 4, 0:W], wt[:, k, (w % 4) * P:(w % 4 + 1) * P], hT[:, k, :],
                                   start=(k == 0), stop=(k == KD - 1))
                mm.then_inc(s["p1_used" if w % 4 == 3 else "win_ps"], 1)

            def chan_dft(g):
                pe.wait_ge(s["win_sb"], 4 + g + 1)
                if g == 0:
                    pe.wait_ge(s["smallw_in"], 32)
                    pe.wait_ge(s["mrow_sb"], 5)
                else:
                    pe.wait_ge(s["z_sb"], g)
                if g >= 2:
                    pe.wait_ge(s["yf_sb"], g - 1)
                for i in range(NT):
                    out = PS[:, 6, i * 256:(i + 1) * 256] if i < 2 else PS[:, 5, 0:256]
                    mm = pe.matmul(out, xf[:, g, TC[i]:TC[i] + P], dft[:, F_CH:F_CH + 256], start=True, stop=True)
                mm.then_inc(s["z_ps"], 1)

            def pos_dft(g):
                pe.wait_ge(s["z_sb"], g + 1)
                if g == 0:
                    pe.wait_ge(s["mrow_sb"], 6)
                need(pe, "f_sb", g)
                z = Z[:, g % 2]
                for h in range(2):
                    pe.matmul(PS[:, 4, 0:SEQ], z[:, 0, h * P:(h + 1) * P], dft[:, F_CTX + h * P:F_CTX + (h + 1) * P],
                              start=(h == 0), stop=(h == 1))
                for m in range(2):
                    for h in range(2):
                        mm = pe.matmul(PS[:, 4, SEQ:TOK], z[:, 1 + m, h * P:(h + 1) * P],
                                       dft[:, F_LAT + 512 * m + 256 * h:F_LAT + 512 * m + 256 * (h + 1)],
                                       start=(m == 0 and h == 0), stop=(m == 1 and h == 1))
                mm.then_inc(s["f_ps"], 1)

            def fourier_out(g):
                pe.wait_ge(s["f_sb"], g + 1)
                pe.wait_ge(s["z_sb"], min(g + 2, FG))
                need(pe, "yf_sb", g)
                pe.matmul(PS[:, 5, 0:TOK], fnw[:, g, :], FTs[:, g % 2, :], start=True, stop=True).then_inc(s["yf_ps"], 1)

            for w in range(12):
                project(w)
            ada_sums(4, 7)
            ada_sums(5, 8)
            ada_cols(4)
            ada_cols(5)
            for g in range(FG + 1):
                if g < FG:
                    chan_dft(g)
                if g > 0:
                    pos_dft(g - 1)
                    fourier_out(g - 1)

            pe.wait_ge(s["wbd_in"], 64)
            for it in range(8):
                c, d = it // 2, it % 2
                pe.wait_ge(s["conv_done"], c + 1)
                if it >= 2:
                    pe.wait_ge(s["gate_act"], it - 1)
                else:
                    pe.wait_ge(s["win_sb"], 12)
                for gi in range(2):
                    mm = pe.matmul(PS[:, 2 * (it % 2) + gi, 0:W], wbd[:, 8 * gi + 4 * d + c, :], xc[:, c, :],
                                   start=True, stop=True)
                mm.then_inc(s["gate_ps"], 1)
                if it == 2:
                    pe.wait_ge(s["f_sb"], FG)
                if 2 <= it < 6:
                    ada_sums(it + 4, it + 7)
                if 3 <= it < 7:
                    ada_cols(it + 3)

            def row(r, j, q):
                if r > 0:
                    pe.wait_ge(s["row_sb"], r)
                else:
                    pe.wait_ge(s["mod_sb"], 10)
                for k in range(KD):
                    mm = pe.matmul(PS[:, 6 + k // 4, (k % 4) * P:(k % 4 + 1) * P],
                                   modT[:, j * KD + k, q:q + 1].broadcast_to([P, P]), ident, start=True, stop=True)
                mm.then_inc(s["row_ps"], 1)

            def mix(h):
                p1_loaded(pe, 13 + h)
                for i in range(NT):
                    for c in range(KD):
                        mm = pe.matmul(PS[:, 2 * i + h, :], mixT[:, c, i * P:(i + 1) * P],
                                       unit3(ring[(14 + h) % RING])[:, c, :], start=(c == 0), stop=(c == KD - 1))
                    if i == NT - 1:
                        mm.then_inc(s["p1_used"], 1)
                    elif h == 1:
                        mm.then_inc(s["mix_ps"], 1)

            row(0, G1, 0)
            row(1, G1, 1)
            pe.wait_ge(s["gate_act"], 8)
            pe.wait_ge(s["yr_done"], CR)
            mix(0)
            mix(1)
            for r, (j, q) in enumerate(((SC2, 0), (SC2, 1), (SH2, 0), (SH2, 1))):
                row(2 + r, j, q)
            pe.wait_ge(s["row_sb"], 6)
            for n in range(10, 12):
                ada_sums(n, n + 5)
                ada_cols(n)

            for i in range(NT):
                pe.wait_ge(s["h2_done"], i + 1)
                for k in range(KD):
                    mm = pe.transpose(PS[:, 2 * i + k // 4, (k % 4) * P:(k % 4 + 1) * P], tt[:, i % 2, k * P:(k + 1) * P], ident)
                mm.then_inc(s["h2T_ps"], 1)
            pe.wait_ge(s["rtr_in"], 64)
            pe.wait_ge(s["x1n"], NT)
            for i in range(NT):
                pe.wait_ge(s["h2T_sb"], i + 1)
                for k in range(KD):
                    mm = pe.matmul(PS[:, 0, 20 * i:20 * i + 20], h2T[:, k, i * P:(i + 1) * P], wr[:, k, :],
                                   start=(k == 0), stop=(k == KD - 1))
            mm.then_inc(s["lg_ps"], 1)
            pe.wait_ge(s["state_done"], 8)
            pe.transpose(PS[0:8, 2, 128:256], stin[:, 0:8], ident).then_inc(s["st_ps"], 1)
            pe.wait_ge(s["assign_done"], 1)
            for i in range(NT + 1):
                for j in range(min(i, NT - 1) + 1):
                    mm = pe.matmul(PS[:, 1, NE * i:NE * (i + 1)], cst[:, C_TRI:C_TRI + P] if j == i else ones,
                                   rt[:, 3, j, :], start=(j == 0), stop=(j == min(i, NT - 1)))
            mm.then_inc(s["rank_ps"], 1)

            def dispatch(ge):
                pe.wait_ge(s["sel_ready"], ge + 1)
                need(pe, "xs_ready", ge)
                for k in range(KD):
                    for n in range(3 * NT):
                        part, i = n // NT, n % NT
                        mm = pe.matmul(PS[:, k // 4, (k % 4) * P:(k % 4 + 1) * P], h2b[:, 2 - part, i, k * P:(k + 1) * P],
                                       sel[:, i, :], start=(n == 0), stop=(n == 3 * NT - 1))
                mm.then_inc(s["x_disp"], 1)

            def prologue(ge):
                if isinstance(ge, int):
                    pe.wait_ge(s["h2b3"], NT)
                    pe.wait_ge(s["route_done"], 2)
                dispatch(ge)

            def body(ge, e, q, p, last):
                for j in range(2):
                    pe.wait_ge(s["lo_done"], ge * 6 + (2 * j + 2))
                    if j == 0:
                        pe.wait_ge(s["xs_ready"], ge + 1)
                        need(pe, "silu_done", ge)
                    else:
                        need(pe, "hid_ready", ge)
                    hi, lo = unit3(whi[j]), unit3(wlo[3 * p + j])
                    for k in range(KD):
                        pe.matmul(PS[:, 2 + j, :], xsH[:, k, :], hi[:, k, :], start=(k == 0), stop=False)
                        pe.matmul(PS[:, 2 + j, :], xsH[:, k, :], lo[:, k, :], start=False, stop=False)
                        mm = pe.matmul(PS[:, 2 + j, :], xsL[:, k, :], hi[:, k, :], start=False, stop=(k == KD - 1))
                    mm.then_inc(s["unit_used"], 1)
                if not last:
                    dispatch(ge + 1)
                pe.wait_ge(s["hid_ready"], ge + 1)
                need(pe, "hts_ready", ge)
                for k in range(KF):
                    mm = pe.transpose(PS[:, 4, k * P:(k + 1) * P], hid[:, k * P:(k + 1) * P], ident)
                mm.then_inc(s["ht_ps"], 1)
                pe.wait_ge(s["hts_ready"], ge + 1)
                pe.wait_ge(s["lo_done"], ge * 6 + 6)
                need(pe, "y_sb", ge)
                hi, lo = unit3(whi[2], D), unit3(wlo[3 * p + 2], D)
                for k in range(KF):
                    for x, w in ((hTH, hi), (hTH, lo), (hTL, hi)):
                        for h in range(2):
                            mm = pe.matmul(PS[:, 5 + h, :], x[:, k, :], w[:, k, h * 512:(h + 1) * 512],
                                           start=(k == 0 and x is hTH and w is hi),
                                           stop=(k == KF - 1 and x is hTL))
                mm.then_inc(s["unit_used"], 1)

            passes(pe, lambda pb: pairs(pe, prologue, body, pb), lambda: None)
            pe.wait_ge(s["passes_done"], 1)
            for q in range(2):
                for k in range(KD):
                    mm = pe.matmul(PS[:, 2 * q + k // 4, (k % 4) * P:(k % 4 + 1) * P],
                                   modT[:, G2 * KD + k, q:q + 1].broadcast_to([P, P]), ident, start=True, stop=True)
            mm.then_inc(s["g2_ps"], 1)


_INS = ["x_prompt", "x_sample", "w_ada", "w_in", "rg_wa", "rg_wi", "fn_w", "w_out", "router_g_w", "router_e_w",
        "router_g_b", "router_e_b", "ex_w_gate", "ex_w_up", "ex_w_down", "ln1_g", "ln1_b", "ln2_g", "ln2_b"]
_ROWS = ["c", "c_ctx", "b_ada", "ln_in_g", "ln_in_b", "conv_w", "conv_b", "rg_ba", "rg_bi", "rg_lam", "fn_b"]


def kernel(**inputs):
    import concourse.bacc as _bacc
    from concourse.bass_utils import run_bass_kernel_spmd as _run

    nc = _bacc.Bacc("TRN2", target_bir_lowering=False, num_devices=1)
    const, dft, pos = constants()
    arrays = {"const": const, "dft": dft, "pos": pos}
    for name in _INS:
        arrays[name] = np.ascontiguousarray(inputs[name])
    for name in _ROWS:
        arrays[name] = np.ascontiguousarray(inputs[name]).reshape(-1, P)
    arrays["state"] = np.ascontiguousarray(inputs["state_rglru"]).reshape(-1, P)
    for name in ("ln_in_g", "ln_in_b"):
        arrays[name + "_row"] = np.ascontiguousarray(inputs[name])
    for name in ("ln1_g", "ln1_b", "ln2_g", "ln2_b", "router_g_b", "router_e_b"):
        arrays[name] = arrays[name].reshape(-1)
    t = {n: nc.dram_tensor("in_" + n, a.shape, mybir.dt.from_np(a.dtype), kind="ExternalInput").ap()
         for n, a in arrays.items()}
    outs = {"y_prompt": (1, SEQ, D), "y_sample": (1, LAT, D), "new_state": (8, P)}
    for n, shape in outs.items():
        t[n] = nc.dram_tensor("out_" + n, shape, F32, kind="ExternalOutput").ap()
    build(nc, t)
    r = _run(nc, [{"in_" + n: a for n, a in arrays.items()}], core_ids=[0]).results[0]
    return (r["out_y_prompt"], r["out_y_sample"], r["out_new_state"].reshape(1, 1, 2, DR))
```

```python
from contextlib import ExitStack

import numpy as np

import concourse.bass as bass
from concourse import mybir

F32 = mybir.dt.float32
F32R = mybir.dt.float32r
BF16 = mybir.dt.bfloat16
U32 = mybir.dt.uint32
I32 = mybir.dt.int32
ALU = mybir.AluOpType
ACT = mybir.ActivationFunctionType
AX = mybir.AxisListType

P = 128
D = 1024
KD = D // P
SEQ = 128
LAT = 256
TOK = SEQ + LAT
NT = TOK // P
DR = D // 2
CR = DR // P
FG = 4
NE = 16
NG = 4
EPG = NE // NG
FE = D // 2
KF = FE // P
GRID_W = 64
ALPHA = 2.0 ** 0.25
LN_EPS = 1e-5
W = SEQ + 3 + LAT + 1
TC = [0, SEQ + 3, SEQ + 3 + P]
SEG = [(0, SEQ), (SEQ + 3, LAT)]
SEGC = [(0, SEQ), (SEQ, LAT)]
XW = W + 3
UNIT = 4096
RING = 6
NP1 = 17
HALF = P // 2
CAP = P
PASSES = TOK // CAP
YROWS = NE * CAP
FAR = 1e5

C_ID, C_TRI, C_ONE, C_IOTA = 0, 128, 256, 384
C_EROW, C_COD16, C_COD4 = C_IOTA + TOK, C_IOTA + TOK + 16, C_IOTA + TOK + 32
C_SUM = C_COD4 + 4
C_TWO = C_SUM + 2
NCONST = C_TWO + 64
F_CH, F_CTX, F_LAT = 0, 256, 512
NDFT = 512 + 2 * 512

A_C, A_CTX, A_BADA, A_LNG, A_LNB, A_CW, A_CB, NA = 0, 8, 16, 64, 72, 80, 96, 100
B_BA, B_BI, B_LAM, B_ST, B_FB, NB = 0, 8, 16, 24, 32, 36

SH1, SC1, G1, SH2, SC2, G2 = range(6)


def constants():
    c = np.zeros((P, NCONST), np.float32)
    c[:, C_ID:C_ID + P] = np.eye(P)
    c[:, C_TRI:C_TRI + P] = np.triu(np.ones((P, P)), 1)
    c[:, C_ONE:C_ONE + P] = 1
    c[:, C_IOTA:C_IOTA + TOK] = np.arange(TOK)
    c[:, C_EROW:C_EROW + NE] = np.arange(NE) * CAP
    c[:, C_COD16:C_COD16 + NE] = NE - np.arange(NE)
    c[:, C_COD4:C_COD4 + NG] = NG - np.arange(NG)
    for q in range(2):
        c[q::32, C_SUM + q] = 1
        c[64 * q:64 * q + 64, C_TWO:C_TWO + 64] = np.eye(64)

    def dft(n):
        a = 2 * np.pi * (np.outer(np.arange(n), np.arange(n)) % n) / n
        return np.cos(a) / np.sqrt(n), np.sin(a) / np.sqrt(n)

    f = np.zeros((P, NDFT), np.float32)
    co, si = dft(P)
    f[:, 0:P], f[:, P:2 * P] = co, si
    f[:, F_CTX:F_CTX + P], f[:, F_CTX + P:F_CTX + 2 * P] = co, -si
    co, si = dft(LAT)
    for m in range(2):
        f[:, F_LAT + 512 * m:F_LAT + 512 * m + LAT] = co[m * P:(m + 1) * P]
        f[:, F_LAT + 512 * m + LAT:F_LAT + 512 * (m + 1)] = -si[m * P:(m + 1) * P]

    q = D // 4
    freqs = (1.0 / (10000.0 ** (np.arange(q, dtype=np.float32) / q))).astype(np.float32)
    r = np.repeat(np.arange(LAT // GRID_W, dtype=np.float32), GRID_W)[:, None] * freqs[None]
    k = np.tile(np.arange(GRID_W, dtype=np.float32), LAT // GRID_W)[:, None] * freqs[None]
    pos = np.concatenate([np.sin(r), np.cos(r), np.sin(k), np.cos(k)], axis=-1).astype(np.float32)
    return c, f, pos


def build(nc, t):
    ctx = ExitStack()
    with ctx:
        def sem(name):
            return ctx.enter_context(nc.semaphore(name))

        def at(name, off, shape, dt=F32):
            return nc.alloc_sbuf_tensor_at(name, shape, dt, offset=off)

        base = (nc._sbuf_addr_for_side("left") + 31) // 32 * 32
        RB = UNIT * 4
        ring = [at(f"ring{s}", base + s * RB, [P, UNIT]) for s in range(RING)]
        wlo = [at(f"wlo{s}", base + s * RB, [P, UNIT], F32R) for s in range(RING)]
        o = base + RING * RB
        xn = at("xn", o, [P, NT, D])
        o += NT * D * 4
        place = [o]

        def keep(name, shape, dt=F32):
            n = int(np.prod(shape[1:])) * (2 if dt == BF16 else 4)
            n = (n + 31) // 32 * 32
            place[0] += n
            return at(name, place[0] - n, shape, dt)

        cst = keep("cst", [P, NCONST])
        modT = keep("modT", [P, 6 * KD, 2])
        mrow = keep("mrow", [P, 512])
        cols = keep("cols", [P, NA + NB])
        cond = keep("cond", [P, KD, 2])
        cond32 = keep("cond32", [P, KD, 32])
        cmod = keep("cmod", [P, 2, KD, 2])
        bga = keep("bga", [P, 16])
        spl = keep("spl", [P, 6, 8])
        stat = keep("stat", [P, NT, 16])
        stin = keep("stin", [P, 16])
        small = keep("small", [P, 8])
        rankA = keep("rankA", [P, NE + 1, NT])
        posn = keep("posn", [P, PASSES, 2, NT], U32)
        wk = keep("wk", [P, 2, NT])
        cnt = keep("cnt", [P, 1 + NE], I32)
        strow = keep("strow", [P, P])
        router0 = place[0]
        wr = keep("wr", [P, KD, NG + NE])
        rb = keep("rb", [P, NG + NE])
        lg = keep("lg", [P, NT, NG + NE])
        rt = keep("rt", [P, 8, NT, NE])
        rs = keep("rs", [P, 12, NT])
        posf = keep("posf", [P, 3, 2, NT])
        place[0] = max(place[0], router0 + D * 4)
        ylow = at("ylow", router0, [HALF, D])
        A0 = place[0]
        AREA = A0
        h2b = at("h2b", A0, [P, 3, NT, D], BF16)
        o = A0 + 3 * NT * D * 2
        M0 = o
        xsH = at("xsH", o, [P, KD, CAP], F32R); o += KD * CAP * 4
        xsL = at("xsL", o, [P, KD, CAP], F32R); o += KD * CAP * 4
        hTH = at("hTH", o, [P, KF, CAP], F32R); o += KF * CAP * 4
        hTL = at("hTL", o, [P, KF, CAP], F32R); o += KF * CAP * 4
        sgT = at("sgT", o - KF * CAP * 4, [P, KF, HALF])
        hidT = at("hidT", o - KF * CAP * 2, [P, KF, HALF])
        sel = at("sel", o, [P, NT, CAP], BF16); o += NT * CAP * 2
        sg = at("sg", o, [P, FE]); o += FE * 4
        hid = at("hid", o, [P, FE]); o += FE * 4
        ysb = at("ysb", o, [P, D]); o += D * 4
        tt = at("tt", M0, [P, 2, D])
        h2T = at("h2T", M0 + 2 * D * 4, [P, KD, TOK])
        B0 = max(o, M0 + 2 * D * 4 + KD * TOK * 4)
        whi = [at(f"whi{j}", B0 + j * RB, [P, UNIT], F32R) for j in range(3)]
        end = B0 + 3 * RB
        assert end <= base + nc.sbuf_bytes_remaining
        hT = at("hT", B0, [P, KD, W])
        mixT = at("mixT", B0, [P, KD, TOK])
        FTs = at("FTs", B0 + KD * W * 4, [P, 2, TOK])
        rtmp = at("rtmp", B0 + KD * W * 4, [P, 2, W])
        assert KD * W * 4 + 2 * W * 4 <= RB
        o = B0 + RB
        gr = at("gr", o, [P, CR, W]); o += CR * W * 4
        xf = at("xf", o, [P, FG, W]); o += FG * W * 4
        Z = at("Z", o, [P, 2, NT, 2 * P]); o += 2 * NT * 2 * P * 4
        dft = at("dft", o, [P, NDFT]); o += NDFT * 4
        fnw = at("fnw", o, [P, FG, P]); o += FG * P * 4
        hfb = at("hfb", o, [P, 2, W]); o += 2 * W * 4
        vtmp = at("vtmp", o, [P, W]); o += W * 4
        assert o <= end
        rows = at("rows", B0 + RB, [P, 8, D])
        o = A0
        gtmp = at("gtmp", o, [P, 3, 4, W])
        pos = at("pos", o, [P, 2, D])
        lnin = at("lnin", o + 2 * D * 4, [P, 2, D])
        o += max(3 * 4 * W * 4, 4 * D * 4)
        xc = at("xc", o, [P, CR, W]); o += CR * W * 4
        xpad = at("xpad", o, [P, CR, XW + 1]); o += CR * (XW + 1) * 4
        wbd = at("wbd", o, [P, 16, P]); o += 16 * P * 4
        assert o <= B0, (o, B0)
        rowA = at("rowA", B0 + 2 * RB, [P, P])
        rowB = at("rowB", B0 + 2 * RB + P * 4, [P, P])
        y12 = at("y12", base, [P, 2, NT, D])
        fin = at("fin", base + 2 * NT * D * 4, [P, NT, D])
        ln2 = at("ln2", base + 3 * NT * D * 4, [P, 2, D])

        PS = ctx.enter_context(nc.psum_tensor("PS", [P, 8, 512], F32))
        Y_dram = [nc.dram_tensor(f"y_rows{pb}", (YROWS, D), F32, kind="Internal").ap() for pb in range(PASSES)]

        s = {n: sem(n) for n in (
            "const_in rowA_in rowB_in x_in pos_in lnin_in wbd_in smallw_in ln1_in ln2_in rtr_in "
            "cols_ps cols_sb cond_done zeroed ln_xhat xT_ps xT_sb mrow_sb modT_ps mod_sb cm_done h_done "
            "win_ps win_sb conv_done gate_ps gate_act rec_v mult_done q_done tanh_done scan_done gelu_t gelu_th gelu_done yr_done "
            "z_ps z_sb f_ps f_sb yf_ps yf_sb row_ps row_sb mix_ps xn_done xn_pool mixsum x1n x1_done h2_done "
            "h2b1 h2r h2b2 h2b3 h2T_ps h2T_sb lg_ps assign_done rank_ps route_done pos_pool "
            "p1_used unit_used hi_done lo_done sel_ready x_disp xs_hi xs_ready g_done u_done silu_done hid_done hth_done ht_act "
            "ht_ps hts_ready y_sb y_sum y_stored y_zeroed passes_done gathered gathered0 gathered1 gathered2 g2_ps fin_act fin_done out_done var_done root_done state_done st_ps st_row st_out "
            "dve_step act_step pool_step").split()}
        ring_in = [sem(f"ring_in{k}") for k in range(RING)]

        def unit3(buf, n=512):
            return buf[:, :].rearrange("p (k n) -> p k n", n=n)

        def need(eng, name, value):
            if isinstance(value, int) and value <= 0:
                return
            eng.wait_ge(s[name], value)

        def p1_loaded(eng, u):
            slot = (u + 1) % RING
            eng.wait_ge(ring_in[slot], 16 * ((u + 1) // RING + (slot > 0)))

        block = ctx.enter_context(nc.Block())

        ada = t["w_ada"][0].rearrange("(k p) n -> p k n", p=P)
        win = t["w_in"][0].rearrange("(k p) n -> p k n", p=P)
        wout = t["w_out"][0].rearrange("(k p) n -> p k n", p=P)
        ADA = {SH1: 0, SC1: 2, G1: 7, SH2: 9, SC2: 11, G2: 15}
        p1_units = ([(ada, SH1 * D), (ada, SH1 * D + 512), (ada, SC1 * D), (ada, SC1 * D + 512)]
                    + [(win, 0), (win, 1024), (win, 512)]
                    + [(ada, G1 * D), (ada, G1 * D + 512), (ada, SH2 * D), (ada, SH2 * D + 512),
                       (ada, SC2 * D), (ada, SC2 * D + 512)]
                    + [(wout, 0), (wout, 512)] + [(ada, G2 * D), (ada, G2 * D + 512)])
        ADA_GROUPS = [4, 6, 10, 12]
        ADA_UNIT = [0, 1, 2, 3, 7, 8, 9, 10, 11, 12, 15, 16]
        ABANK = [6, 4] * 5 + [6, 6]
        ada_order = [SH1, SC1, G1, SH2, SC2, G2]
        experts = [
            t["ex_w_gate"][0].rearrange("e (k p) n -> p e k n", p=P),
            t["ex_w_up"][0].rearrange("e (k p) n -> p e k n", p=P),
            t["ex_w_down"][0].rearrange("e (k p) n -> p e k n", p=P),
        ]

        def passes(eng, body, after_counts):
            body(0)
            after_counts()
            most = eng.value_load(cnt[0:1, 0:1], min_val=0, max_val=TOK)
            with eng.Fori(1, PASSES) as pb:
                with eng.If(most > pb * CAP):
                    body(pb)

        def tokens_of(eng, e, pb):
            return eng.value_load(cnt[0:1, bass.ds(e + 1, 1)], min_val=0, max_val=TOK) if isinstance(pb, int) and pb == 0 else None

        def fork(eng, n, few, many):
            if n is None:
                many()
                return
            with eng.If(n > HALF):
                many()
            with eng.Else():
                few()

        def pairs(eng, prologue, body, pb):
            ge0 = pb * NE
            prologue(ge0)
            for p in range(2):
                body(ge0 + p, p, pb * (NE // 2), p, False)
            with eng.Fori(1, NE // 2 - 1) as it:
                for p in range(2):
                    body(ge0 + it * 2 + p, it * 2 + p, pb * (NE // 2) + it, p, False)
            for p in range(2):
                body(ge0 + NE - 2 + p, NE - 2 + p, pb * (NE // 2) + NE // 2 - 1, p, p == 1)

        @block.sync
        def _(sp):
            for i in range(NT):
                src = t["x_prompt"][0] if i == 0 else t["x_sample"][0, (i - 1) * P:i * P]
                sp.dma_start(xn[:, i, :], src).then_inc(s["x_in"], 16)
            sp.dma_start(pos[:, :, :], t["pos"].rearrange("(i p) d -> p i d", p=P)).then_inc(s["pos_in"], 16)
            sp.wait_ge(s["const_in"], 16)
            sp.wait_ge(s["rowA_in"], 16 * 7)
            sp.wait_ge(s["rowB_in"], 16 * 5)
            for u, (src, c0) in enumerate(p1_units):
                if u + 1 >= RING + 1:
                    sp.wait_ge(s["p1_used"], u + 1 - RING)
                sp.dma_start(unit3(ring[(u + 1) % RING]), src[:, :, c0:c0 + 512]).then_inc(ring_in[(u + 1) % RING], 16)

            def load(ge, e, p, first):
                for j in range(3):
                    if first:
                        sp.wait_ge(s["p1_used"], NP1 + 1 - RING + 3 * p + j)
                    else:
                        sp.wait_ge(s["unit_used"], ge * 3 + (j - 5))
                    slot = 3 * p + j
                    sp.dma_start(unit3(ring[slot], D if j == 2 else 512),
                                 experts[j][:, e]).then_inc(ring_in[slot], 16)

            for p in range(2):
                load(p, p, p, True)
            with sp.Fori(1, NE // 2) as it:
                for p in range(2):
                    load(it * 2 + p, it * 2 + p, p, False)
            sp.wait_ge(s["route_done"], 1)
            most = sp.value_load(cnt[0:1, 0:1], min_val=0, max_val=TOK)
            with sp.Fori(1, PASSES) as pb:
                with sp.If(most > pb * CAP):
                    with sp.Fori(0, NE // 2) as it:
                        for p in range(2):
                            load(pb * NE + it * 2 + p, it * 2 + p, p, False)
            sp.wait_ge(s["passes_done"], 1)
            for r, n in enumerate(("ln2_g", "ln2_b")):
                sp.dma_start(ln2[:, r, :], t[n].partition_broadcast(P)).then_inc(s["ln2_in"], 16)
            for i in range(NT):
                sp.wait_ge(s["fin_done"], i + 1)
                dst = t["y_prompt"][0] if i == 0 else t["y_sample"][0, (i - 1) * P:i * P]
                sp.dma_start(dst, fin[:, i, :]).then_inc(s["out_done"], 16)
            sp.wait_ge(s["out_done"], 16 * NT)

        @block.scalar
        def _(act):
            n_step = [0]

            def root(n):
                i = n % NT
                act.wait_ge(s["var_done"], n + 1)
                act.activation(stat[:, i, 13:14], stat[:, i, 13:14], ACT.Sqrt).then_inc(s["root_done"], 1)

            def link(ins):
                n_step[0] += 1
                ins.then_inc(s["act_step"], 1)
                act.wait_ge(s["act_step"], n_step[0])

            act.dma_start(cst[:, :], t["const"]).then_inc(s["const_in"], 16)
            for n, r0, k in (("c", A_C, 8), ("c_ctx", A_CTX, 8), ("b_ada", A_BADA, 48), ("ln_in_g", A_LNG, 8),
                             ("ln_in_b", A_LNB, 8), ("conv_w", A_CW, 16), ("conv_b", A_CB, 4)):
                act.dma_start(rowA[r0:r0 + k, :], t[n]).then_inc(s["rowA_in"], 16)
            for n, r0, k in (("rg_ba", B_BA, 8), ("rg_bi", B_BI, 8), ("rg_lam", B_LAM, 8), ("state", B_ST, 8),
                             ("fn_b", B_FB, 4)):
                act.dma_start(rowB[r0:r0 + k, :], t[n]).then_inc(s["rowB_in"], 16)
            for r, n in enumerate(("ln_in_g", "ln_in_b")):
                act.dma_start(lnin[:, r, :], t[n + "_row"].partition_broadcast(P)).then_inc(s["lnin_in"], 16)
            act.wait_ge(s["zeroed"], 1)
            for gi, n in enumerate(("rg_wa", "rg_wi")):
                for h in range(2):
                    act.dma_start(wbd[64 * h:64 * h + 64, 8 * gi:8 * gi + 8, 64 * h:64 * h + 64],
                                  t[n][0].rearrange("d (c q) i j -> q i (d c) j", q=2)[h]).then_inc(s["wbd_in"], 16)
            act.dma_start(fnw[:, :, :], t["fn_w"][0].rearrange("g i j -> i g j")).then_inc(s["smallw_in"], 16)
            act.dma_start(dft[:, :], t["dft"]).then_inc(s["smallw_in"], 16)

            for i in range(NT):
                root(i)
            act.wait_ge(s["cols_sb"], 1)
            for q, c0 in enumerate((A_CTX, A_C)):
                act.activation(cond[:, :, q], cols[:, c0:c0 + KD], ACT.Exp, scale=-1.0).then_inc(s["cond_done"], 1)
            act.activation(spl[:, 0, :], cols[:, NA + B_LAM:NA + B_LAM + 8], ACT.Abs).then_inc(s["act_step"], 1)
            n_step[0] += 1
            act.wait_ge(s["act_step"], n_step[0])
            act.activation(spl[:, 1, :], spl[:, 0, :], ACT.Exp, scale=-1.0).then_inc(s["cond_done"], 1)

            act.wait_ge(s["zeroed"], 3)
            for i in range(NT):
                for hf in range(2):
                    act.wait_ge(s["xT_ps"], 2 * i + hf + 1)
                    act.copy(hT[:, 4 * hf:4 * hf + 4, TC[i]:TC[i] + P],
                             PS[:, 2 * i + hf, :].rearrange("p (k n) -> p k n", n=P)).then_inc(s["xT_sb"], 1)

            def ada_rows(n):
                act.wait_ge(s["p1_used"], ADA_UNIT[n] + 1)
                need(act, "modT_ps", n)
                act.copy(mrow[:, :], PS[:, ABANK[n], :]).then_inc(s["mrow_sb"], 1)

            for n in range(4):
                ada_rows(n)

            for w in range(12):
                if w % 4 == 3:
                    act.wait_ge(s["p1_used"], 5 + w // 4)
                else:
                    act.wait_ge(s["win_ps"], w + 1 - w // 4)
                c = w % 4
                src = PS[:, w % 4, 0:W]
                if w < 4:
                    act.copy(xpad[:, c, 2:2 + W], src).then_inc(s["win_sb"], 1)
                elif w < 8:
                    act.copy(xf[:, c, :], src).then_inc(s["win_sb"], 1)
                else:
                    act.copy(gr[:, c, :], src).then_inc(s["win_sb"], 1)
            for n in range(4, 6):
                ada_rows(n)
            for g in range(FG):
                act.wait_ge(s["z_ps"], g + 1)
                if g >= 2:
                    act.wait_ge(s["f_ps"], g - 1)
                act.copy(Z[:, g % 2, 0:2, :], PS[:, 6, :].rearrange("p (i n) -> p i n", n=256))
                act.copy(Z[:, g % 2, 2, :], PS[:, 5, 0:256]).then_inc(s["z_sb"], 1)

            act.wait_ge(s["gelu_t"], 3)
            act.activation(xpad[:, :, 0:W], xpad[:, :, 0:W], ACT.Tanh, scale=float(np.sqrt(2 / np.pi))).then_inc(s["gelu_th"], 1)

            for it in range(8):
                c, d = it // 2, it % 2
                q = it % 4
                act.wait_ge(s["gate_ps"], it + 1)
                if it == 0:
                    act.wait_ge(s["yf_ps"], FG)
                if it >= 4:
                    act.wait_ge(s["scan_done"], it - 3)
                bk = 2 * (it % 2)
                tr, a_, q_, v_ = rtmp[:, it % 2], gtmp[:, 0, q], gtmp[:, 1, q], gtmp[:, 2, q]
                link(act.activation(tr, PS[:, bk, 0:W], ACT.Tanh, bias=bga[:, 4 * d + c:4 * d + c + 1], scale=0.5))
                act.activation(q_, PS[:, bk + 1, 0:W], ACT.Tanh, bias=bga[:, 8 + 4 * d + c:9 + 4 * d + c], scale=0.5)\
                    .then_inc(s["gate_act"], 1)
                sc = spl[:, 5, 4 * d + c:4 * d + c + 1]
                act.activation(v_, tr, ACT.Tanh, bias=sc, scale=sc).then_inc(s["tanh_done"], 1)
                act.activation(a_, tr, ACT.Exp, bias=sc, scale=sc).then_inc(s["tanh_done"], 1)
                act.wait_ge(s["tanh_done"], 2 * it + 2)
                if 2 <= it < 6:
                    ada_rows(it + 4)
                if q == 3:
                    act.wait_ge(s["rec_v"], it + 1)
                    act.activation(gtmp[:, 2], gtmp[:, 2], ACT.Sqrt).then_inc(s["mult_done"], 1)

            act.wait_ge(s["yr_done"], CR)
            for r in range(6):
                act.wait_ge(s["row_ps"], r + 1)
                act.activation(rows[:, r, :], PS[:, 6:8, :].rearrange("p a n -> p (a n)"), ACT.Identity,
                               bias=1.0 if r in (2, 3) else 0.0).then_inc(s["row_sb"], 1)
                if r == 0:
                    for k, n in enumerate(("ln1_g", "ln1_b")):
                        act.dma_start(rows[:, 6 + k, :], t[n].partition_broadcast(P)).then_inc(s["ln1_in"], 16)

            for n in range(10, 12):
                ada_rows(n)
            root(NT)
            root(NT + 1)
            for i in range(NT):
                if i == 1:
                    root(NT + 2)
                act.wait_ge(s["h2_done"], i + 1)
                act.copy(h2b[:, 0, i, :], tt[:, i % 2, :]).then_inc(s["h2b1"], 1)
                act.wait_ge(s["h2T_ps"], i + 1)
                act.copy(h2T[:, :, i * P:(i + 1) * P], PS[:, 2 * i:2 * i + 2, :].rearrange("p a (k n) -> p (a k) n", n=P))\
                    .then_inc(s["h2T_sb"], 1)
                act.wait_ge(s["h2r"], i + 1)
                act.copy(h2b[:, 1, i, :], tt[:, i % 2, :]).then_inc(s["h2b2"], 1)
            act.wait_ge(s["assign_done"], 1)
            act.activation(rt[:, 6, :, 0:NG], rt[:, 5, :, 0:NG], ACT.Exp).then_inc(s["pos_pool"], 1)
            act.activation(rs[:, 5, :], rs[:, 4, :], ACT.Exp).then_inc(s["pos_pool"], 1)

            halves = [(0, UNIT // 2), (UNIT // 2, UNIT)]

            def split_hi(ge, q, p, j, hs=(0, 1)):
                for h in hs:
                    if h == 0:
                        act.wait_ge(ring_in[3 * p + j], q * 16 + 16 * ((NP1 + 1) // RING + (3 * p + j > 0)))
                        need(act, "unit_used", ge * 3 + (j - 2))
                    a, b = halves[h]
                    act.copy(whi[j][:, a:b], ring[3 * p + j][:, a:b]).then_inc(s["hi_done"], 1)

            def x_hi(ge, n):
                def copy(dst, src):
                    act.wait_ge(s["x_disp"], ge + 1)
                    need(act, "unit_used", ge * 3 - 1)
                    act.copy(dst, src).then_inc(s["xs_hi"], 1)

                fork(act, n,
                     lambda: copy(xsH[:, :, 0:HALF], PS[:, 0, :].rearrange("p (k n) -> p k n", n=HALF)),
                     lambda: copy(xsH[:, :, :], PS[:, 0:2, :].rearrange("p a (k n) -> p (a k) n", n=CAP)))

            def prologue(ge, pb):
                q = ge // 2
                if isinstance(ge, int):
                    act.wait_ge(s["h2_done"], NT)
                    act.wait_ge(s["route_done"], 1)
                n = tokens_of(act, 0, pb)
                split_hi(ge, q, 0, 0)
                x_hi(ge, n)
                split_hi(ge, q, 0, 1)
                split_hi(ge, q, 0, 2)

            def body(ge, e, q, p, last, pb):
                q1 = q + p
                n = tokens_of(act, e, pb)
                n1 = None if last else tokens_of(act, e + 1, pb)

                def gate_few():
                    act.wait_ge(s["unit_used"], ge * 3 + 1)
                    need(act, "ht_ps", ge)
                    act.copy(sg[:, :], PS[:, 2, :]).then_inc(s["g_done"], 1)

                def gate_many():
                    act.wait_ge(s["unit_used"], ge * 3 + 1)
                    need(act, "ht_ps", ge)
                    act.activation(sg[:, :], PS[:, 2, :], ACT.Tanh, scale=0.5).then_inc(s["g_done"], 1)

                def hidden_few():
                    act.wait_ge(s["ht_ps"], ge + 1)
                    need(act, "unit_used", ge * 3)
                    act.activation(sgT[:, :, :], PS[:, 4, 0:KF * HALF].rearrange("p (k n) -> p k n", n=HALF), ACT.Tanh,
                                   scale=0.5).then_inc(s["ht_act"], 1)

                def hidden_many():
                    act.wait_ge(s["ht_ps"], ge + 1)
                    need(act, "unit_used", ge * 3)
                    act.copy(hTH[:, :, :], PS[:, 4, :].rearrange("p (k n) -> p k n", n=CAP)).then_inc(s["ht_act"], 1)

                def rows_few():
                    act.wait_ge(s["unit_used"], ge * 3 + 3)
                    need(act, "y_stored", ge * 16)
                    act.copy(ylow[:, :], PS[HALF:CAP, 5:7, :].rearrange("p a n -> p (a n)"))
                    act.copy(ysb[0:HALF, :], PS[0:HALF, 5:7, :].rearrange("p a n -> p (a n)")).then_inc(s["y_sb"], 1)

                def rows_many():
                    act.wait_ge(s["unit_used"], ge * 3 + 3)
                    need(act, "y_stored", ge * 16)
                    act.copy(ysb[:, :], PS[:, 5:7, :].rearrange("p a n -> p (a n)")).then_inc(s["y_sb"], 1)

                fork(act, n, gate_few, gate_many)
                if not last:
                    split_hi(ge + 1, q1, 1 - p, 0)
                fork(act, n, hidden_few, hidden_many)
                if not last:
                    split_hi(ge + 1, q1, 1 - p, 1, (0,))
                    x_hi(ge + 1, n1)
                    split_hi(ge + 1, q1, 1 - p, 1, (1,))
                    split_hi(ge + 1, q1, 1 - p, 2)
                fork(act, n, rows_few, rows_many)

            passes(act, lambda pb: pairs(act, lambda ge: prologue(ge, pb), lambda *a: body(*a, pb), pb), lambda: None)
            for i in range(NT):
                root(2 * NT + i)

        @block.vector
        def _(dve):
            n_step = [0]
            n_norm = [0]

            def step(ins):
                n_step[0] += 1
                ins.then_inc(s["dve_step"], 1)

            def link(ins):
                step(ins)
                dve.wait_ge(s["dve_step"], n_step[0])

            def norm_stats(x, i, st):
                step(dve.bn_stats(st[:, 0:6], x[:, 0:512]))
                link(dve.bn_stats(st[:, 6:12], x[:, 512:1024]))
                link(dve.bn_aggr(st[:, 12:14], st[:, 0:12].rearrange("p (a b) -> p a b", b=6)))
                dve.tensor_scalar(st[:, 13:14], st[:, 13:14], LN_EPS, None, ALU.add).then_inc(s["var_done"], 1)
                n_norm[0] += 1
                dve.wait_ge(s["root_done"], n_norm[0])
                link(dve.reciprocal(st[:, 13:14], st[:, 13:14]))

            for i in range(NT):
                dve.wait_ge(s["x_in"], 16 * NT)
                if i > 0:
                    dve.wait_ge(s["xn_pool"], i)
                norm_stats(xn[:, i, :], i, stat[:, i, :])
                dve.tensor_scalar(xn[:, i, :], xn[:, i, :], stat[:, i, 12:13], stat[:, i, 13:14],
                                  ALU.subtract, ALU.mult).then_inc(s["ln_xhat"], 1)

            dve.wait_ge(s["cols_ps"], 1)
            dve.tensor_copy(cols[:, :], PS[:, 0, 0:NA + NB]).then_inc(s["cols_sb"], 1)
            dve.wait_ge(s["cols_sb"], 1)
            dve.wait_ge(s["cond_done"], 3)
            link(dve.tensor_scalar(cond[:, :, :], cond[:, :, :], 1.0, None, ALU.add))
            link(dve.reciprocal(cond[:, :, :], cond[:, :, :]))
            for q, c0 in enumerate((A_CTX, A_C)):
                dve.tensor_tensor(cond[:, :, q], cond[:, :, q], cols[:, c0:c0 + KD], ALU.mult).then_inc(s["cond_done"], 1)
            dve.wait_ge(s["zeroed"], 3)
            dve.wait_ge(s["cond_done"], 5)
            dve.tensor_copy(cond32[:, :, 0:2], cond[:, :, :]).then_inc(s["cond_done"], 1)
            dve.tensor_scalar(bga[:, :], cols[:, NA + B_BA:NA + B_BA + 16], 0.5, None, ALU.mult).then_inc(s["cond_done"], 1)
            z, w, w2, acc = spl[:, 1, :], spl[:, 2, :], spl[:, 3, :], spl[:, 4, :]
            link(dve.tensor_scalar(w, z, 2.0, None, ALU.add))
            link(dve.reciprocal(w, w))
            link(dve.tensor_tensor(w, w, z, ALU.mult))
            link(dve.tensor_tensor(w2, w, w, ALU.mult))
            link(dve.tensor_scalar(acc, w2, 1.0 / 17, 1.0 / 15, ALU.mult, ALU.add))
            for n in (13, 11, 9, 7, 5, 3, 1):
                link(dve.tensor_tensor(acc, acc, w2, ALU.mult))
                link(dve.tensor_scalar(acc, acc, 1.0 / n, None, ALU.add))
            link(dve.tensor_tensor(acc, acc, w, ALU.mult))
            link(dve.tensor_scalar(w, cols[:, NA + B_LAM:NA + B_LAM + 8], -1.0, 0.0, ALU.mult, ALU.max))
            link(dve.scalar_tensor_tensor(out=acc, in0=acc, scalar=2.0, in1=w, op0=ALU.mult, op1=ALU.add))
            dve.tensor_scalar(spl[:, 5, :], acc, -4.0, None, ALU.mult).then_inc(s["cond_done"], 1)

            def mod_out(n):
                c0 = ada_order[n // 2] * KD + 4 * (n % 2)
                dve.wait_ge(s["modT_ps"], next(g for g in ADA_GROUPS if g > n))
                dve.tensor_tensor(modT[:, c0:c0 + 4, :], PS[:, 7, 2 * c0:2 * c0 + 8].rearrange("p (n s) -> p n s", s=2),
                                  cols[:, A_BADA + c0:A_BADA + c0 + 4].unsqueeze(2).broadcast_to([P, 4, 2]),
                                  ALU.add).then_inc(s["mod_sb"], 1)

            for n in range(4):
                mod_out(n)
            dve.wait_ge(s["mod_sb"], 4)
            sc1 = cmod[:, 0]
            sh1 = cmod[:, 1]
            gcol = cols[:, A_LNG:A_LNG + KD].unsqueeze(2).broadcast_to([P, KD, 2])
            bcol = cols[:, A_LNB:A_LNB + KD].unsqueeze(2).broadcast_to([P, KD, 2])
            link(dve.tensor_scalar(sc1, modT[:, SC1 * KD:SC1 * KD + KD, :], 1.0, None, ALU.add))
            link(dve.tensor_tensor(sh1, sc1, bcol, ALU.mult))
            link(dve.tensor_tensor(sh1, sh1, modT[:, SH1 * KD:SH1 * KD + KD, :], ALU.add))
            link(dve.tensor_tensor(sc1, sc1, gcol, ALU.mult))
            dve.wait_ge(s["xT_sb"], 6)
            for k in range(KD):
                for q, (c0, n) in enumerate(SEG):
                    last = dve.tensor_scalar(hT[:, k, c0:c0 + n], hT[:, k, c0:c0 + n], cmod[:, 0, k, q:q + 1],
                                             cmod[:, 1, k, q:q + 1], ALU.mult, ALU.add)
                last.then_inc(s["h_done"], 1)

            dve.wait_ge(s["zeroed"], 3)
            for c in range(CR):
                dve.wait_ge(s["win_sb"], c + 1)
                for k in range(4):
                    cw = cols[:, A_CW + 4 * k + c:A_CW + 4 * k + c + 1]
                    if k == 0:
                        link(dve.tensor_scalar(xc[:, c, :], xpad[:, c, 0:W], cw, cols[:, A_CB + c:A_CB + c + 1],
                                               ALU.mult, ALU.add))
                    elif k < 3:
                        link(dve.scalar_tensor_tensor(out=xc[:, c, :], in0=xpad[:, c, k:k + W], scalar=cw,
                                                      in1=xc[:, c, :], op0=ALU.mult, op1=ALU.add))
                    else:
                        dve.scalar_tensor_tensor(out=xc[:, c, :], in0=xpad[:, c, k:k + W], scalar=cw,
                                                 in1=xc[:, c, :], op0=ALU.mult, op1=ALU.add).then_inc(s["conv_done"], 1)
            for g in range(FG):
                dve.wait_ge(s["f_ps"], g + 1)
                if g >= 2:
                    dve.wait_ge(s["yf_ps"], g - 1)
                dve.tensor_copy(FTs[:, g % 2, :], PS[:, 4, 0:TOK]).then_inc(s["f_sb"], 1)
                dve.wait_ge(s["yf_ps"], g + 1)
                dve.wait_ge(s["p1_used"], 7)
                dve.tensor_scalar(mixT[:, CR + g, :], PS[:, 5, 0:TOK], cols[:, NA + B_FB + g:NA + B_FB + g + 1], None,
                                  ALU.add).then_inc(s["yf_sb"], 1)
            for n in range(4, 6):
                mod_out(n)

            for b in range(2):
                for it in range(4 * b, 4 * b + 4):
                    v_, t_ = gtmp[:, 2, it % 4], vtmp[:, :]
                    dve.wait_ge(s["tanh_done"], 2 * it + 1)
                    link(dve.tensor_scalar(t_, v_, -1.0, 1.0, ALU.mult, ALU.add))
                    link(dve.reciprocal(t_, t_))
                    link(dve.scalar_tensor_tensor(out=v_, in0=v_, scalar=-2.0, in1=t_, op0=ALU.mult, op1=ALU.mult))
                    dve.tensor_scalar(v_, v_, 0.0, None, ALU.max).then_inc(s["rec_v"], 1)
                if b == 1:
                    for n in range(6, 10):
                        mod_out(n)
                dve.wait_ge(s["mult_done"], b + 1)
                dve.wait_ge(s["q_done"], 4 * b + 4)
                dve.wait_ge(s["tanh_done"], 8 * b + 8)
                link(dve.scalar_tensor_tensor(out=gtmp[:, 1], in0=gtmp[:, 2], scalar=0.5, in1=gtmp[:, 1],
                                              op0=ALU.mult, op1=ALU.mult))
                for it in range(4 * b, 4 * b + 4):
                    c, d = it // 2, it % 2
                    for n, (c0, m) in enumerate(SEG):
                        st = cols[:, NA + B_ST + 4 * d + c:NA + B_ST + 4 * d + c + 1] if n else 0.0
                        a_, b_, h_ = (v[:, c0:c0 + m] for v in (gtmp[:, 0, it % 4], gtmp[:, 1, it % 4], hfb[:, d]))
                        if d:
                            a_, b_, h_ = a_[:, ::-1], b_[:, ::-1], h_[:, ::-1]
                        sc_ = dve.tensor_tensor_scan(h_, a_, b_, st, ALU.mult, ALU.add)
                        if n == 0:
                            step(sc_)
                    sc_.then_inc(s["scan_done"], 1)
                    dve.wait_ge(s["scan_done"], it + 1)
                    dve.wait_ge(s["dve_step"], n_step[0])
                    edge = 0 if d else SEQ - 1
                    dve.tensor_copy(stin[:, 4 * d + c:4 * d + c + 1], hfb[:, d, edge:edge + 1]).then_inc(s["state_done"], 1)
                    dve.wait_ge(s["state_done"], it + 1)
                    if d:
                        dve.wait_ge(s["gelu_done"], 1)
                        for c0, m in SEG:
                            link(dve.tensor_tensor(hfb[:, 1, c0:c0 + m], hfb[:, 0, c0:c0 + m], hfb[:, 1, c0:c0 + m],
                                                   ALU.add))
                        for (c0, m), (k0, _) in zip(SEG, SEGC):
                            step(dve.scalar_tensor_tensor(out=mixT[:, c, k0:k0 + m], in0=hfb[:, 1, c0:c0 + m],
                                                          scalar=0.5, in1=gr[:, c, c0:c0 + m], op0=ALU.mult, op1=ALU.mult))
                        dve.wait_ge(s["dve_step"], n_step[0])
                        dve.nop().then_inc(s["yr_done"], 1)

            dve.wait_ge(s["row_sb"], 6)
            dve.wait_ge(s["xn_done"], NT)
            dve.wait_ge(s["ln1_in"], 32)

            def low_parts(i):
                dve.wait_ge(s["h2b1"], i + 1)
                dve.wait_ge(s["h2T_ps"], i + 1)
                dve.tensor_tensor(tt[:, i % 2, :], tt[:, i % 2, :], h2b[:, 0, i, :], ALU.subtract).then_inc(s["h2r"], 1)
                dve.wait_ge(s["h2b2"], i + 1)
                dve.wait_ge(s["h2r"], i + 1)
                dve.tensor_tensor(h2b[:, 2, i, :], tt[:, i % 2, :], h2b[:, 1, i, :], ALU.subtract).then_inc(s["h2b3"], 1)

            for i in range(NT):
                if i < NT - 1:
                    dve.wait_ge(s["mix_ps"], i + 1)
                else:
                    dve.wait_ge(s["p1_used"], 15)
                if i >= 2:
                    low_parts(i - 2)
                    dve.wait_ge(s["h2b3"], i - 1)
                m = tt[:, i % 2, :]
                link(dve.tensor_tensor(m, PS[:, 2 * i:2 * i + 2, :].rearrange("p a n -> p (a n)"),
                                       rows[:, 1 if i else 0, :], ALU.mult))
                link(dve.scalar_tensor_tensor(out=m, in0=xn[:, i, :], scalar=ALPHA, in1=m, op0=ALU.mult, op1=ALU.add))
                norm_stats(m, i, stat[:, i, :])
                dve.tensor_scalar(m, m, stat[:, i, 12:13], stat[:, i, 13:14], ALU.subtract, ALU.mult)\
                    .then_inc(s["x1n"], 1)
            low_parts(1)
            low_parts(2)
            for n in range(10, 12):
                mod_out(n)

            dve.wait_ge(s["lg_ps"], 1)
            dve.wait_ge(s["rtr_in"], 64)
            link(dve.tensor_tensor(lg[:, :, :], PS[:, 0, 0:NT * 20].rearrange("p (i n) -> p i n", n=20),
                                   rb[:, :].unsqueeze(1).broadcast_to([P, NT, 20]), ALU.add))
            gl, el = lg[:, :, 0:NG], lg[:, :, NG:]

            def wide(v, n):
                return v.unsqueeze(2).broadcast_to([P, NT, n])

            def first_max(x, n, code, oh, mx, tmp):
                link(dve.tensor_reduce(mx, x, AX.X, ALU.max))
                link(dve.tensor_tensor(tmp, x, wide(mx, n), ALU.is_equal))
                cd = cst[:, code:code + n].unsqueeze(1).broadcast_to([P, NT, n])
                link(dve.tensor_tensor(tmp, tmp, cd, ALU.mult))
                link(dve.tensor_reduce(rs[:, 11, :], tmp, AX.X, ALU.max))
                link(dve.tensor_tensor(oh, cd, wide(rs[:, 11, :], n), ALU.is_equal))

            dve.wait_ge(s["st_ps"], 1)
            dve.tensor_copy(strow[0:8, :], PS[0:8, 2, 128:256]).then_inc(s["st_row"], 1)

            og, oh1, oh2, asg = rt[:, 0, :, 0:NG], rt[:, 1], rt[:, 2], rt[:, 3]
            first_max(gl, NG, C_COD4, og, rs[:, 0, :], rt[:, 4, :, 0:NG])
            link(dve.tensor_tensor(rt[:, 5, :, 0:NG], gl, wide(rs[:, 0, :], NG), ALU.subtract))
            marks = og.unsqueeze(3).broadcast_to([P, NT, NG, EPG])
            m4 = rt[:, 4].rearrange("p i (g e) -> p i g e", e=EPG)
            link(dve.tensor_copy(m4, marks))
            link(dve.tensor_tensor(rt[:, 7], el, rt[:, 4], ALU.mult))
            link(dve.tensor_scalar(rt[:, 4], rt[:, 4], -1.0, 1e30, ALU.add, ALU.mult))
            link(dve.tensor_tensor(rt[:, 7], rt[:, 7], rt[:, 4], ALU.add))
            first_max(rt[:, 7], NE, C_COD16, oh1, rs[:, 1, :], rt[:, 4])
            link(dve.scalar_tensor_tensor(out=rt[:, 7], in0=oh1, scalar=-2e30, in1=rt[:, 7], op0=ALU.mult, op1=ALU.add))
            first_max(rt[:, 7], NE, C_COD16, oh2, rs[:, 2, :], rt[:, 4])
            link(dve.tensor_tensor(asg, oh1, oh2, ALU.add))
            dve.tensor_tensor(rs[:, 4, :], rs[:, 2, :], rs[:, 1, :], ALU.subtract).then_inc(s["assign_done"], 1)
            dve.wait_ge(s["pos_pool"], 2)
            link(dve.tensor_reduce(rs[:, 6, :], rt[:, 6, :, 0:NG], AX.X, ALU.add))
            link(dve.tensor_scalar(rs[:, 7, :], rs[:, 5, :], 1.0, None, ALU.add))
            link(dve.tensor_tensor(rs[:, 6, :], rs[:, 6, :], rs[:, 7, :], ALU.mult))
            link(dve.reciprocal(wk[:, 0, :], rs[:, 6, :]))
            link(dve.tensor_tensor(wk[:, 1, :], wk[:, 0, :], rs[:, 5, :], ALU.mult))
            dve.wait_ge(s["rank_ps"], 1)
            rank = PS[:, 1, 0:NT * NE].rearrange("p (i e) -> p i e", e=NE)
            link(dve.scalar_tensor_tensor(out=rt[:, 4], in0=rank, scalar=1.0, in1=asg, op0=ALU.add, op1=ALU.mult))
            link(dve.tensor_scalar(rankA[:, 0:NE, :].rearrange("p e i -> p i e"), rt[:, 4], -1.0, None, ALU.add))
            link(dve.tensor_reduce(small[:, 0:1], PS[:, 1, NT * NE:(NT + 1) * NE], AX.X, ALU.max))
            link(dve.tensor_copy(cnt[:, 1:1 + NE], PS[:, 1, NT * NE:(NT + 1) * NE]))
            dve.tensor_copy(cnt[:, 0:1], small[:, 0:1]).then_inc(s["route_done"], 1)
            erow = cst[:, C_EROW:C_EROW + NE].unsqueeze(1).broadcast_to([P, NT, NE])
            for q, oh in enumerate((oh1, oh2)):
                for k, v in enumerate((rank, erow)):
                    link(dve.tensor_tensor(rt[:, 4], v, oh, ALU.mult))
                    link(dve.tensor_reduce(posf[:, k, q, :], rt[:, 4], AX.X, ALU.add))
            for pb in range(PASSES):
                r, b = posf[:, 0], posf[:, 2]
                if pb:
                    link(dve.tensor_scalar(r, r, float(-CAP), None, ALU.add))
                link(dve.tensor_scalar(b, r, 0.0, FAR, ALU.is_lt, ALU.mult))
                link(dve.tensor_tensor(b, b, r, ALU.add))
                link(dve.tensor_tensor(b, b, posf[:, 1], ALU.add))
                link(dve.tensor_copy(posn[:, pb], b))
                link(dve.tensor_scalar(b, r, CAP - 0.5, FAR, ALU.is_gt, ALU.mult))
                link(dve.tensor_tensor(b, b, posn[:, pb], ALU.add))
                link(dve.tensor_copy(posn[:, pb], b))
            dve.nop().then_inc(s["route_done"], 1)

            def split_lo(ge, p, j, hs=(0, 1)):
                for h in hs:
                    a, b = h * UNIT // 2, (h + 1) * UNIT // 2
                    dve.wait_ge(s["hi_done"], ge * 6 + (2 * j + h + 1))
                    dve.tensor_tensor(wlo[3 * p + j][:, a:b], ring[3 * p + j][:, a:b], whi[j][:, a:b].bitcast(F32),
                                      ALU.subtract).then_inc(s["lo_done"], 1)

            def x_lo(ge, n):
                def rest(dst, src, high):
                    dve.wait_ge(s["xs_hi"], ge + 1)
                    need(dve, "unit_used", ge * 3 - 1)
                    dve.tensor_tensor(dst, src, high.bitcast(F32), ALU.subtract).then_inc(s["xs_ready"], 1)

                fork(dve, n,
                     lambda: rest(xsH[:, :, HALF:CAP], PS[:, 0, :].rearrange("p (k n) -> p k n", n=HALF),
                                  xsH[:, :, 0:HALF]),
                     lambda: rest(xsL[:, :, :], PS[:, 0:2, :].rearrange("p a (k n) -> p (a k) n", n=CAP),
                                  xsH[:, :, :]))

            def choose(ge, e, pb):
                need(dve, "x_disp", ge)
                i0 = cst[:, bass.ds(pb * CAP + C_IOTA, CAP)] if not isinstance(pb, int) else \
                    cst[:, C_IOTA + pb * CAP:C_IOTA + (pb + 1) * CAP]
                ra = rankA[:, bass.ds(e, 1), :].rearrange("p a i -> p (a i)") if not isinstance(e, int) else rankA[:, e, :]
                dve.tensor_tensor(sel[:, :, :], i0.unsqueeze(1).broadcast_to([P, NT, CAP]),
                                   ra.unsqueeze(2).broadcast_to([P, NT, CAP]), ALU.is_equal).then_inc(s["sel_ready"], 1)

            def prologue(ge, pb):
                if isinstance(ge, int):
                    dve.wait_ge(s["route_done"], 2)
                n = tokens_of(dve, 0, pb)
                choose(ge, 0, pb)
                split_lo(ge, 0, 0)
                x_lo(ge, n)
                split_lo(ge, 0, 1)
                split_lo(ge, 0, 2)

            def body(ge, e, q, p, last, pb):
                n = tokens_of(dve, e, pb)
                n1 = None if last else tokens_of(dve, e + 1, pb)

                def up_few():
                    dve.wait_ge(s["unit_used"], ge * 3 + 2)
                    need(dve, "ht_ps", ge)
                    dve.tensor_copy(hid[:, :], PS[:, 3, :]).then_inc(s["u_done"], 1)

                def up_many():
                    dve.wait_ge(s["unit_used"], ge * 3 + 2)
                    dve.wait_ge(s["g_done"], ge + 1)
                    need(dve, "ht_ps", ge)
                    dve.scalar_tensor_tensor(out=hid[:, :], in0=sg[:, :], scalar=1.0, in1=PS[:, 2, :], op0=ALU.add,
                                             op1=ALU.mult).then_inc(s["silu_done"], 1)
                    dve.wait_ge(s["silu_done"], ge + 1)
                    dve.scalar_tensor_tensor(out=hid[:, :], in0=hid[:, :], scalar=0.5, in1=PS[:, 3, :], op0=ALU.mult,
                                             op1=ALU.mult).then_inc(s["u_done"], 1)

                def hidden_few():
                    dve.wait_ge(s["ht_act"], ge + 1)
                    dve.scalar_tensor_tensor(out=hidT[:, :, :], in0=sgT[:, :, :], scalar=1.0,
                                             in1=PS[:, 4, 0:KF * HALF].rearrange("p (k n) -> p k n", n=HALF),
                                             op0=ALU.add, op1=ALU.mult).then_inc(s["silu_done"], 1)
                    dve.wait_ge(s["silu_done"], ge + 1)
                    dve.scalar_tensor_tensor(out=hidT[:, :, :], in0=hidT[:, :, :], scalar=0.5,
                                             in1=PS[:, 7, 0:KF * HALF].rearrange("p (k n) -> p k n", n=HALF),
                                             op0=ALU.mult, op1=ALU.mult).then_inc(s["hid_done"], 1)
                    dve.wait_ge(s["hid_done"], ge + 1)
                    dve.tensor_copy(hTH[:, :, 0:HALF], hidT[:, :, :]).then_inc(s["hth_done"], 1)
                    dve.wait_ge(s["hth_done"], ge + 1)
                    dve.tensor_tensor(hTH[:, :, HALF:CAP], hidT[:, :, :], hTH[:, :, 0:HALF].bitcast(F32), ALU.subtract)\
                        .then_inc(s["hts_ready"], 1)

                def hidden_many():
                    dve.nop().then_inc(s["hid_done"], 1)
                    dve.nop().then_inc(s["hth_done"], 1)
                    dve.wait_ge(s["ht_act"], ge + 1)
                    dve.tensor_tensor(hTL[:, :, :], PS[:, 4, :].rearrange("p (k n) -> p k n", n=CAP),
                                      hTH[:, :, :].bitcast(F32), ALU.subtract).then_inc(s["hts_ready"], 1)

                if not last:
                    choose(ge + 1, e + 1, pb)
                fork(dve, n, up_few, up_many)
                if not last:
                    split_lo(ge + 1, 1 - p, 0, (0,))
                fork(dve, n, hidden_few, hidden_many)
                if not last:
                    split_lo(ge + 1, 1 - p, 0, (1,))
                    x_lo(ge + 1, n1)
                    split_lo(ge + 1, 1 - p, 1)
                    split_lo(ge + 1, 1 - p, 2)

            passes(dve, lambda pb: pairs(dve, lambda ge: prologue(ge, pb), lambda *a: body(*a, pb), pb), lambda: None)

            dve.wait_ge(s["g2_ps"], 1)
            dve.wait_ge(s["ln2_in"], 32)
            for i in range(NT):
                dve.wait_ge(s["gathered"], 1)
                m = fin[:, i, :]
                link(dve.tensor_scalar(m, y12[:, 0, i, :], wk[:, 0, i:i + 1], None, ALU.mult))
                link(dve.scalar_tensor_tensor(out=m, in0=y12[:, 1, i, :], scalar=wk[:, 1, i:i + 1], in1=m,
                                              op0=ALU.mult, op1=ALU.add))
                b = 2 if i else 0
                link(dve.tensor_tensor(m, m, PS[:, b:b + 2, :].rearrange("p a n -> p (a n)"), ALU.mult))
                link(dve.scalar_tensor_tensor(out=m, in0=xn[:, i, :], scalar=ALPHA, in1=m, op0=ALU.mult, op1=ALU.add))
                norm_stats(m, i, stat[:, i, :])
                link(dve.tensor_scalar(m, m, stat[:, i, 12:13], stat[:, i, 13:14], ALU.subtract, ALU.mult))
                link(dve.tensor_tensor(m, m, ln2[:, 0, :], ALU.mult))
                dve.tensor_tensor(m, m, ln2[:, 1, :], ALU.add).then_inc(s["fin_done"], 1)

        @block.gpsimd
        def _(pool):
            n_step = [0]

            def link(ins):
                n_step[0] += 1
                ins.then_inc(s["pool_step"], 1)
                pool.wait_ge(s["pool_step"], n_step[0])

            pool.memset(wbd[:, :, :], 0.0).then_inc(s["zeroed"], 1)
            pool.memset(cond32[:, :, :], 0.0).then_inc(s["zeroed"], 1)
            pool.memset(ylow[:, :], 0.0)
            pool.memset(rankA[:, NE:NE + 1, :], -1.0)
            pool.memset(xpad[:, :, 0:2], 0.0)
            pool.memset(xpad[:, :, 2 + W:XW], 0.0)
            pool.memset(hT[:, :, SEQ:SEQ + 3], 0.0)
            pool.memset(hT[:, :, W - 1:W], 0.0).then_inc(s["zeroed"], 1)
            pool.wait_ge(s["x_in"], 16 * NT)
            pool.wait_ge(s["pos_in"], 16)
            for i in range(1, NT):
                pool.tensor_tensor(xn[:, i, :], xn[:, i, :], pos[:, i - 1, :], ALU.add).then_inc(s["xn_pool"], 1)
            pool.wait_ge(s["lnin_in"], 32)
            pool.wait_ge(s["xT_ps"], 6)
            for i in range(NT):
                link(pool.tensor_tensor(xn[:, i, :], xn[:, i, :], lnin[:, 0, :], ALU.mult))
                pool.tensor_tensor(xn[:, i, :], xn[:, i, :], lnin[:, 1, :], ALU.add).then_inc(s["xn_done"], 1)

            pool.wait_ge(s["p1_used"], 5)
            pool.dma_start(Y_dram[0].rearrange("(e r) d -> r e d", r=CAP)[HALF:CAP],
                           ylow[:, :].unsqueeze(1).broadcast_to([HALF, NE, D])).then_inc(s["y_zeroed"], 16)
            pool.wait_ge(s["y_zeroed"], 16)
            pool.dma_start(wr[:, :, 0:NG], t["router_g_w"][0].rearrange("(k p) n -> p k n", p=P)).then_inc(s["rtr_in"], 16)
            pool.dma_start(wr[:, :, NG:], t["router_e_w"][0].rearrange("(k p) n -> p k n", p=P)).then_inc(s["rtr_in"], 16)
            pool.dma_start(rb[:, 0:NG], t["router_g_b"].partition_broadcast(P)).then_inc(s["rtr_in"], 16)
            pool.dma_start(rb[:, NG:], t["router_e_b"].partition_broadcast(P)).then_inc(s["rtr_in"], 16)

            def q_item(it):
                pool.wait_ge(s["gate_act"], it + 1)
                g = gtmp[:, 1, it % 4]
                link(pool.tensor_scalar(g, g, 1.0, None, ALU.add))
                pool.tensor_tensor(g, g, xc[:, it // 2, :], ALU.mult).then_inc(s["q_done"], 1)

            pool.wait_ge(s["win_sb"], 12)
            pool.wait_ge(s["conv_done"], CR)
            tg = xpad[:, :, 0:W]
            pool.tensor_tensor(tg, gr[:, :, :], gr[:, :, :], ALU.mult).then_inc(s["gelu_t"], 1)
            pool.wait_ge(s["gelu_t"], 1)
            pool.tensor_scalar(tg, tg, 0.044715, 1.0, ALU.mult, ALU.add).then_inc(s["gelu_t"], 1)
            pool.wait_ge(s["gelu_t"], 2)
            pool.tensor_tensor(tg, tg, gr[:, :, :], ALU.mult).then_inc(s["gelu_t"], 1)
            pool.wait_ge(s["gelu_th"], 1)
            link(pool.tensor_scalar(tg, tg, 1.0, None, ALU.add))
            pool.tensor_tensor(gr[:, :, :], gr[:, :, :], tg, ALU.mult).then_inc(s["gelu_done"], 1)
            for it in range(8):
                q_item(it)

            for i in range(NT):
                q = 1 if i else 0
                m = tt[:, i % 2, :]
                pool.wait_ge(s["x1n"], i + 1)
                link(pool.tensor_tensor(m, m, rows[:, 6, :], ALU.mult))
                link(pool.tensor_tensor(xn[:, i, :], m, rows[:, 7, :], ALU.add))
                link(pool.tensor_tensor(m, xn[:, i, :], rows[:, 2 + q, :], ALU.mult))
                pool.tensor_tensor(m, m, rows[:, 4 + q, :], ALU.add).then_inc(s["h2_done"], 1)

            pool.wait_ge(s["st_row"], 1)
            pool.dma_start(t["new_state"], strow[0:2 * CR, :]).then_inc(s["st_out"], 16)
            pool.wait_ge(s["st_out"], 16)

            pool.wait_ge(s["route_done"], 2)

            def run(pb):
                def body(ge, e, q, p, last):
                    n = tokens_of(pool, e, pb)

                    def few():
                        pool.wait_ge(s["y_sb"], ge + 1)
                        pool.tensor_tensor(ysb[0:HALF, :], ysb[0:HALF, :], ylow[:, :], ALU.add).then_inc(s["y_sum"], 1)
                        pool.wait_ge(s["y_sum"], ge + 1)
                        pool.dma_start(Y_dram[pb][bass.ds(e * CAP, HALF)], ysb[0:HALF, :]).then_inc(s["y_stored"], 16)

                    def many():
                        pool.nop().then_inc(s["y_sum"], 1)
                        pool.wait_ge(s["y_sb"], ge + 1)
                        pool.dma_start(Y_dram[pb][bass.ds(e * CAP, CAP)], ysb[:, :]).then_inc(s["y_stored"], 16)

                    fork(pool, n, few, many)

                pairs(pool, lambda ge: None, body, pb)
                pool.wait_ge(s["y_stored"], pb * (16 * NE) + 16 * NE)

            run(0)
            most = pool.value_load(cnt[0:1, 0:1], min_val=0, max_val=TOK)
            for pb in range(1, PASSES):
                with pool.If(most > pb * CAP):
                    run(pb)
            pool.nop().then_inc(s["passes_done"], 1)

            def gather(pb, name):
                for i in range(NT):
                    for q in range(2):
                        pool.indirect_dma_start(
                            out=y12[:, q, i, :], out_offset=None, in_=Y_dram[pb],
                            in_offset=bass.IndirectOffsetOnAxis(ap=posn[:, pb, q, i:i + 1], axis=0),
                            bounds_check=YROWS - 1, oob_is_err=False,
                        ).then_inc(s[name], 16)
                pool.wait_ge(s[name], 16 * 2 * NT)

            gather(0, "gathered0")
            for pb in range(1, PASSES):
                with pool.If(most > pb * CAP):
                    gather(pb, f"gathered{pb}")
            pool.nop().then_inc(s["gathered"], 1)

        @block.tensor
        def _(pe):
            ident = cst[:, C_ID:C_ID + P]
            ones = cst[:, C_ONE:C_ONE + P]

            pe.wait_ge(s["const_in"], 16)
            pe.wait_ge(s["rowA_in"], 16 * 7)
            pe.transpose(PS[:, 0, 0:NA], rowA[0:NA, :], cst[0:NA, C_ID:C_ID + NA])
            pe.wait_ge(s["rowB_in"], 16 * 5)
            pe.transpose(PS[:, 0, NA:NA + NB], rowB[0:NB, :], cst[0:NB, C_ID:C_ID + NB]).then_inc(s["cols_ps"], 1)

            def ada_sums(n, u):
                p1_loaded(pe, u)
                w = unit3(ring[(u + 1) % RING])
                if n == 1:
                    pe.wait_ge(s["xT_sb"], 6)
                elif n >= 2:
                    pe.wait_ge(s["mrow_sb"], n - 1 if n < 10 else n)
                for k in range(KD):
                    j = k % 4
                    mm = pe.matmul(PS[32 * j:32 * j + 32, ABANK[n], :], cond32[:, k, :], w[:, k, :],
                                   start=(k < 4), stop=(k >= 4))
                mm.then_inc(s["p1_used"], 1)

            def ada_cols(n):
                c0 = ada_order[n // 2] * KD + 4 * (n % 2)
                if n in ADA_GROUPS:
                    pe.wait_ge(s["mod_sb"], n)
                pe.wait_ge(s["mrow_sb"], n + 1)
                for q in range(4):
                    mm = pe.matmul(PS[:, 7, 2 * (c0 + q):2 * (c0 + q) + 2], mrow[:, q * P:(q + 1) * P],
                                   cst[:, C_SUM:C_SUM + 2], start=True, stop=True)
                mm.then_inc(s["modT_ps"], 1)

            for i in range(NT):
                pe.wait_ge(s["ln_xhat"], i + 1)
                if i == 0:
                    pe.wait_ge(s["cols_sb"], 1)
                for k in range(KD):
                    mm = pe.transpose(PS[:, 2 * i + k // 4, (k % 4) * P:(k % 4 + 1) * P], xn[:, i, k * P:(k + 1) * P], ident)
                    if k % 4 == 3:
                        mm.then_inc(s["xT_ps"], 1)
            pe.wait_ge(s["cond_done"], 6)
            ada_sums(0, 0)
            for n in range(4):
                if n < 3:
                    ada_sums(n + 1, n + 1)
                ada_cols(n)

            def project(w):
                if w % 4 == 0:
                    p1_loaded(pe, 4 + w // 4)
                if w < 4:
                    pe.wait_ge(s["xT_sb"], 6)
                else:
                    pe.wait_ge(s["win_sb"], w - 3)
                wt = unit3(ring[(5 + w // 4) % RING])
                for k in range(KD):
                    if w == 0:
                        pe.wait_ge(s["h_done"], k + 1)
                    mm = pe.matmul(PS[:, w % 4, 0:W], wt[:, k, (w % 4) * P:(w % 4 + 1) * P], hT[:, k, :],
                                   start=(k == 0), stop=(k == KD - 1))
                mm.then_inc(s["p1_used" if w % 4 == 3 else "win_ps"], 1)

            def chan_dft(g):
                pe.wait_ge(s["win_sb"], 4 + g + 1)
                if g == 0:
                    pe.wait_ge(s["smallw_in"], 32)
                    pe.wait_ge(s["mrow_sb"], 5)
                else:
                    pe.wait_ge(s["z_sb"], g)
                if g >= 2:
                    pe.wait_ge(s["yf_sb"], g - 1)
                for i in range(NT):
                    out = PS[:, 6, i * 256:(i + 1) * 256] if i < 2 else PS[:, 5, 0:256]
                    mm = pe.matmul(out, xf[:, g, TC[i]:TC[i] + P], dft[:, F_CH:F_CH + 256], start=True, stop=True)
                mm.then_inc(s["z_ps"], 1)

            def pos_dft(g):
                pe.wait_ge(s["z_sb"], g + 1)
                if g == 0:
                    pe.wait_ge(s["mrow_sb"], 6)
                need(pe, "f_sb", g)
                z = Z[:, g % 2]
                for h in range(2):
                    pe.matmul(PS[:, 4, 0:SEQ], z[:, 0, h * P:(h + 1) * P], dft[:, F_CTX + h * P:F_CTX + (h + 1) * P],
                              start=(h == 0), stop=(h == 1))
                for m in range(2):
                    for h in range(2):
                        mm = pe.matmul(PS[:, 4, SEQ:TOK], z[:, 1 + m, h * P:(h + 1) * P],
                                       dft[:, F_LAT + 512 * m + 256 * h:F_LAT + 512 * m + 256 * (h + 1)],
                                       start=(m == 0 and h == 0), stop=(m == 1 and h == 1))
                mm.then_inc(s["f_ps"], 1)

            def fourier_out(g):
                pe.wait_ge(s["f_sb"], g + 1)
                pe.wait_ge(s["z_sb"], min(g + 2, FG))
                need(pe, "yf_sb", g)
                pe.matmul(PS[:, 5, 0:TOK], fnw[:, g, :], FTs[:, g % 2, :], start=True, stop=True).then_inc(s["yf_ps"], 1)

            for w in range(12):
                project(w)
            ada_sums(4, 7)
            ada_sums(5, 8)
            ada_cols(4)
            ada_cols(5)
            for g in range(FG + 1):
                if g < FG:
                    chan_dft(g)
                if g > 0:
                    pos_dft(g - 1)
                    fourier_out(g - 1)

            pe.wait_ge(s["wbd_in"], 64)
            for it in range(8):
                c, d = it // 2, it % 2
                pe.wait_ge(s["conv_done"], c + 1)
                if it >= 2:
                    pe.wait_ge(s["gate_act"], it - 1)
                else:
                    pe.wait_ge(s["win_sb"], 12)
                for gi in range(2):
                    mm = pe.matmul(PS[:, 2 * (it % 2) + gi, 0:W], wbd[:, 8 * gi + 4 * d + c, :], xc[:, c, :],
                                   start=True, stop=True)
                mm.then_inc(s["gate_ps"], 1)
                if it == 2:
                    pe.wait_ge(s["f_sb"], FG)
                if 2 <= it < 6:
                    ada_sums(it + 4, it + 7)
                if 3 <= it < 7:
                    ada_cols(it + 3)

            def row(r, j, q):
                if r > 0:
                    pe.wait_ge(s["row_sb"], r)
                else:
                    pe.wait_ge(s["mod_sb"], 10)
                for k in range(KD):
                    mm = pe.matmul(PS[:, 6 + k // 4, (k % 4) * P:(k % 4 + 1) * P],
                                   modT[:, j * KD + k, q:q + 1].broadcast_to([P, P]), ident, start=True, stop=True)
                mm.then_inc(s["row_ps"], 1)

            def mix(h):
                p1_loaded(pe, 13 + h)
                for i in range(NT):
                    for c in range(KD):
                        mm = pe.matmul(PS[:, 2 * i + h, :], mixT[:, c, i * P:(i + 1) * P],
                                       unit3(ring[(14 + h) % RING])[:, c, :], start=(c == 0), stop=(c == KD - 1))
                    if i == NT - 1:
                        mm.then_inc(s["p1_used"], 1)
                    elif h == 1:
                        mm.then_inc(s["mix_ps"], 1)

            row(0, G1, 0)
            row(1, G1, 1)
            pe.wait_ge(s["gate_act"], 8)
            pe.wait_ge(s["yr_done"], CR)
            mix(0)
            mix(1)
            for r, (j, q) in enumerate(((SC2, 0), (SC2, 1), (SH2, 0), (SH2, 1))):
                row(2 + r, j, q)
            pe.wait_ge(s["row_sb"], 6)
            for n in range(10, 12):
                ada_sums(n, n + 5)
                ada_cols(n)

            for i in range(NT):
                pe.wait_ge(s["h2_done"], i + 1)
                for k in range(KD):
                    mm = pe.transpose(PS[:, 2 * i + k // 4, (k % 4) * P:(k % 4 + 1) * P], tt[:, i % 2, k * P:(k + 1) * P], ident)
                mm.then_inc(s["h2T_ps"], 1)
            pe.wait_ge(s["rtr_in"], 64)
            pe.wait_ge(s["x1n"], NT)
            for i in range(NT):
                pe.wait_ge(s["h2T_sb"], i + 1)
                for k in range(KD):
                    mm = pe.matmul(PS[:, 0, 20 * i:20 * i + 20], h2T[:, k, i * P:(i + 1) * P], wr[:, k, :],
                                   start=(k == 0), stop=(k == KD - 1))
            mm.then_inc(s["lg_ps"], 1)
            pe.wait_ge(s["state_done"], 8)
            pe.transpose(PS[0:8, 2, 128:256], stin[:, 0:8], ident).then_inc(s["st_ps"], 1)
            pe.wait_ge(s["assign_done"], 1)
            for i in range(NT + 1):
                for j in range(min(i, NT - 1) + 1):
                    mm = pe.matmul(PS[:, 1, NE * i:NE * (i + 1)], cst[:, C_TRI:C_TRI + P] if j == i else ones,
                                   rt[:, 3, j, :], start=(j == 0), stop=(j == min(i, NT - 1)))
            mm.then_inc(s["rank_ps"], 1)

            def dispatch(ge, n):
                pe.wait_ge(s["sel_ready"], ge + 1)
                need(pe, "xs_ready", ge)

                def tokens(slots):
                    per = 512 // slots
                    for k in range(KD):
                        out = PS[:, k // per, (k % per) * slots:(k % per + 1) * slots]
                        for m in range(3 * NT):
                            part, i = m // NT, m % NT
                            mm = pe.matmul(out, h2b[:, 2 - part, i, k * P:(k + 1) * P],
                                           sel[:, i, 0:slots], start=(m == 0), stop=(m == 3 * NT - 1))
                    mm.then_inc(s["x_disp"], 1)

                fork(pe, n, lambda: tokens(HALF), lambda: tokens(CAP))

            def prologue(ge, pb):
                if isinstance(ge, int):
                    pe.wait_ge(s["h2b3"], NT)
                    pe.wait_ge(s["route_done"], 2)
                dispatch(ge, tokens_of(pe, 0, pb))

            def body(ge, e, q, p, last, pb):
                n = tokens_of(pe, e, pb)
                n1 = None if last else tokens_of(pe, e + 1, pb)

                def products(out, xh, xl, wh, wl, kk, width):
                    n_h = width // 512
                    trio = [(xh, wh), (xh, wl)] + ([(xl, wh)] if xl is not None else [])
                    for k in range(kk):
                        for m, (x, w) in enumerate(trio):
                            for h in range(n_h):
                                mm = pe.matmul(out[h], x[:, k, :], w[:, k, h * 512:(h + 1) * 512],
                                               start=(k == 0 and m == 0), stop=(k == kk - 1 and m == len(trio) - 1))
                    mm.then_inc(s["unit_used"], 1)

                def first(many):
                    for j in range(2):
                        pe.wait_ge(s["lo_done"], ge * 6 + (2 * j + 2))
                        if j == 0:
                            pe.wait_ge(s["xs_ready"], ge + 1)
                            need(pe, "g_done", ge)
                            need(pe, "u_done", ge)
                        products([PS[:, 2 + j, :]], xsH, xsL if many else None, unit3(whi[j]), unit3(wlo[3 * p + j]), KD, 512)

                def turn(many):
                    pe.wait_ge(s["g_done"], ge + 1)
                    pe.wait_ge(s["u_done"], ge + 1)
                    need(pe, "hts_ready", ge)
                    if many:
                        for k in range(KF):
                            mm = pe.transpose(PS[:, 4, k * P:(k + 1) * P], hid[:, k * P:(k + 1) * P], ident)
                    else:
                        for x, bank in ((sg, 4), (hid, 7)):
                            for k in range(KF):
                                mm = pe.matmul(PS[:, bank, k * HALF:(k + 1) * HALF], x[:, k * P:(k + 1) * P],
                                               cst[:, C_TWO:C_TWO + HALF], start=True, stop=True)
                    mm.then_inc(s["ht_ps"], 1)

                def down(many):
                    pe.wait_ge(s["hts_ready"], ge + 1)
                    pe.wait_ge(s["lo_done"], ge * 6 + 6)
                    need(pe, "y_sb", ge)
                    products([PS[:, 5, :], PS[:, 6, :]], hTH, hTL if many else None, unit3(whi[2], D),
                             unit3(wlo[3 * p + 2], D), KF, D)

                def whole(many):
                    first(many)
                    turn(many)

                fork(pe, n, lambda: whole(False), lambda: whole(True))
                if not last:
                    dispatch(ge + 1, n1)
                fork(pe, n, lambda: down(False), lambda: down(True))

            passes(pe, lambda pb: pairs(pe, lambda ge: prologue(ge, pb), lambda *a: body(*a, pb), pb), lambda: None)
            pe.wait_ge(s["passes_done"], 1)
            for q in range(2):
                for k in range(KD):
                    mm = pe.matmul(PS[:, 2 * q + k // 4, (k % 4) * P:(k % 4 + 1) * P],
                                   modT[:, G2 * KD + k, q:q + 1].broadcast_to([P, P]), ident, start=True, stop=True)
            mm.then_inc(s["g2_ps"], 1)


_INS = ["x_prompt", "x_sample", "w_ada", "w_in", "rg_wa", "rg_wi", "fn_w", "w_out", "router_g_w", "router_e_w",
        "router_g_b", "router_e_b", "ex_w_gate", "ex_w_up", "ex_w_down", "ln1_g", "ln1_b", "ln2_g", "ln2_b"]
_ROWS = ["c", "c_ctx", "b_ada", "ln_in_g", "ln_in_b", "conv_w", "conv_b", "rg_ba", "rg_bi", "rg_lam", "fn_b"]


def kernel(**inputs):
    import concourse.bacc as _bacc
    from concourse.bass_utils import run_bass_kernel_spmd as _run

    nc = _bacc.Bacc("TRN2", target_bir_lowering=False, num_devices=1)
    const, dft, pos = constants()
    arrays = {"const": const, "dft": dft, "pos": pos}
    for name in _INS:
        arrays[name] = np.ascontiguousarray(inputs[name])
    for name in _ROWS:
        arrays[name] = np.ascontiguousarray(inputs[name]).reshape(-1, P)
    arrays["state"] = np.ascontiguousarray(inputs["state_rglru"]).reshape(-1, P)
    for name in ("ln_in_g", "ln_in_b"):
        arrays[name + "_row"] = np.ascontiguousarray(inputs[name])
    for name in ("ln1_g", "ln1_b", "ln2_g", "ln2_b", "router_g_b", "router_e_b"):
        arrays[name] = arrays[name].reshape(-1)
    t = {n: nc.dram_tensor("in_" + n, a.shape, mybir.dt.from_np(a.dtype), kind="ExternalInput").ap()
         for n, a in arrays.items()}
    outs = {"y_prompt": (1, SEQ, D), "y_sample": (1, LAT, D), "new_state": (8, P)}
    for n, shape in outs.items():
        t[n] = nc.dram_tensor("out_" + n, shape, F32, kind="ExternalOutput").ap()
    build(nc, t)
    r = _run(nc, [{"in_" + n: a for n, a in arrays.items()}], core_ids=[0]).results[0]
    return (r["out_y_prompt"], r["out_y_sample"], r["out_new_state"].reshape(1, 1, 2, DR))
```

```python
from contextlib import ExitStack

import numpy as np

import concourse.bass as bass
from concourse import mybir

F32 = mybir.dt.float32
F32R = mybir.dt.float32r
BF16 = mybir.dt.bfloat16
U32 = mybir.dt.uint32
I32 = mybir.dt.int32
ALU = mybir.AluOpType
ACT = mybir.ActivationFunctionType
AX = mybir.AxisListType

P = 128
D = 1024
KD = D // P
SEQ = 128
LAT = 256
TOK = SEQ + LAT
NT = TOK // P
DR = D // 2
CR = DR // P
FG = 4
NE = 16
NG = 4
EPG = NE // NG
FE = D // 2
KF = FE // P
GRID_W = 64
ALPHA = 2.0 ** 0.25
LN_EPS = 1e-5
W = SEQ + 3 + LAT + 1
TC = [0, SEQ + 3, SEQ + 3 + P]
SEG = [(0, SEQ), (SEQ + 3, LAT)]
SEGC = [(0, SEQ), (SEQ, LAT)]
XW = W + 3
UNIT = 4096
RING = 6
NP1 = 17
HALF = P // 2
CAP = P
PASSES = TOK // CAP
YROWS = NE * CAP
FAR = 1e5

C_ID, C_IOTA = 0, 128
C_EROW, C_COD16, C_COD4 = C_IOTA + TOK, C_IOTA + TOK + 16, C_IOTA + TOK + 32
C_SUM = C_COD4 + 4
C_TWO = C_SUM + 2
C_PASS = C_TWO + 64
NCONST = C_PASS + PASSES
F_CH, F_CTX, F_LAT = 0, 256, 512
F_TRI = F_LAT + 2 * 512
NDFT = F_TRI + 2 * P

A_C, A_CTX, A_BADA, A_LNG, A_LNB, A_CW, A_CB, A_L1G, A_L1B, NA = 0, 8, 16, 64, 72, 80, 96, 100, 108, 116
B_BA, B_BI, B_LAM, B_ST, B_FB, NB = 0, 8, 16, 24, 32, 36

SH1, SC1, G1, SH2, SC2, G2 = range(6)


def constants():
    c = np.zeros((P, NCONST), np.float32)
    c[:, C_ID:C_ID + P] = np.eye(P)
    c[:, C_IOTA:C_IOTA + TOK] = np.arange(TOK)
    c[:, C_EROW:C_EROW + NE] = np.arange(NE) * CAP
    c[:, C_COD16:C_COD16 + NE] = NE - np.arange(NE)
    c[:, C_COD4:C_COD4 + NG] = NG - np.arange(NG)
    c[:, C_PASS:C_PASS + PASSES] = np.arange(PASSES) * CAP
    for q in range(2):
        c[q::32, C_SUM + q] = 1
        c[64 * q:64 * q + 64, C_TWO:C_TWO + 64] = np.eye(64)

    def dft(n):
        a = 2 * np.pi * (np.outer(np.arange(n), np.arange(n)) % n) / n
        return np.cos(a) / np.sqrt(n), np.sin(a) / np.sqrt(n)

    f = np.zeros((P, NDFT), np.float32)
    co, si = dft(P)
    f[:, 0:P], f[:, P:2 * P] = co, si
    f[:, F_TRI:F_TRI + P] = np.triu(np.ones((P, P)), 1)
    f[:, F_TRI + P:] = 1
    f[:, F_CTX:F_CTX + P], f[:, F_CTX + P:F_CTX + 2 * P] = co, -si
    co, si = dft(LAT)
    for m in range(2):
        f[:, F_LAT + 512 * m:F_LAT + 512 * m + LAT] = co[m * P:(m + 1) * P]
        f[:, F_LAT + 512 * m + LAT:F_LAT + 512 * (m + 1)] = -si[m * P:(m + 1) * P]

    q = D // 4
    freqs = (1.0 / (10000.0 ** (np.arange(q, dtype=np.float32) / q))).astype(np.float32)
    r = np.repeat(np.arange(LAT // GRID_W, dtype=np.float32), GRID_W)[:, None] * freqs[None]
    k = np.tile(np.arange(GRID_W, dtype=np.float32), LAT // GRID_W)[:, None] * freqs[None]
    pos = np.concatenate([np.sin(r), np.cos(r), np.sin(k), np.cos(k)], axis=-1).astype(np.float32)
    return c, f, pos


def build(nc, t):
    ctx = ExitStack()
    with ctx:
        def sem(name):
            return ctx.enter_context(nc.semaphore(name))

        def at(name, off, shape, dt=F32):
            return nc.alloc_sbuf_tensor_at(name, shape, dt, offset=off)

        base = (nc._sbuf_addr_for_side("left") + 31) // 32 * 32
        RB = UNIT * 4
        ring = [at(f"ring{s}", base + s * RB, [P, UNIT]) for s in range(RING)]
        wlo = [at(f"wlo{s}", base + s * RB, [P, UNIT], F32R) for s in range(RING)]
        o = base + RING * RB
        xn = at("xn", o, [P, NT, D])
        o += NT * D * 4
        place = [o]

        def keep(name, shape, dt=F32):
            n = int(np.prod(shape[1:])) * (2 if dt == BF16 else 4)
            n = (n + 31) // 32 * 32
            place[0] += n
            return at(name, place[0] - n, shape, dt)

        cst = keep("cst", [P, NCONST])
        tri_ones = keep("tri_ones", [P, 2, P], BF16)
        marks16 = keep("marks16", [P, NT, NE], BF16)
        modT = keep("modT", [P, 6 * KD, 2])
        mrow = keep("mrow", [P, 512])
        cols = keep("cols", [P, NA + NB])
        cond = keep("cond", [P, KD, 2])
        cond32 = keep("cond32", [P, KD, 32])
        cmod = keep("cmod", [P, 2, KD, 2])
        bga = keep("bga", [P, 16])
        spl = keep("spl", [P, 6, 8])
        stat = keep("stat", [P, NT, 16])
        stin = keep("stin", [P, 16])
        small = keep("small", [P, 8])
        rankA = keep("rankA", [P, NE + 1, NT])
        posn = keep("posn", [P, PASSES, 2, NT], U32)
        wk = keep("wk", [P, 2, NT])
        cnt = keep("cnt", [P, 1 + NE], I32)
        strow = keep("strow", [P, P])
        router0 = place[0]
        wr = keep("wr", [P, KD, NG + NE])
        rb = keep("rb", [P, NG + NE])
        lg = keep("lg", [P, NT, NG + NE])
        rt = keep("rt", [P, 8, NT, NE])
        rs = keep("rs", [P, 12, NT])
        posf = keep("posf", [P, 2, 2 * NT])
        posw = keep("posw", [P, 2, PASSES, 2 * NT])
        place[0] = max(place[0], router0 + D * 4)
        ylow = at("ylow", router0, [HALF, D])
        A0 = place[0]
        h2b = at("h2b", A0, [P, 3, NT, D], BF16)
        o = A0 + 3 * NT * D * 2
        M0 = o
        xsH = at("xsH", o, [P, KD, CAP], F32R); o += KD * CAP * 4
        xsL = at("xsL", o, [P, KD, CAP], F32R); o += KD * CAP * 4
        hTH = at("hTH", o, [P, KF, CAP], F32R); o += KF * CAP * 4
        hTL = at("hTL", o, [P, KF, CAP], F32R); o += KF * CAP * 4
        sgT = at("sgT", o - KF * CAP * 4, [P, KF, HALF])
        hidT = at("hidT", o - KF * CAP * 2, [P, KF, HALF])
        sel = at("sel", o, [P, NT, CAP], BF16); o += NT * CAP * 2
        sg = at("sg", o, [P, FE]); o += FE * 4
        hid = at("hid", o, [P, FE]); o += FE * 4
        ysb = at("ysb", o, [P, D]); o += D * 4
        tt = at("tt", M0, [P, 2, D])
        h2T = at("h2T", M0 + 2 * D * 4, [P, KD, TOK])
        B0 = max(o, M0 + 2 * D * 4 + KD * TOK * 4)
        whi = [at(f"whi{j}", B0 + j * RB, [P, UNIT], F32R) for j in range(3)]
        end = B0 + 3 * RB
        assert end <= base + nc.sbuf_bytes_remaining
        hT = at("hT", B0, [P, KD, W])
        mixT = at("mixT", B0, [P, CR, TOK])
        FTs = at("FTs", B0 + KD * W * 4, [P, 2, TOK])
        rtmp = at("rtmp", B0 + KD * W * 4, [P, 2, W])
        assert KD * W * 4 + 2 * W * 4 <= RB
        tt3 = at("tt3", B0 + 8192, [P, D])
        assert CR * TOK * 4 <= 8192 and 8192 + D * 4 <= KD * W * 4
        tts = [tt[:, 0, :], tt[:, 1, :], tt3[:, :]]
        o = B0 + RB
        gr = at("gr", o, [P, CR, W]); o += CR * W * 4
        xf = at("xf", o, [P, FG, W]); o += FG * W * 4
        Z = at("Z", o, [P, 2, NT, 2 * P]); o += 2 * NT * 2 * P * 4
        dft = at("dft", o, [P, NDFT]); o += NDFT * 4
        fnw = at("fnw", o, [P, FG, P]); o += FG * P * 4
        hfb = at("hfb", o, [P, 2, W]); o += 2 * W * 4
        assert o <= end
        rows = at("rows", B0 + RB, [P, 8, D])
        o = A0
        gtmp = at("gtmp", o, [P, 3, 4, W])
        pos = at("pos", o, [P, 2, D])
        lnin = at("lnin", o + 2 * D * 4, [P, 2, D])
        o += max(3 * 4 * W * 4, 4 * D * 4)
        xc = at("xc", o, [P, CR, W]); o += CR * W * 4
        xpad = at("xpad", o, [P, CR, XW + 1]); o += CR * (XW + 1) * 4
        wbd = at("wbd", o, [P, 16, P]); o += 16 * P * 4
        assert o <= B0, (o, B0)
        yfs = at("yfs", A0, [P, CR, TOK])
        rowA = at("rowA", B0 + 2 * RB, [P, P])
        rowB = at("rowB", B0 + 2 * RB + P * 4, [P, P])
        y12 = at("y12", base, [P, 2, NT, D])
        fin = at("fin", base + 2 * NT * D * 4, [P, NT, D])
        ln2 = at("ln2", base + 3 * NT * D * 4, [P, 2, D])

        PS = ctx.enter_context(nc.psum_tensor("PS", [P, 8, 512], F32))
        Y_dram = [nc.dram_tensor(f"y_rows{pb}", (YROWS, D), F32, kind="Internal").ap() for pb in range(PASSES)]

        s = {n: sem(n) for n in (
            "const_in rowA_in rowB_in x_in pos_in lnin_in wbd_in smallw_in ln1_in ln2_in rtr_in cols_ps "
            "cols_sb cond_done zeroed ln_xhat xT_ps xT_sb mrow_sb modT_ps mod_sb h_done win_ps win_sb "
            "conv_done gate_ps gate_act rec_v mult_done q_done ta_done sq_done scan_done gelu_t gelu_th "
            "gelu_done yr_done z_ps z_sb f_ps f_sb yf_ps yf_sb row_ps row_sb mix_ps xn_done xn_pool x1n "
            "x1_done h2_done h2b1 mod2_done h2r h2b2 h2b3 h2T_ps h2T_sb lg_ps assign_done rank_ps route_done "
            "pos_pool p1_used unit_used hi_done lo_done lo_pool sel_ready x_disp xs_hi xs_ready g_done "
            "u_done silu_done hid_done hth_done ht_act ht_ps hts_ready y_sb y_sum y_stored y_zeroed "
            "passes_done gathered g2_ps fin_y1 fin_stat fin_norm fin_mul fin_done fin_last banks_free "
            "out_done var_done root_done state_done st_ps st_row st_out tri_done dve_step act_step pool_step").split()}
        gathered_in = [[sem(f"gathered_in{pb}_{i}") for i in range(NT)] for pb in range(PASSES)]
        ring_in = [sem(f"ring_in{k}") for k in range(RING)]

        def unit3(buf, n=512):
            return buf[:, :].rearrange("p (k n) -> p k n", n=n)

        def need(eng, name, value):
            if isinstance(value, int) and value <= 0:
                return
            eng.wait_ge(s[name], value)

        def p1_loaded(eng, u):
            slot = (u + 1) % RING
            eng.wait_ge(ring_in[slot], 16 * ((u + 1) // RING + (slot > 0)))

        block = ctx.enter_context(nc.Block())

        ada = t["w_ada"][0].rearrange("(k p) n -> p k n", p=P)
        win = t["w_in"][0].rearrange("(k p) n -> p k n", p=P)
        wout = t["w_out"][0].rearrange("(k p) n -> p k n", p=P)
        p1_units = ([(ada, SH1 * D), (ada, SH1 * D + 512), (ada, SC1 * D), (ada, SC1 * D + 512)]
                    + [(win, 0), (win, 1024), (win, 512)]
                    + [(ada, G1 * D), (ada, G1 * D + 512), (ada, SH2 * D), (ada, SH2 * D + 512),
                       (ada, SC2 * D), (ada, SC2 * D + 512)]
                    + [(wout, 0), (wout, 512)] + [(ada, G2 * D), (ada, G2 * D + 512)])
        GATE_WITHIN = {5: 1, 6: 3, 7: 4, 8: 6}
        GATE_AFTER = {4: 0, 5: 2, 7: 5, 8: 7}
        ADA_GROUPS = [4, 6, 10, 12]
        ADA_UNIT = [0, 1, 2, 3, 7, 8, 9, 10, 11, 12, 15, 16]
        ABANK = [6, 4] * 5 + [6, 6]
        ada_order = [SH1, SC1, G1, SH2, SC2, G2]
        experts = [
            t["ex_w_gate"][0].rearrange("e (k p) n -> p e k n", p=P),
            t["ex_w_up"][0].rearrange("e (k p) n -> p e k n", p=P),
            t["ex_w_down"][0].rearrange("e (k p) n -> p e k n", p=P),
        ]

        def passes(eng, body):
            body(0)
            most = eng.value_load(cnt[0:1, 0:1], min_val=0, max_val=TOK)
            with eng.Fori(1, PASSES) as pb:
                with eng.If(most > pb * CAP):
                    body(pb)

        def tokens_of(eng, e, pb):
            return eng.value_load(cnt[0:1, bass.ds(e + 1, 1)], min_val=0, max_val=TOK) if isinstance(pb, int) and pb == 0 else None

        def fork(eng, n, few, many):
            if n is None:
                many()
                return
            with eng.If(n > HALF):
                many()
            with eng.Else():
                few()

        def pairs(eng, prologue, body, pb):
            ge0 = pb * NE
            prologue(ge0)
            for p in range(2):
                body(ge0 + p, p, pb * (NE // 2), p, False)
            with eng.Fori(1, NE // 2 - 1) as it:
                for p in range(2):
                    body(ge0 + it * 2 + p, it * 2 + p, pb * (NE // 2) + it, p, False)
            for p in range(2):
                body(ge0 + NE - 2 + p, NE - 2 + p, pb * (NE // 2) + NE // 2 - 1, p, p == 1)

        @block.sync
        def _(sp):
            for u, (src, c0) in enumerate(p1_units):
                if u == 1:
                    for i in range(NT):
                        tokens = t["x_prompt"][0] if i == 0 else t["x_sample"][0, (i - 1) * P:i * P]
                        sp.dma_start(xn[:, i, :], tokens).then_inc(s["x_in"], 16)
                    sp.dma_start(pos[:, :, :], t["pos"].rearrange("(i p) d -> p i d", p=P)).then_inc(s["pos_in"], 16)
                    sp.wait_ge(s["const_in"], 16)
                    sp.wait_ge(s["rowA_in"], 16 * 9)
                    sp.wait_ge(s["rowB_in"], 16 * 5)
                if u + 1 >= RING + 1:
                    sp.wait_ge(s["p1_used"], u + 1 - RING)
                sp.dma_start(unit3(ring[(u + 1) % RING]), src[:, :, c0:c0 + 512]).then_inc(ring_in[(u + 1) % RING], 16)

            def load(ge, e, p, first):
                for j in range(3):
                    if first:
                        sp.wait_ge(s["p1_used"], NP1 + 1 - RING + 3 * p + j)
                    else:
                        sp.wait_ge(s["unit_used"], ge * 3 + (j - 5))
                    slot = 3 * p + j
                    sp.dma_start(unit3(ring[slot], D if j == 2 else 512),
                                 experts[j][:, e]).then_inc(ring_in[slot], 16)

            for p in range(2):
                load(p, p, p, True)
            with sp.Fori(1, NE // 2) as it:
                for p in range(2):
                    load(it * 2 + p, it * 2 + p, p, False)
            sp.wait_ge(s["route_done"], 1)
            most = sp.value_load(cnt[0:1, 0:1], min_val=0, max_val=TOK)
            with sp.Fori(1, PASSES) as pb:
                with sp.If(most > pb * CAP):
                    with sp.Fori(0, NE // 2) as it:
                        for p in range(2):
                            load(pb * NE + it * 2 + p, it * 2 + p, p, False)
            sp.wait_ge(s["passes_done"], 1)
            for r, n in enumerate(("ln2_g", "ln2_b")):
                sp.dma_start(ln2[:, r, :], t[n].partition_broadcast(P)).then_inc(s["ln2_in"], 16)
            for i in range(NT):
                if i < NT - 1:
                    sp.wait_ge(s["fin_done"], i + 1)
                else:
                    sp.wait_ge(s["fin_last"], 1)
                dst = t["y_prompt"][0] if i == 0 else t["y_sample"][0, (i - 1) * P:i * P]
                sp.dma_start(dst, fin[:, i, :]).then_inc(s["out_done"], 16)
            sp.wait_ge(s["out_done"], 16 * NT)

        @block.scalar
        def _(act):
            n_step = [0]

            def root(n):
                i = n % NT
                act.wait_ge(s["var_done"], n + 1)
                act.activation(stat[:, i, 13:14], stat[:, i, 13:14], ACT.Sqrt).then_inc(s["root_done"], 1)

            def link(ins):
                n_step[0] += 1
                ins.then_inc(s["act_step"], 1)
                act.wait_ge(s["act_step"], n_step[0])

            act.dma_start(cst[:, :], t["const"]).then_inc(s["const_in"], 16)
            for n, r0, k in (("c", A_C, 8), ("c_ctx", A_CTX, 8), ("b_ada", A_BADA, 48), ("ln_in_g", A_LNG, 8),
                             ("ln_in_b", A_LNB, 8), ("conv_w", A_CW, 16), ("conv_b", A_CB, 4),
                             ("ln1_g_col", A_L1G, 8), ("ln1_b_col", A_L1B, 8)):
                act.dma_start(rowA[r0:r0 + k, :], t[n]).then_inc(s["rowA_in"], 16)
            for n, r0, k in (("rg_ba", B_BA, 8), ("rg_bi", B_BI, 8), ("rg_lam", B_LAM, 8), ("state", B_ST, 8),
                             ("fn_b", B_FB, 4)):
                act.dma_start(rowB[r0:r0 + k, :], t[n]).then_inc(s["rowB_in"], 16)
            act.wait_ge(s["cols_sb"], 1)
            for q, c0 in enumerate((A_CTX, A_C)):
                act.activation(cond[:, :, q], cols[:, c0:c0 + KD], ACT.Exp, scale=-1.0).then_inc(s["cond_done"], 1)
            act.activation(spl[:, 0, :], cols[:, NA + B_LAM:NA + B_LAM + 8], ACT.Abs).then_inc(s["act_step"], 1)
            n_step[0] += 1
            act.wait_ge(s["act_step"], n_step[0])
            act.activation(spl[:, 1, :], spl[:, 0, :], ACT.Exp, scale=-1.0).then_inc(s["cond_done"], 1)

            for r, n in enumerate(("ln_in_g", "ln_in_b")):
                act.dma_start(lnin[:, r, :], t[n + "_row"].partition_broadcast(P)).then_inc(s["lnin_in"], 16)
            act.wait_ge(s["zeroed"], 1)
            for gi, n in enumerate(("rg_wa", "rg_wi")):
                for h in range(2):
                    act.dma_start(wbd[64 * h:64 * h + 64, 8 * gi:8 * gi + 8, 64 * h:64 * h + 64],
                                  t[n][0].rearrange("d (c q) i j -> q i (d c) j", q=2)[h]).then_inc(s["wbd_in"], 16)
            act.dma_start(fnw[:, :, :], t["fn_w"][0].rearrange("g i j -> i g j")).then_inc(s["smallw_in"], 16)
            act.dma_start(dft[:, :], t["dft"]).then_inc(s["smallw_in"], 16)

            def ada_rows(n):
                act.wait_ge(s["p1_used"], ADA_UNIT[n] + 1)
                need(act, "modT_ps", n)
                act.copy(mrow[:, :], PS[:, ABANK[n], :]).then_inc(s["mrow_sb"], 1)

            ada_rows(0)
            ada_rows(1)
            for i in range(NT):
                root(i)

            act.wait_ge(s["zeroed"], 3)
            for i in range(NT):
                for hf in range(2):
                    act.wait_ge(s["xT_ps"], 2 * i + hf + 1)
                    act.copy(hT[:, 4 * hf:4 * hf + 4, TC[i]:TC[i] + P],
                             PS[:, 2 * i + hf, :].rearrange("p (k n) -> p k n", n=P)).then_inc(s["xT_sb"], 1)

            ada_rows(2)
            ada_rows(3)

            def gate(it):
                c, d = it // 2, it % 2
                q = it % 4
                act.wait_ge(s["gate_ps"], it + 1)
                if it >= 4:
                    act.wait_ge(s["scan_done"], it - 3)
                if it >= 2:
                    act.wait_ge(s["rec_v"], it - 1)
                tr, a_, q_, v_ = rtmp[:, it % 2], gtmp[:, 0, q], gtmp[:, 1, q], gtmp[:, 2, q]
                if it == 0:
                    act.wait_ge(s["xn_done"], NT)
                link(act.activation(tr, PS[:, 4, 0:W], ACT.Tanh, bias=bga[:, 4 * d + c:4 * d + c + 1], scale=0.5))
                act.activation(q_, PS[:, 5, 0:W], ACT.Tanh, bias=bga[:, 8 + 4 * d + c:9 + 4 * d + c], scale=0.5)\
                    .then_inc(s["gate_act"], 1)
                sc = spl[:, 5, 4 * d + c:4 * d + c + 1]
                act.activation(v_, tr, ACT.Tanh, bias=sc, scale=sc).then_inc(s["ta_done"], 1)
                act.activation(a_, tr, ACT.Exp, bias=sc, scale=sc).then_inc(s["ta_done"], 1)
                act.wait_ge(s["ta_done"], 2 * it + 2)
                act.activation(tr, a_, ACT.Square).then_inc(s["sq_done"], 1)
                if q == 3:
                    act.wait_ge(s["rec_v"], it + 1)
                    act.activation(gtmp[:, 2], gtmp[:, 2], ACT.Sqrt, scale=-1.0).then_inc(s["mult_done"], 1)

            def gelu_tanh(c):
                act.wait_ge(s["gelu_t"], c + 1)
                act.activation(xpad[:, c, 0:W], xpad[:, c, 0:W], ACT.Tanh, scale=float(np.sqrt(2 / np.pi)))\
                    .then_inc(s["gelu_th"], 1)

            for w in range(12):
                if w in GATE_WITHIN:
                    gate(GATE_WITHIN[w])
                if w % 4 == 3:
                    act.wait_ge(s["p1_used"], 5 + w // 4)
                else:
                    act.wait_ge(s["win_ps"], w + 1 - w // 4)
                c = w % 4
                src = PS[:, w % 4, 0:W]
                if w < 4:
                    act.copy(xpad[:, c, 2:2 + W], src).then_inc(s["win_sb"], 1)
                elif w < 8:
                    act.copy(xf[:, c, :], src).then_inc(s["win_sb"], 1)
                else:
                    act.copy(gr[:, c, :], src).then_inc(s["win_sb"], 1)
                if w in GATE_AFTER:
                    gate(GATE_AFTER[w])
                if w >= 8:
                    act.wait_ge(s["z_ps"], c + 1)
                    if c >= 2:
                        act.wait_ge(s["f_ps"], c - 1)
                    act.copy(Z[:, c % 2, 0:2, :], PS[:, 6, :].rearrange("p (i n) -> p i n", n=256))
                    act.copy(Z[:, c % 2, 2, :], PS[:, 7, 0:256]).then_inc(s["z_sb"], 1)
                    gelu_tanh(c)
            act.wait_ge(s["smallw_in"], 32)
            act.copy(tri_ones[:, :, :], dft[:, F_TRI:].rearrange("p (a n) -> p a n", n=P)).then_inc(s["tri_done"], 1)
            for n in range(4, 10):
                ada_rows(n)

            act.wait_ge(s["yr_done"], CR)
            for r in range(6):
                act.wait_ge(s["row_ps"], r + 1)
                act.copy(rows[:, r, :], PS[:, 6:8, :].rearrange("p a n -> p (a n)")).then_inc(s["row_sb"], 1)
                if r == 1:
                    root(NT)
                if r == 0:
                    for k, n in enumerate(("ln1_g", "ln1_b")):
                        act.dma_start(rows[:, 6 + k, :], t[n].partition_broadcast(P)).then_inc(s["ln1_in"], 16)

            def h2_copies(i):
                act.wait_ge(s["h2_done"], i + 1)
                act.copy(h2b[:, 0, i, :], tts[i]).then_inc(s["h2b1"], 1)
                act.wait_ge(s["h2T_ps"], i + 1)
                act.copy(h2T[:, :, i * P:(i + 1) * P], PS[:, 2 * i:2 * i + 2, :].rearrange("p a (k n) -> p (a k) n", n=P))\
                    .then_inc(s["h2T_sb"], 1)

            def h2_second(i):
                act.wait_ge(s["h2r"], i + 1)
                act.copy(h2b[:, 1, i, :], tts[i]).then_inc(s["h2b2"], 1)

            root(NT + 1)
            ada_rows(10)
            h2_copies(0)
            root(NT + 2)
            ada_rows(11)
            h2_copies(1)
            h2_copies(2)
            for i in range(NT):
                h2_second(i)

            halves = [(0, UNIT // 2), (UNIT // 2, UNIT)]

            def split_hi(ge, q, p, j, hs=(0, 1)):
                for h in hs:
                    if h == 0:
                        act.wait_ge(ring_in[3 * p + j], q * 16 + 16 * ((NP1 + 1) // RING + (3 * p + j > 0)))
                        need(act, "unit_used", ge * 3 + (j - 2))
                    a, b = halves[h]
                    act.copy(whi[j][:, a:b], ring[3 * p + j][:, a:b]).then_inc(s["hi_done"], 1)

            def x_hi(ge, n):
                def copy(dst, src):
                    act.wait_ge(s["x_disp"], ge + 1)
                    need(act, "unit_used", ge * 3 - 1)
                    act.copy(dst, src).then_inc(s["xs_hi"], 1)

                fork(act, n,
                     lambda: copy(xsH[:, :, 0:HALF], PS[:, 0, :].rearrange("p (k n) -> p k n", n=HALF)),
                     lambda: copy(xsH[:, :, :], PS[:, 0:2, :].rearrange("p a (k n) -> p (a k) n", n=CAP)))

            def rows_out(ge, n):
                def few():
                    act.wait_ge(s["unit_used"], ge * 3 + 3)
                    need(act, "y_stored", ge * 16)
                    act.copy(ylow[:, :], PS[HALF:CAP, 5:7, :].rearrange("p a n -> p (a n)"))
                    act.copy(ysb[0:HALF, :], PS[0:HALF, 5:7, :].rearrange("p a n -> p (a n)")).then_inc(s["y_sb"], 1)

                def many():
                    act.wait_ge(s["unit_used"], ge * 3 + 3)
                    need(act, "y_stored", ge * 16)
                    act.copy(ysb[:, :], PS[:, 5:7, :].rearrange("p a n -> p (a n)")).then_inc(s["y_sb"], 1)

                fork(act, n, few, many)

            def prologue(ge, pb):
                q = ge // 2
                if isinstance(ge, int):
                    act.wait_ge(s["h2b3"], NT)
                split_hi(ge, q, 0, 0)
                if isinstance(ge, int):
                    act.wait_ge(s["assign_done"], 1)
                    act.activation(rt[:, 6, :, 0:NG], rt[:, 5, :, 0:NG], ACT.Exp).then_inc(s["pos_pool"], 1)
                    act.activation(rs[:, 5, :], rs[:, 4, :], ACT.Exp).then_inc(s["pos_pool"], 1)
                    act.wait_ge(s["h2_done"], NT)
                split_hi(ge, q, 0, 1)
                if isinstance(ge, int):
                    act.wait_ge(s["route_done"], 1)
                n = tokens_of(act, 0, pb)
                x_hi(ge, n)
                if isinstance(ge, int):
                    act.wait_ge(s["x1_done"], NT)
                split_hi(ge, q, 0, 2)
                if isinstance(ge, int):
                    act.wait_ge(s["route_done"], 2)

            def body(ge, e, q, p, last, pb):
                q1 = q + p
                n = tokens_of(act, e, pb)
                n1 = None if last else tokens_of(act, e + 1, pb)

                def gate_few():
                    act.wait_ge(s["unit_used"], ge * 3 + 1)
                    need(act, "ht_ps", ge)
                    act.copy(sg[:, :], PS[:, 2, :]).then_inc(s["g_done"], 1)

                def gate_many():
                    act.wait_ge(s["unit_used"], ge * 3 + 1)
                    need(act, "ht_ps", ge)
                    act.activation(sg[:, :], PS[:, 2, :], ACT.Tanh, scale=0.5).then_inc(s["g_done"], 1)

                def hidden_few():
                    act.wait_ge(s["ht_ps"], ge + 1)
                    need(act, "unit_used", ge * 3)
                    act.activation(sgT[:, :, :], PS[:, 4, 0:KF * HALF].rearrange("p (k n) -> p k n", n=HALF), ACT.Tanh,
                                   scale=0.5).then_inc(s["ht_act"], 1)

                def hidden_many():
                    act.wait_ge(s["ht_ps"], ge + 1)
                    need(act, "unit_used", ge * 3)
                    act.copy(hTH[:, :, :], PS[:, 4, :].rearrange("p (k n) -> p k n", n=CAP)).then_inc(s["ht_act"], 1)

                fork(act, n, gate_few, gate_many)
                if not last:
                    split_hi(ge + 1, q1, 1 - p, 0)
                fork(act, n, hidden_few, hidden_many)
                if not (isinstance(e, int) and e == 0):
                    rows_out(ge - 1, tokens_of(act, e - 1, pb))
                if not last:
                    split_hi(ge + 1, q1, 1 - p, 1, (0,))
                    x_hi(ge + 1, n1)
                    split_hi(ge + 1, q1, 1 - p, 1, (1,))
                    split_hi(ge + 1, q1, 1 - p, 2)
                else:
                    rows_out(ge, n)

            passes(act, lambda pb: pairs(act, lambda ge: prologue(ge, pb), lambda *a: body(*a, pb), pb))

            def share(i):
                act.wait_ge(gathered_in[0][i], 32)
                act.wait_ge(s["gathered"], i + 1)
                act.activation(fin[:, i, :], y12[:, 0, i, :], ACT.Copy, scale=wk[:, 0, i:i + 1]).then_inc(s["fin_y1"], 1)

            def normal(i):
                root(2 * NT + i)
                act.wait_ge(s["fin_stat"], i + 1)
                act.activation(fin[:, i, :], fin[:, i, :], ACT.Identity, scale=stat[:, i, 13:14],
                               bias=stat[:, i, 14:15]).then_inc(s["fin_norm"], 1)

            share(0)
            share(1)
            normal(0)
            share(2)
            normal(1)
            normal(2)

        @block.vector
        def _(dve):
            n_step = [0]
            n_norm = [0]

            def step(ins):
                n_step[0] += 1
                ins.then_inc(s["dve_step"], 1)

            def link(ins):
                step(ins)
                dve.wait_ge(s["dve_step"], n_step[0])

            def norm_var(x, st):
                step(dve.bn_stats(st[:, 0:6], x[:, 0:512]))
                link(dve.bn_stats(st[:, 6:12], x[:, 512:1024]))
                link(dve.bn_aggr(st[:, 12:14], st[:, 0:12].rearrange("p (a b) -> p a b", b=6)))
                dve.tensor_scalar(st[:, 13:14], st[:, 13:14], LN_EPS, None, ALU.add).then_inc(s["var_done"], 1)

            def norm_root(st):
                n_norm[0] += 1
                dve.wait_ge(s["root_done"], n_norm[0])
                link(dve.reciprocal(st[:, 13:14], st[:, 13:14]))

            def norm_stats(x, st):
                norm_var(x, st)
                norm_root(st)

            dve.wait_ge(s["cols_ps"], 1)
            dve.tensor_copy(cols[:, :], PS[:, 0, 0:NA + NB]).then_inc(s["cols_sb"], 1)
            dve.wait_ge(s["cols_sb"], 1)
            dve.wait_ge(s["cond_done"], 3)
            link(dve.tensor_scalar(cond[:, :, :], cond[:, :, :], 1.0, None, ALU.add))
            link(dve.reciprocal(cond[:, :, :], cond[:, :, :]))
            for q, c0 in enumerate((A_CTX, A_C)):
                dve.tensor_tensor(cond[:, :, q], cond[:, :, q], cols[:, c0:c0 + KD], ALU.mult).then_inc(s["cond_done"], 1)
            dve.wait_ge(s["zeroed"], 3)
            dve.wait_ge(s["cond_done"], 5)
            dve.tensor_copy(cond32[:, :, 0:2], cond[:, :, :]).then_inc(s["cond_done"], 1)
            dve.tensor_scalar(bga[:, :], cols[:, NA + B_BA:NA + B_BA + 16], 0.5, None, ALU.mult).then_inc(s["cond_done"], 1)
            z, w, w2, acc = spl[:, 1, :], spl[:, 2, :], spl[:, 3, :], spl[:, 4, :]
            link(dve.tensor_scalar(w, z, 2.0, None, ALU.add))
            link(dve.reciprocal(w, w))
            link(dve.tensor_tensor(w, w, z, ALU.mult))
            link(dve.tensor_tensor(w2, w, w, ALU.mult))
            link(dve.tensor_scalar(acc, w2, 1.0 / 17, 1.0 / 15, ALU.mult, ALU.add))
            for n in (13, 11, 9, 7, 5, 3, 1):
                link(dve.tensor_tensor(acc, acc, w2, ALU.mult))
                link(dve.tensor_scalar(acc, acc, 1.0 / n, None, ALU.add))
            link(dve.tensor_tensor(acc, acc, w, ALU.mult))
            link(dve.tensor_scalar(w, cols[:, NA + B_LAM:NA + B_LAM + 8], -1.0, 0.0, ALU.mult, ALU.max))
            link(dve.scalar_tensor_tensor(out=acc, in0=acc, scalar=2.0, in1=w, op0=ALU.mult, op1=ALU.add))
            dve.tensor_scalar(spl[:, 5, :], acc, -4.0, None, ALU.mult).then_inc(s["cond_done"], 1)

            for i in range(NT):
                dve.wait_ge(s["x_in"], 16 * NT)
                if i > 0:
                    dve.wait_ge(s["xn_pool"], i)
                norm_stats(xn[:, i, :], stat[:, i, :])
                dve.tensor_scalar(xn[:, i, :], xn[:, i, :], stat[:, i, 12:13], stat[:, i, 13:14],
                                  ALU.subtract, ALU.mult).then_inc(s["ln_xhat"], 1)

            def mod_out(n):
                c0 = ada_order[n // 2] * KD + 4 * (n % 2)
                dve.wait_ge(s["modT_ps"], next(g for g in ADA_GROUPS if g > n))
                dve.tensor_tensor(modT[:, c0:c0 + 4, :], PS[:, 7, 2 * c0:2 * c0 + 8].rearrange("p (n s) -> p n s", s=2),
                                  cols[:, A_BADA + c0:A_BADA + c0 + 4].unsqueeze(2).broadcast_to([P, 4, 2]),
                                  ALU.add).then_inc(s["mod_sb"], 1)

            for n in range(4):
                mod_out(n)
            dve.wait_ge(s["mod_sb"], 4)
            sc1 = cmod[:, 0]
            sh1 = cmod[:, 1]
            gcol = cols[:, A_LNG:A_LNG + KD].unsqueeze(2).broadcast_to([P, KD, 2])
            bcol = cols[:, A_LNB:A_LNB + KD].unsqueeze(2).broadcast_to([P, KD, 2])
            link(dve.tensor_scalar(sc1, modT[:, SC1 * KD:SC1 * KD + KD, :], 1.0, None, ALU.add))
            link(dve.tensor_tensor(sh1, sc1, bcol, ALU.mult))
            link(dve.tensor_tensor(sh1, sh1, modT[:, SH1 * KD:SH1 * KD + KD, :], ALU.add))
            link(dve.tensor_tensor(sc1, sc1, gcol, ALU.mult))
            dve.wait_ge(s["xT_sb"], 6)
            for k in range(KD):
                for q, (c0, n) in enumerate(SEG):
                    last = dve.tensor_scalar(hT[:, k, c0:c0 + n], hT[:, k, c0:c0 + n], cmod[:, 0, k, q:q + 1],
                                             cmod[:, 1, k, q:q + 1], ALU.mult, ALU.add)
                last.then_inc(s["h_done"], 1)

            dve.wait_ge(s["zeroed"], 3)
            for c in range(CR):
                dve.wait_ge(s["win_sb"], c + 1)
                for k in range(4):
                    cw = cols[:, A_CW + 4 * k + c:A_CW + 4 * k + c + 1]
                    if k == 0:
                        link(dve.tensor_scalar(xc[:, c, :], xpad[:, c, 0:W], cw, cols[:, A_CB + c:A_CB + c + 1],
                                               ALU.mult, ALU.add))
                    elif k < 3:
                        link(dve.scalar_tensor_tensor(out=xc[:, c, :], in0=xpad[:, c, k:k + W], scalar=cw,
                                                      in1=xc[:, c, :], op0=ALU.mult, op1=ALU.add))
                    else:
                        dve.scalar_tensor_tensor(out=xc[:, c, :], in0=xpad[:, c, k:k + W], scalar=cw,
                                                 in1=xc[:, c, :], op0=ALU.mult, op1=ALU.add).then_inc(s["conv_done"], 1)
            for b in range(2):
                for it in range(4 * b, 4 * b + 4):
                    v_, e_ = gtmp[:, 2, it % 4], rtmp[:, it % 2]
                    dve.wait_ge(s["sq_done"], it + 1)
                    link(dve.tensor_scalar(e_, e_, 1.0, None, ALU.add))
                    dve.scalar_tensor_tensor(out=v_, in0=v_, scalar=0.0, in1=e_, op0=ALU.min, op1=ALU.mult)\
                        .then_inc(s["rec_v"], 1)
                dve.wait_ge(s["mult_done"], b + 1)
                dve.wait_ge(s["q_done"], 4 * b + 4)
                link(dve.scalar_tensor_tensor(out=gtmp[:, 1], in0=gtmp[:, 2], scalar=0.5, in1=gtmp[:, 1],
                                              op0=ALU.mult, op1=ALU.mult))
                for it in range(4 * b, 4 * b + 4):
                    c, d = it // 2, it % 2
                    for n, (c0, m) in enumerate(SEG):
                        st = cols[:, NA + B_ST + 4 * d + c:NA + B_ST + 4 * d + c + 1] if n else 0.0
                        a_, b_, h_ = (v[:, c0:c0 + m] for v in (gtmp[:, 0, it % 4], gtmp[:, 1, it % 4], hfb[:, d]))
                        if d:
                            a_, b_, h_ = a_[:, ::-1], b_[:, ::-1], h_[:, ::-1]
                        sc_ = dve.tensor_tensor_scan(h_, a_, b_, st, ALU.mult, ALU.add)
                        if n == 0:
                            step(sc_)
                    sc_.then_inc(s["scan_done"], 1)
                    dve.wait_ge(s["scan_done"], it + 1)
                    dve.wait_ge(s["dve_step"], n_step[0])
                    edge = 0 if d else SEQ - 1
                    dve.tensor_copy(stin[:, 4 * d + c:4 * d + c + 1], hfb[:, d, edge:edge + 1]).then_inc(s["state_done"], 1)
                    if d:
                        for c0, m in SEG:
                            link(dve.tensor_tensor(xc[:, c, c0:c0 + m], hfb[:, 0, c0:c0 + m], hfb[:, 1, c0:c0 + m],
                                                   ALU.add))
                    dve.wait_ge(s["state_done"], it + 1)

            for g in range(FG):
                dve.wait_ge(s["f_ps"], g + 1)
                if g >= 2:
                    dve.wait_ge(s["yf_ps"], g - 1)
                dve.tensor_copy(FTs[:, g % 2, :], PS[:, 4, 0:TOK]).then_inc(s["f_sb"], 1)
                dve.wait_ge(s["yf_ps"], g + 1)
                dve.tensor_scalar(yfs[:, g, :], PS[:, 5, 0:TOK], cols[:, NA + B_FB + g:NA + B_FB + g + 1], None,
                                  ALU.add).then_inc(s["yf_sb"], 1)
            dve.wait_ge(s["p1_used"], 7)
            for c in range(CR):
                dve.wait_ge(s["gelu_done"], c + 1)
                for (c0, m), (k0, _) in zip(SEG, SEGC):
                    step(dve.scalar_tensor_tensor(out=mixT[:, c, k0:k0 + m], in0=xc[:, c, c0:c0 + m],
                                                  scalar=0.5, in1=gr[:, c, c0:c0 + m], op0=ALU.mult, op1=ALU.mult))
                dve.wait_ge(s["dve_step"], n_step[0])
                dve.nop().then_inc(s["yr_done"], 1)
            for n in range(4, 10):
                mod_out(n)
            dve.wait_ge(s["mod_sb"], 10)
            sc2 = modT[:, SC2 * KD:SC2 * KD + KD, :]
            sh2 = modT[:, SH2 * KD:SH2 * KD + KD, :]
            g1col = cols[:, A_L1G:A_L1G + KD].unsqueeze(2).broadcast_to([P, KD, 2])
            b1col = cols[:, A_L1B:A_L1B + KD].unsqueeze(2).broadcast_to([P, KD, 2])
            link(dve.tensor_scalar(sc2, sc2, 1.0, None, ALU.add))
            link(dve.tensor_tensor(cmod[:, 1], sc2, b1col, ALU.mult))
            link(dve.tensor_tensor(sh2, sh2, cmod[:, 1], ALU.add))
            dve.tensor_tensor(sc2, sc2, g1col, ALU.mult).then_inc(s["mod2_done"], 1)

            dve.wait_ge(s["row_sb"], 2)
            dve.wait_ge(s["xn_done"], NT)

            def low_parts():
                for i in range(NT):
                    dve.wait_ge(s["h2b1"], i + 1)
                    dve.wait_ge(s["h2T_ps"], i + 1)
                    dve.wait_ge(s["h2_done"], i + 1)
                    dve.tensor_tensor(tts[i], tts[i], h2b[:, 0, i, :], ALU.subtract).then_inc(s["h2r"], 1)
                for i in range(NT):
                    dve.wait_ge(s["h2b2"], i + 1)
                    dve.wait_ge(s["h2r"], i + 1)
                    dve.tensor_tensor(h2b[:, 2, i, :], tts[i], h2b[:, 1, i, :], ALU.subtract).then_inc(s["h2b3"], 1)

            for i in range(NT):
                if i < NT - 1:
                    dve.wait_ge(s["mix_ps"], i + 1)
                else:
                    dve.wait_ge(s["p1_used"], 15)
                x, m = xn[:, i, :], tts[i]
                link(dve.tensor_tensor(m, PS[:, 2 * i:2 * i + 2, :].rearrange("p a n -> p (a n)"),
                                       rows[:, 1 if i else 0, :], ALU.mult))
                link(dve.scalar_tensor_tensor(out=x, in0=x, scalar=ALPHA, in1=m, op0=ALU.mult, op1=ALU.add))
                norm_var(x, stat[:, i, :])
                q = 1 if i else 0
                if i == 0:
                    dve.wait_ge(s["row_sb"], 6)
                step(dve.scalar_tensor_tensor(out=m, in0=x, scalar=stat[:, i, 12:13], in1=rows[:, 2 + q, :],
                                              op0=ALU.subtract, op1=ALU.mult))
                norm_root(stat[:, i, :])
                dve.scalar_tensor_tensor(out=m, in0=m, scalar=stat[:, i, 13:14], in1=rows[:, 4 + q, :],
                                         op0=ALU.mult, op1=ALU.add).then_inc(s["h2_done"], 1)
                dve.tensor_scalar(x, x, stat[:, i, 12:13], stat[:, i, 13:14], ALU.subtract, ALU.mult)\
                    .then_inc(s["x1n"], 1)
            for n in range(10, 12):
                mod_out(n)
            low_parts()

            dve.wait_ge(s["lg_ps"], 1)
            dve.wait_ge(s["rtr_in"], 64)
            link(dve.tensor_tensor(lg[:, :, :], PS[:, 0, 0:NT * 20].rearrange("p (i n) -> p i n", n=20),
                                   rb[:, :].unsqueeze(1).broadcast_to([P, NT, 20]), ALU.add))
            gl, el = lg[:, :, 0:NG], lg[:, :, NG:]

            def wide(v, n):
                return v.unsqueeze(2).broadcast_to([P, NT, n])

            def first_max(x, n, code, oh, mx, tmp):
                link(dve.tensor_reduce(mx, x, AX.X, ALU.max))
                link(dve.tensor_tensor(tmp, x, wide(mx, n), ALU.is_equal))
                cd = cst[:, code:code + n].unsqueeze(1).broadcast_to([P, NT, n])
                link(dve.tensor_tensor(tmp, tmp, cd, ALU.mult))
                link(dve.tensor_reduce(rs[:, 11, :], tmp, AX.X, ALU.max))
                link(dve.tensor_tensor(oh, cd, wide(rs[:, 11, :], n), ALU.is_equal))

            dve.wait_ge(s["st_ps"], 1)
            dve.tensor_copy(strow[0:8, :], PS[0:8, 2, 128:256]).then_inc(s["st_row"], 1)

            og, oh1, oh2, asg = rt[:, 0, :, 0:NG], rt[:, 1], rt[:, 2], marks16[:, :, :]
            first_max(gl, NG, C_COD4, og, rs[:, 0, :], rt[:, 4, :, 0:NG])
            link(dve.tensor_tensor(rt[:, 5, :, 0:NG], gl, wide(rs[:, 0, :], NG), ALU.subtract))
            marks = og.unsqueeze(3).broadcast_to([P, NT, NG, EPG])
            m4 = rt[:, 4].rearrange("p i (g e) -> p i g e", e=EPG)
            link(dve.tensor_copy(m4, marks))
            link(dve.tensor_tensor(rt[:, 7], el, rt[:, 4], ALU.mult))
            link(dve.tensor_scalar(rt[:, 4], rt[:, 4], -1.0, 1e30, ALU.add, ALU.mult))
            link(dve.tensor_tensor(rt[:, 7], rt[:, 7], rt[:, 4], ALU.add))
            first_max(rt[:, 7], NE, C_COD16, oh1, rs[:, 1, :], rt[:, 4])
            link(dve.scalar_tensor_tensor(out=rt[:, 7], in0=oh1, scalar=-2e30, in1=rt[:, 7], op0=ALU.mult, op1=ALU.add))
            first_max(rt[:, 7], NE, C_COD16, oh2, rs[:, 2, :], rt[:, 4])
            link(dve.tensor_tensor(asg, oh1, oh2, ALU.add))
            dve.tensor_tensor(rs[:, 4, :], rs[:, 2, :], rs[:, 1, :], ALU.subtract).then_inc(s["assign_done"], 1)
            dve.wait_ge(s["pos_pool"], 2)
            link(dve.tensor_reduce(rs[:, 6, :], rt[:, 6, :, 0:NG], AX.X, ALU.add))
            link(dve.tensor_scalar(rs[:, 7, :], rs[:, 5, :], 1.0, None, ALU.add))
            link(dve.tensor_tensor(rs[:, 6, :], rs[:, 6, :], rs[:, 7, :], ALU.mult))
            link(dve.reciprocal(wk[:, 0, :], rs[:, 6, :]))
            link(dve.tensor_tensor(wk[:, 1, :], wk[:, 0, :], rs[:, 5, :], ALU.mult))
            erow = cst[:, C_EROW:C_EROW + NE].unsqueeze(1).broadcast_to([P, NT, NE])

            def chosen(k, v):
                for q, oh in enumerate((oh1, oh2)):
                    link(dve.tensor_tensor(rt[:, 4], v, oh, ALU.mult))
                    link(dve.tensor_reduce(posf[:, k, q * NT:(q + 1) * NT], rt[:, 4], AX.X, ALU.add))

            chosen(1, erow)
            dve.wait_ge(s["rank_ps"], 1)
            rank = rt[:, 7]
            step(dve.tensor_copy(rank, PS[:, 1, 0:NT * NE].rearrange("p (i e) -> p i e", e=NE)))
            link(dve.tensor_reduce(small[:, 0:1], PS[:, 1, NT * NE:(NT + 1) * NE], AX.X, ALU.max))
            step(dve.tensor_copy(cnt[:, 1:1 + NE], PS[:, 1, NT * NE:(NT + 1) * NE]))
            link(dve.scalar_tensor_tensor(out=rt[:, 4], in0=rank, scalar=1.0, in1=asg, op0=ALU.add, op1=ALU.mult))
            link(dve.tensor_scalar(rankA[:, 0:NE, :].rearrange("p e i -> p i e"), rt[:, 4], -1.0, None, ALU.add))
            dve.tensor_copy(cnt[:, 0:1], small[:, 0:1]).then_inc(s["route_done"], 1)

            def positions():
                chosen(0, rank)

                def every(v):
                    return v.unsqueeze(1).broadcast_to([P, PASSES, 2 * NT])

                r, b = posw[:, 0], posw[:, 1]
                link(dve.tensor_tensor(r, every(posf[:, 0]), cst[:, C_PASS:C_PASS + PASSES].unsqueeze(2)
                                       .broadcast_to([P, PASSES, 2 * NT]), ALU.subtract))
                link(dve.tensor_scalar(b, r, 0.0, FAR, ALU.is_lt, ALU.mult))
                link(dve.tensor_tensor(b, b, r, ALU.add))
                link(dve.tensor_tensor(b, b, every(posf[:, 1]), ALU.add))
                link(dve.tensor_scalar(r, r, CAP - 0.5, FAR, ALU.is_gt, ALU.mult))
                link(dve.tensor_tensor(b, b, r, ALU.add))
                dve.tensor_copy(posn[:, :, :, :].rearrange("p a q i -> p a (q i)"), b).then_inc(s["route_done"], 1)

            def split_lo(ge, p, j, hs=(0, 1)):
                for h in hs:
                    a, b = h * UNIT // 2, (h + 1) * UNIT // 2
                    dve.wait_ge(s["hi_done"], ge * 6 + (2 * j + h + 1))
                    dve.tensor_tensor(wlo[3 * p + j][:, a:b], ring[3 * p + j][:, a:b], whi[j][:, a:b].bitcast(F32),
                                      ALU.subtract).then_inc(s["lo_done"], 1)

            def x_lo(ge, n):
                def rest(dst, src, high):
                    dve.wait_ge(s["xs_hi"], ge + 1)
                    need(dve, "unit_used", ge * 3 - 1)
                    dve.tensor_tensor(dst, src, high.bitcast(F32), ALU.subtract).then_inc(s["xs_ready"], 1)

                fork(dve, n,
                     lambda: rest(xsH[:, :, HALF:CAP], PS[:, 0, :].rearrange("p (k n) -> p k n", n=HALF),
                                  xsH[:, :, 0:HALF]),
                     lambda: rest(xsL[:, :, :], PS[:, 0:2, :].rearrange("p a (k n) -> p (a k) n", n=CAP),
                                  xsH[:, :, :]))

            def choose(ge, e, pb):
                need(dve, "x_disp", ge)
                i0 = cst[:, bass.ds(pb * CAP + C_IOTA, CAP)] if not isinstance(pb, int) else \
                    cst[:, C_IOTA + pb * CAP:C_IOTA + (pb + 1) * CAP]
                ra = rankA[:, bass.ds(e, 1), :].rearrange("p a i -> p (a i)") if not isinstance(e, int) else rankA[:, e, :]
                dve.tensor_tensor(sel[:, :, :], i0.unsqueeze(1).broadcast_to([P, NT, CAP]),
                                   ra.unsqueeze(2).broadcast_to([P, NT, CAP]), ALU.is_equal).then_inc(s["sel_ready"], 1)

            def prologue(ge, pb):
                if isinstance(ge, int):
                    dve.wait_ge(s["route_done"], 1)
                choose(ge, 0, pb)
                if isinstance(ge, int):
                    positions()
                n = tokens_of(dve, 0, pb)
                split_lo(ge, 0, 0)
                x_lo(ge, n)
                split_lo(ge, 0, 1)
                split_lo(ge, 0, 2, (0,))

            def body(ge, e, q, p, last, pb):
                n = tokens_of(dve, e, pb)
                n1 = None if last else tokens_of(dve, e + 1, pb)

                def up_few():
                    dve.wait_ge(s["unit_used"], ge * 3 + 2)
                    need(dve, "ht_ps", ge)
                    dve.tensor_copy(hid[:, :], PS[:, 3, :]).then_inc(s["u_done"], 1)

                def up_many():
                    dve.wait_ge(s["unit_used"], ge * 3 + 2)
                    dve.wait_ge(s["g_done"], ge + 1)
                    need(dve, "ht_ps", ge)
                    dve.scalar_tensor_tensor(out=hid[:, :], in0=sg[:, :], scalar=1.0, in1=PS[:, 2, :], op0=ALU.add,
                                             op1=ALU.mult).then_inc(s["silu_done"], 1)
                    dve.wait_ge(s["silu_done"], ge + 1)
                    dve.scalar_tensor_tensor(out=hid[:, :], in0=hid[:, :], scalar=0.5, in1=PS[:, 3, :], op0=ALU.mult,
                                             op1=ALU.mult).then_inc(s["u_done"], 1)

                def hidden_few():
                    dve.wait_ge(s["ht_act"], ge + 1)
                    dve.scalar_tensor_tensor(out=hidT[:, :, :], in0=sgT[:, :, :], scalar=1.0,
                                             in1=PS[:, 4, 0:KF * HALF].rearrange("p (k n) -> p k n", n=HALF),
                                             op0=ALU.add, op1=ALU.mult).then_inc(s["silu_done"], 1)
                    dve.wait_ge(s["silu_done"], ge + 1)
                    dve.scalar_tensor_tensor(out=hidT[:, :, :], in0=hidT[:, :, :], scalar=0.5,
                                             in1=PS[:, 7, 0:KF * HALF].rearrange("p (k n) -> p k n", n=HALF),
                                             op0=ALU.mult, op1=ALU.mult).then_inc(s["hid_done"], 1)
                    dve.wait_ge(s["hid_done"], ge + 1)
                    dve.tensor_copy(hTH[:, :, 0:HALF], hidT[:, :, :]).then_inc(s["hth_done"], 1)
                    dve.wait_ge(s["hth_done"], ge + 1)
                    dve.tensor_tensor(hTH[:, :, HALF:CAP], hidT[:, :, :], hTH[:, :, 0:HALF].bitcast(F32), ALU.subtract)\
                        .then_inc(s["hts_ready"], 1)

                def hidden_many():
                    dve.nop().then_inc(s["hid_done"], 1)
                    dve.nop().then_inc(s["hth_done"], 1)
                    dve.wait_ge(s["ht_act"], ge + 1)
                    dve.tensor_tensor(hTL[:, :, :], PS[:, 4, :].rearrange("p (k n) -> p k n", n=CAP),
                                      hTH[:, :, :].bitcast(F32), ALU.subtract).then_inc(s["hts_ready"], 1)

                if not last:
                    choose(ge + 1, e + 1, pb)
                fork(dve, n, up_few, up_many)
                if not last:
                    split_lo(ge + 1, 1 - p, 0, (0,))
                fork(dve, n, hidden_few, hidden_many)
                if not last:
                    split_lo(ge + 1, 1 - p, 0, (1,))
                    x_lo(ge + 1, n1)
                    split_lo(ge + 1, 1 - p, 1)
                    split_lo(ge + 1, 1 - p, 2, (0,))

            passes(dve, lambda pb: pairs(dve, lambda ge: prologue(ge, pb), lambda *a: body(*a, pb), pb))

            dve.nop().then_inc(s["banks_free"], 1)

            def residual(i):
                dve.wait_ge(s["fin_y1"], i + 1)
                m = fin[:, i, :]
                link(dve.scalar_tensor_tensor(out=m, in0=y12[:, 1, i, :], scalar=wk[:, 1, i:i + 1], in1=m,
                                              op0=ALU.mult, op1=ALU.add))
                b = 2 if i else 0
                if i == 0:
                    dve.wait_ge(s["g2_ps"], 1)
                link(dve.tensor_tensor(m, m, PS[:, b:b + 2, :].rearrange("p a n -> p (a n)"), ALU.mult))
                link(dve.scalar_tensor_tensor(out=m, in0=xn[:, i, :], scalar=ALPHA, in1=m, op0=ALU.mult, op1=ALU.add))
                norm_var(m, stat[:, i, :])

            def spread(i):
                st = stat[:, i, :]
                norm_root(st)
                dve.scalar_tensor_tensor(out=st[:, 14:15], in0=st[:, 12:13], scalar=-1.0, in1=st[:, 13:14],
                                         op0=ALU.mult, op1=ALU.mult).then_inc(s["fin_stat"], 1)

            def scale(i):
                dve.wait_ge(s["fin_norm"], i + 1)
                dve.wait_ge(s["ln2_in"], 32)
                dve.tensor_tensor(fin[:, i, :], fin[:, i, :], ln2[:, 0, :], ALU.mult).then_inc(s["fin_mul"], 1)

            residual(0)
            residual(1)
            spread(0)
            residual(2)
            scale(0)
            spread(1)
            scale(1)
            spread(2)
            scale(2)
            dve.wait_ge(s["fin_mul"], NT)
            dve.tensor_tensor(fin[:, 2, :], fin[:, 2, :], ln2[:, 1, :], ALU.add).then_inc(s["fin_last"], 1)

        @block.gpsimd
        def _(pool):
            n_step = [0]

            def link(ins):
                n_step[0] += 1
                ins.then_inc(s["pool_step"], 1)
                pool.wait_ge(s["pool_step"], n_step[0])

            pool.memset(wbd[:, :, :], 0.0).then_inc(s["zeroed"], 1)
            pool.memset(cond32[:, :, :], 0.0).then_inc(s["zeroed"], 1)
            pool.memset(ylow[:, :], 0.0)
            pool.memset(rankA[:, NE:NE + 1, :], -1.0)
            pool.memset(xpad[:, :, 0:2], 0.0)
            pool.memset(xpad[:, :, 2 + W:XW], 0.0)
            pool.memset(hT[:, :, SEQ:SEQ + 3], 0.0)
            pool.memset(hT[:, :, W - 1:W], 0.0).then_inc(s["zeroed"], 1)
            pool.wait_ge(s["x_in"], 16 * NT)
            pool.wait_ge(s["pos_in"], 16)
            for i in range(1, NT):
                pool.tensor_tensor(xn[:, i, :], xn[:, i, :], pos[:, i - 1, :], ALU.add).then_inc(s["xn_pool"], 1)
            pool.wait_ge(s["lnin_in"], 32)
            pool.wait_ge(s["xT_ps"], 6)
            for i in range(NT):
                link(pool.tensor_tensor(xn[:, i, :], xn[:, i, :], lnin[:, 0, :], ALU.mult))
                pool.tensor_tensor(xn[:, i, :], xn[:, i, :], lnin[:, 1, :], ALU.add).then_inc(s["xn_done"], 1)

            pool.wait_ge(s["p1_used"], 5)
            pool.dma_start(Y_dram[0].rearrange("(e r) d -> r e d", r=CAP)[HALF:CAP],
                           ylow[:, :].unsqueeze(1).broadcast_to([HALF, NE, D])).then_inc(s["y_zeroed"], 16)

            def q_item(it):
                pool.wait_ge(s["gate_act"], it + 1)
                g = gtmp[:, 1, it % 4]
                link(pool.tensor_scalar(g, g, 1.0, None, ALU.add))
                pool.tensor_tensor(g, g, xc[:, it // 2, :], ALU.mult).then_inc(s["q_done"], 1)

            pool.wait_ge(s["conv_done"], CR)
            for it in range(8):
                q_item(it)
            for c in range(CR):
                tg, g = xpad[:, c, 0:W], gr[:, c, :]
                pool.wait_ge(s["win_sb"], 8 + c + 1)
                link(pool.tensor_tensor(tg, g, g, ALU.mult))
                link(pool.tensor_scalar(tg, tg, 0.044715, 1.0, ALU.mult, ALU.add))
                pool.tensor_tensor(tg, tg, g, ALU.mult).then_inc(s["gelu_t"], 1)
                pool.wait_ge(s["gelu_th"], c + 1)
                link(pool.tensor_scalar(tg, tg, 1.0, None, ALU.add))
                pool.tensor_tensor(g, g, tg, ALU.mult).then_inc(s["gelu_done"], 1)

            pool.wait_ge(s["y_zeroed"], 16)
            pool.dma_start(wr[:, :, 0:NG], t["router_g_w"][0].rearrange("(k p) n -> p k n", p=P)).then_inc(s["rtr_in"], 16)
            pool.dma_start(wr[:, :, NG:], t["router_e_w"][0].rearrange("(k p) n -> p k n", p=P)).then_inc(s["rtr_in"], 16)
            pool.dma_start(rb[:, 0:NG], t["router_g_b"].partition_broadcast(P)).then_inc(s["rtr_in"], 16)
            pool.dma_start(rb[:, NG:], t["router_e_b"].partition_broadcast(P)).then_inc(s["rtr_in"], 16)

            pool.wait_ge(s["ln1_in"], 32)
            for i in range(NT):
                pool.wait_ge(s["x1n"], i + 1)
                link(pool.tensor_tensor(xn[:, i, :], xn[:, i, :], rows[:, 6, :], ALU.mult))
                pool.tensor_tensor(xn[:, i, :], xn[:, i, :], rows[:, 7, :], ALU.add).then_inc(s["x1_done"], 1)

            pool.wait_ge(s["st_row"], 1)
            pool.dma_start(t["new_state"], strow[0:2 * CR, :]).then_inc(s["st_out"], 16)
            pool.wait_ge(s["st_out"], 16)

            pool.wait_ge(s["route_done"], 2)

            def split_lo_down(ge, p):
                pool.wait_ge(s["hi_done"], ge * 6 + 6)
                pool.tensor_tensor(wlo[3 * p + 2][:, UNIT // 2:], ring[3 * p + 2][:, UNIT // 2:],
                                   whi[2][:, UNIT // 2:].bitcast(F32), ALU.subtract).then_inc(s["lo_pool"], 1)

            def run(pb):
                def body(ge, e, q, p, last):
                    n = tokens_of(pool, e, pb)
                    if not last:
                        split_lo_down(ge + 1, 1 - p)

                    def few():
                        pool.wait_ge(s["y_sb"], ge + 1)
                        pool.tensor_tensor(ysb[0:HALF, :], ysb[0:HALF, :], ylow[:, :], ALU.add).then_inc(s["y_sum"], 1)
                        pool.wait_ge(s["y_sum"], ge + 1)
                        pool.dma_start(Y_dram[pb][bass.ds(e * CAP, HALF)], ysb[0:HALF, :]).then_inc(s["y_stored"], 16)

                    def many():
                        pool.nop().then_inc(s["y_sum"], 1)
                        pool.wait_ge(s["y_sb"], ge + 1)
                        pool.dma_start(Y_dram[pb][bass.ds(e * CAP, CAP)], ysb[:, :]).then_inc(s["y_stored"], 16)

                    fork(pool, n, few, many)

                pairs(pool, lambda ge: split_lo_down(ge, 0), body, pb)
                pool.wait_ge(s["y_stored"], pb * (16 * NE) + 16 * NE)

            run(0)
            most = pool.value_load(cnt[0:1, 0:1], min_val=0, max_val=TOK)
            for pb in range(1, PASSES):
                with pool.If(most > pb * CAP):
                    run(pb)
            pool.nop().then_inc(s["passes_done"], 1)

            def gather(pb, i):
                for q in range(2):
                    pool.indirect_dma_start(
                        out=y12[:, q, i, :], out_offset=None, in_=Y_dram[pb],
                        in_offset=bass.IndirectOffsetOnAxis(ap=posn[:, pb, q, i:i + 1], axis=0),
                        bounds_check=YROWS - 1, oob_is_err=False,
                    ).then_inc(gathered_in[pb][i], 16)

            for i in range(NT):
                gather(0, i)
                for pb in range(1, PASSES):
                    with pool.If(most > pb * CAP):
                        pool.wait_ge(gathered_in[pb - 1][i], 32)
                        gather(pb, i)
                        pool.wait_ge(gathered_in[pb][i], 32)
                pool.nop().then_inc(s["gathered"], 1)

            pool.wait_ge(s["ln2_in"], 32)
            for i in range(NT - 1):
                pool.wait_ge(s["fin_mul"], i + 1)
                pool.tensor_tensor(fin[:, i, :], fin[:, i, :], ln2[:, 1, :], ALU.add).then_inc(s["fin_done"], 1)

        @block.tensor
        def _(pe):
            ident = cst[:, C_ID:C_ID + P]

            pe.wait_ge(s["const_in"], 16)
            pe.wait_ge(s["rowA_in"], 16 * 9)
            pe.transpose(PS[:, 0, 0:NA], rowA[0:NA, :], cst[0:NA, C_ID:C_ID + NA])
            pe.wait_ge(s["rowB_in"], 16 * 5)
            pe.transpose(PS[:, 0, NA:NA + NB], rowB[0:NB, :], cst[0:NB, C_ID:C_ID + NB]).then_inc(s["cols_ps"], 1)

            def ada_sums(n, u):
                p1_loaded(pe, u)
                w = unit3(ring[(u + 1) % RING])
                if n == 3:
                    pe.wait_ge(s["xT_sb"], 6)
                if n >= 2:
                    pe.wait_ge(s["mrow_sb"], n - 1 if n < 10 else n)
                for k in range(KD):
                    j = k % 4
                    mm = pe.matmul(PS[32 * j:32 * j + 32, ABANK[n], :], cond32[:, k, :], w[:, k, :],
                                   start=(k < 4), stop=(k >= 4))
                mm.then_inc(s["p1_used"], 1)

            def ada_cols(n):
                c0 = ada_order[n // 2] * KD + 4 * (n % 2)
                if n in ADA_GROUPS:
                    pe.wait_ge(s["mod_sb"], n)
                pe.wait_ge(s["mrow_sb"], n + 1)
                for q in range(4):
                    mm = pe.matmul(PS[:, 7, 2 * (c0 + q):2 * (c0 + q) + 2], mrow[:, q * P:(q + 1) * P],
                                   cst[:, C_SUM:C_SUM + 2], start=True, stop=True)
                mm.then_inc(s["modT_ps"], 1)

            pe.wait_ge(s["cond_done"], 6)
            ada_sums(0, 0)
            ada_sums(1, 1)
            ada_cols(0)
            ada_cols(1)
            for i in range(NT):
                pe.wait_ge(s["ln_xhat"], i + 1)
                if i == 0:
                    pe.wait_ge(s["cols_sb"], 1)
                if i == 2:
                    pe.wait_ge(s["mrow_sb"], 2)
                for k in range(KD):
                    mm = pe.transpose(PS[:, 2 * i + k // 4, (k % 4) * P:(k % 4 + 1) * P], xn[:, i, k * P:(k + 1) * P], ident)
                    if k % 4 == 3:
                        mm.then_inc(s["xT_ps"], 1)
            ada_sums(2, 2)
            ada_sums(3, 3)
            ada_cols(2)
            ada_cols(3)

            def gate(it):
                c, d = it // 2, it % 2
                pe.wait_ge(s["conv_done"], c + 1)
                if it == 0:
                    pe.wait_ge(s["wbd_in"], 64)
                    pe.wait_ge(s["mrow_sb"], 4)
                else:
                    pe.wait_ge(s["gate_act"], it)
                for gi in range(2):
                    mm = pe.matmul(PS[:, 4 + gi, 0:W], wbd[:, 8 * gi + 4 * d + c, :], xc[:, c, :],
                                   start=True, stop=True)
                mm.then_inc(s["gate_ps"], 1)

            def project(w):
                if w % 4 == 0:
                    p1_loaded(pe, 4 + w // 4)
                if w < 4:
                    pe.wait_ge(s["xT_sb"], 6)
                else:
                    pe.wait_ge(s["win_sb"], w - 3)
                wt = unit3(ring[(5 + w // 4) % RING])
                for k in range(KD):
                    if w == 0:
                        pe.wait_ge(s["h_done"], k + 1)
                    mm = pe.matmul(PS[:, w % 4, 0:W], wt[:, k, (w % 4) * P:(w % 4 + 1) * P], hT[:, k, :],
                                   start=(k == 0), stop=(k == KD - 1))
                    if k == KD // 2 - 1 and w in GATE_WITHIN:
                        gate(GATE_WITHIN[w])
                mm.then_inc(s["p1_used" if w % 4 == 3 else "win_ps"], 1)

            def chan_dft(g):
                pe.wait_ge(s["win_sb"], 4 + g + 1)
                if g == 0:
                    pe.wait_ge(s["smallw_in"], 32)
                    pe.wait_ge(s["mod_sb"], 4)
                    pe.wait_ge(s["mrow_sb"], 4)
                else:
                    pe.wait_ge(s["z_sb"], g)
                for i in range(NT):
                    out = PS[:, 6, i * 256:(i + 1) * 256] if i < 2 else PS[:, 7, 0:256]
                    mm = pe.matmul(out, xf[:, g, TC[i]:TC[i] + P], dft[:, F_CH:F_CH + 256], start=True, stop=True)
                mm.then_inc(s["z_ps"], 1)

            def pos_dft(g):
                pe.wait_ge(s["z_sb"], g + 1)
                if g == 0:
                    pe.wait_ge(s["gate_act"], 8)
                need(pe, "f_sb", g)
                z = Z[:, g % 2]
                for h in range(2):
                    pe.matmul(PS[:, 4, 0:SEQ], z[:, 0, h * P:(h + 1) * P], dft[:, F_CTX + h * P:F_CTX + (h + 1) * P],
                              start=(h == 0), stop=(h == 1))
                for m in range(2):
                    for h in range(2):
                        mm = pe.matmul(PS[:, 4, SEQ:TOK], z[:, 1 + m, h * P:(h + 1) * P],
                                       dft[:, F_LAT + 512 * m + 256 * h:F_LAT + 512 * m + 256 * (h + 1)],
                                       start=(m == 0 and h == 0), stop=(m == 1 and h == 1))
                mm.then_inc(s["f_ps"], 1)

            def fourier_out(g):
                pe.wait_ge(s["f_sb"], g + 1)
                need(pe, "yf_sb", g)
                pe.matmul(PS[:, 5, 0:TOK], fnw[:, g, :], FTs[:, g % 2, :], start=True, stop=True).then_inc(s["yf_ps"], 1)

            for w in range(12):
                project(w)
                if w in GATE_AFTER:
                    gate(GATE_AFTER[w])
                if w > 8:
                    pos_dft(w - 9)
                if w >= 8:
                    chan_dft(w - 8)
                if w > 9:
                    fourier_out(w - 10)
            pos_dft(FG - 1)
            pe.wait_ge(s["z_sb"], FG)
            ada_sums(4, 7)
            fourier_out(FG - 2)
            ada_cols(4)
            fourier_out(FG - 1)
            pe.wait_ge(s["f_sb"], FG)
            ada_sums(5, 8)
            for n in range(5, 10):
                if n < 9:
                    ada_sums(n + 1, n + 4)
                ada_cols(n)

            def row(r, j, q):
                if r > 0:
                    pe.wait_ge(s["row_sb"], r)
                else:
                    pe.wait_ge(s["mod_sb"], 10)
                if r == 2:
                    pe.wait_ge(s["mod2_done"], 1)
                for k in range(KD):
                    mm = pe.matmul(PS[:, 6 + k // 4, (k % 4) * P:(k % 4 + 1) * P],
                                   modT[:, j * KD + k, q:q + 1].broadcast_to([P, P]), ident, start=True, stop=True)
                mm.then_inc(s["row_ps"], 1)

            order = [(G1, 0), (G1, 1), (SC2, 0), (SC2, 1), (SH2, 0), (SH2, 1)]

            pe.wait_ge(s["yf_sb"], FG)
            n_row = 0
            for i in range(NT):
                for h in range(2):
                    if i == 0:
                        p1_loaded(pe, 13 + h)
                    for n, c in enumerate((4, 5, 6, 7, 0, 1, 2, 3)):
                        x = mixT[:, c, i * P:(i + 1) * P] if c < CR else yfs[:, c - CR, i * P:(i + 1) * P]
                        if h == 0 and i == 0 and c < CR:
                            pe.wait_ge(s["yr_done"], c + 1)
                        mm = pe.matmul(PS[:, 2 * i + h, :], x,
                                       unit3(ring[(14 + h) % RING])[:, c, :], start=(n == 0), stop=(n == KD - 1))
                        if n == KD - 1 and i == NT - 1:
                            mm.then_inc(s["p1_used"], 1)
                        elif n == KD - 1 and h == 1:
                            mm.then_inc(s["mix_ps"], 1)
                        if n % 4 == 3 and n_row < 6 and (i, h) != (0, 0):
                            row(n_row, *order[n_row])
                            n_row += 1

            def h2_cols(i):
                pe.wait_ge(s["h2_done"], i + 1)
                for k in range(KD):
                    mm = pe.transpose(PS[:, 2 * i + k // 4, (k % 4) * P:(k % 4 + 1) * P], tts[i][:, k * P:(k + 1) * P], ident)
                mm.then_inc(s["h2T_ps"], 1)

            def logits(i):
                pe.wait_ge(s["h2T_sb"], i + 1)
                for k in range(KD):
                    mm = pe.matmul(PS[:, 0, 20 * i:20 * i + 20], h2T[:, k, i * P:(i + 1) * P], wr[:, k, :],
                                   start=(k == 0), stop=(k == KD - 1))
                return mm

            pe.wait_ge(s["row_sb"], 6)
            ada_sums(10, 15)
            ada_cols(10)
            h2_cols(0)
            ada_sums(11, 16)
            ada_cols(11)
            h2_cols(1)
            pe.wait_ge(s["rtr_in"], 64)
            logits(0)
            logits(1)
            h2_cols(2)
            logits(2).then_inc(s["lg_ps"], 1)
            pe.wait_ge(s["state_done"], 8)
            pe.transpose(PS[0:8, 2, 128:256], stin[:, 0:8], ident).then_inc(s["st_ps"], 1)
            pe.wait_ge(s["tri_done"], 1)
            pe.wait_ge(s["assign_done"], 1)
            for i in range(NT + 1):
                for j in range(min(i, NT - 1) + 1):
                    mm = pe.matmul(PS[:, 1, NE * i:NE * (i + 1)], tri_ones[:, 0 if j == i else 1, :],
                                   marks16[:, j, :], start=(j == 0), stop=(j == min(i, NT - 1)))
            mm.then_inc(s["rank_ps"], 1)

            def dispatch(ge, n):
                pe.wait_ge(s["sel_ready"], ge + 1)
                need(pe, "xs_ready", ge)

                def tokens(slots):
                    per = 512 // slots
                    for k in range(KD):
                        out = PS[:, k // per, (k % per) * slots:(k % per + 1) * slots]
                        for m in range(3 * NT):
                            part, i = m // NT, m % NT
                            mm = pe.matmul(out, h2b[:, 2 - part, i, k * P:(k + 1) * P],
                                           sel[:, i, 0:slots], start=(m == 0), stop=(m == 3 * NT - 1))
                    mm.then_inc(s["x_disp"], 1)

                fork(pe, n, lambda: tokens(HALF), lambda: tokens(CAP))

            def prologue(ge, pb):
                if isinstance(ge, int):
                    pe.wait_ge(s["h2b3"], NT)
                    pe.wait_ge(s["route_done"], 1)
                dispatch(ge, tokens_of(pe, 0, pb))

            def body(ge, e, q, p, last, pb):
                n = tokens_of(pe, e, pb)
                n1 = None if last else tokens_of(pe, e + 1, pb)

                def products(out, xh, xl, wh, wl, kk, width):
                    n_h = width // 512
                    trio = [(xh, wh), (xh, wl)] + ([(xl, wh)] if xl is not None else [])
                    for k in range(kk):
                        for m, (x, w) in enumerate(trio):
                            for h in range(n_h):
                                mm = pe.matmul(out[h], x[:, k, :], w[:, k, h * 512:(h + 1) * 512],
                                               start=(k == 0 and m == 0), stop=(k == kk - 1 and m == len(trio) - 1))
                    mm.then_inc(s["unit_used"], 1)

                def first(many):
                    for j in range(2):
                        pe.wait_ge(s["lo_done"], ge * 5 + (2 * j + 2))
                        if j == 0:
                            pe.wait_ge(s["xs_ready"], ge + 1)
                            need(pe, "g_done", ge)
                            need(pe, "u_done", ge)
                        products([PS[:, 2 + j, :]], xsH, xsL if many else None, unit3(whi[j]), unit3(wlo[3 * p + j]), KD, 512)

                def turn(many):
                    pe.wait_ge(s["g_done"], ge + 1)
                    pe.wait_ge(s["u_done"], ge + 1)
                    need(pe, "hts_ready", ge)
                    if many:
                        for k in range(KF):
                            mm = pe.transpose(PS[:, 4, k * P:(k + 1) * P], hid[:, k * P:(k + 1) * P], ident)
                    else:
                        for x, bank in ((sg, 4), (hid, 7)):
                            for k in range(KF):
                                mm = pe.matmul(PS[:, bank, k * HALF:(k + 1) * HALF], x[:, k * P:(k + 1) * P],
                                               cst[:, C_TWO:C_TWO + HALF], start=True, stop=True)
                    mm.then_inc(s["ht_ps"], 1)

                def down(many):
                    pe.wait_ge(s["hts_ready"], ge + 1)
                    pe.wait_ge(s["lo_done"], ge * 5 + 5)
                    pe.wait_ge(s["lo_pool"], ge + 1)
                    need(pe, "y_sb", ge)
                    products([PS[:, 5, :], PS[:, 6, :]], hTH, hTL if many else None, unit3(whi[2], D),
                             unit3(wlo[3 * p + 2], D), KF, D)

                def whole(many):
                    first(many)
                    turn(many)

                fork(pe, n, lambda: whole(False), lambda: whole(True))
                if not last:
                    dispatch(ge + 1, n1)
                fork(pe, n, lambda: down(False), lambda: down(True))

            passes(pe, lambda pb: pairs(pe, lambda ge: prologue(ge, pb), lambda *a: body(*a, pb), pb))
            pe.wait_ge(s["banks_free"], 1)
            for q in range(2):
                for k in range(KD):
                    mm = pe.matmul(PS[:, 2 * q + k // 4, (k % 4) * P:(k % 4 + 1) * P],
                                   modT[:, G2 * KD + k, q:q + 1].broadcast_to([P, P]), ident, start=True, stop=True)
            mm.then_inc(s["g2_ps"], 1)


_INS = ["x_prompt", "x_sample", "w_ada", "w_in", "rg_wa", "rg_wi", "fn_w", "w_out", "router_g_w", "router_e_w",
        "router_g_b", "router_e_b", "ex_w_gate", "ex_w_up", "ex_w_down", "ln1_g", "ln1_b", "ln2_g", "ln2_b"]
_ROWS = ["c", "c_ctx", "b_ada", "ln_in_g", "ln_in_b", "conv_w", "conv_b", "rg_ba", "rg_bi", "rg_lam", "fn_b"]


def kernel(**inputs):
    import concourse.bacc as _bacc
    from concourse.bass_utils import run_bass_kernel_spmd as _run

    nc = _bacc.Bacc("TRN2", target_bir_lowering=False, num_devices=1)
    const, dft, pos = constants()
    arrays = {"const": const, "dft": dft, "pos": pos}
    for name in _INS:
        arrays[name] = np.ascontiguousarray(inputs[name])
    for name in _ROWS:
        arrays[name] = np.ascontiguousarray(inputs[name]).reshape(-1, P)
    arrays["state"] = np.ascontiguousarray(inputs["state_rglru"]).reshape(-1, P)
    for name in ("ln_in_g", "ln_in_b"):
        arrays[name + "_row"] = np.ascontiguousarray(inputs[name])
    for name in ("ln1_g", "ln1_b"):
        arrays[name + "_col"] = arrays[name].reshape(-1, P)
    for name in ("ln1_g", "ln1_b", "ln2_g", "ln2_b", "router_g_b", "router_e_b"):
        arrays[name] = arrays[name].reshape(-1)
    t = {n: nc.dram_tensor("in_" + n, a.shape, mybir.dt.from_np(a.dtype), kind="ExternalInput").ap()
         for n, a in arrays.items()}
    outs = {"y_prompt": (1, SEQ, D), "y_sample": (1, LAT, D), "new_state": (8, P)}
    for n, shape in outs.items():
        t[n] = nc.dram_tensor("out_" + n, shape, F32, kind="ExternalOutput").ap()
    build(nc, t)
    r = _run(nc, [{"in_" + n: a for n, a in arrays.items()}], core_ids=[0]).results[0]
    return (r["out_y_prompt"], r["out_y_sample"], r["out_new_state"].reshape(1, 1, 2, DR))
```
